# Optimizing a Trainium2 kernel written in Bass

```python
import jax, jax.numpy as jnp
from jax import lax
import numpy as np

D_MODEL = 1024
BATCH = 1
SEQ = 256
DEPTH = 1
DEC_BATCH = 1
DEC_SEQ = 1024
PAST_LEN = 128

FOURIER_GROUPS = 4
FOURIER_GROUP_DIM = 128
FOURIER_WIDTH = FOURIER_GROUPS * FOURIER_GROUP_DIM
ATTN_GROUPS = ((128, 1), (512, 4), (2048, 16))
N_ATTN_GROUPS = 3
HEADS_PER_GROUP = 4
HEAD_DIM = 128
ATTN_GROUP_WIDTH = HEADS_PER_GROUP * HEAD_DIM
ATTN_WIDTH = N_ATTN_GROUPS * ATTN_GROUP_WIDTH
ATTN_OUT_WIDTH = HEADS_PER_GROUP * HEAD_DIM
ROPE_DIM = HEAD_DIM // 4
ROPE_THETA = 500000.0
IN_WIDTH = FOURIER_WIDTH + 3 * ATTN_WIDTH + 2 * D_MODEL
N_KEYS = 128
N_EXPERTS = N_KEYS * N_KEYS
PEER_HEADS = 8
PEER_TOPK = 16
PEER_KEY_DIM = 256
PEER_CHUNK = 128
NORM_EPS = 1e-6
NEG_INF = -1e30

kernel_name = 'hybrid_fnet_dilated_attn_peer_encoder'

def rmsnorm(x, g):
    xf = x.astype(jnp.float32)
    y = xf * lax.rsqrt(jnp.mean(xf * xf, axis=-1, keepdims=True) + NORM_EPS)
    return (y * g.astype(jnp.float32)).astype(x.dtype)

def partial_rope(x):
    s = x.shape[1]
    half = ROPE_DIM // 2
    inv_freq = ROPE_THETA ** (-jnp.arange(half, dtype=jnp.float32) * 2.0 / ROPE_DIM)
    ang = jnp.arange(s, dtype=jnp.float32)[:, None] * inv_freq[None, :]
    cos = jnp.cos(ang)[None, :, None, None, :]
    sin = jnp.sin(ang)[None, :, None, None, :]
    xr = x[..., :ROPE_DIM].astype(jnp.float32)
    x1, x2 = xr[..., :half], xr[..., half:]
    rot = jnp.concatenate([x1 * cos - x2 * sin, x2 * cos + x1 * sin], axis=-1).astype(x.dtype)
    return jnp.concatenate([rot, x[..., ROPE_DIM:]], axis=-1)

def dilated_window_attention(q, k, v, window, dilation):
    b, s, h, e = q.shape
    span = window // (2 * dilation)
    L = s // dilation
    nb = -(-L // span)
    Lp = nb * span

    def to_sub(t):
        t = t.reshape(b, L, dilation, h, e).transpose(0, 2, 1, 3, 4)
        return jnp.pad(t, ((0, 0), (0, 0), (0, Lp - L), (0, 0), (0, 0)))

    def band(t):
        t = jnp.pad(t, ((0, 0), (0, 0), (span, span), (0, 0), (0, 0)))
        t = t.reshape(b, dilation, nb + 2, span, h, e)
        return jnp.concatenate([t[:, :, :-2], t[:, :, 1:-1], t[:, :, 2:]], axis=3)

    qb = to_sub(q).reshape(b, dilation, nb, span, h, e)
    kb = band(to_sub(k))
    vb = band(to_sub(v))
    scores = jnp.einsum('bdnqhe,bdnkhe->bdnhqk', qb, kb).astype(jnp.float32) * (HEAD_DIM ** -0.5)
    qpos = jnp.arange(nb)[:, None, None] * span + jnp.arange(span)[None, :, None]
    kpos = jnp.arange(nb)[:, None, None] * span + jnp.arange(3 * span)[None, None, :] - span
    valid = (jnp.abs(kpos - qpos) <= span) & (kpos >= 0) & (kpos < L)
    scores = jnp.where(valid[None, None, :, None], scores, NEG_INF)
    m = jnp.max(scores, axis=-1, keepdims=True)
    p = jnp.exp(scores - m)
    l = jnp.sum(p, axis=-1, keepdims=True)
    o = jnp.einsum('bdnhqk,bdnkhe->bdnhqe', p, vb.astype(jnp.float32)) / l
    o = o.transpose(0, 1, 2, 4, 3, 5).reshape(b, dilation, Lp, h, e)[:, :, :L]
    o = o.transpose(0, 2, 1, 3, 4).reshape(b, s, h, e)
    logden = (m + jnp.log(l))[..., 0]
    logden = logden.transpose(0, 1, 2, 4, 3).reshape(b, dilation, Lp, h)[:, :, :L]
    logden = logden.transpose(0, 2, 1, 3).reshape(b, s, h)
    return o, logden

def fourier_mix(f):
    b, s, _ = f.shape
    fg = f.reshape(b, s, FOURIER_GROUPS, FOURIER_GROUP_DIM).astype(jnp.float32)
    return jnp.fft.fft2(fg, axes=(1, 3), norm='ortho').real.reshape(b, s, FOURIER_WIDTH)

def peer(xn, w_query, sub_keys, expert_u, expert_v):
    b, s, d = xn.shape
    t = b * s
    xt = xn.reshape(t, d)
    q = (xt @ w_query).reshape(t, PEER_HEADS, 2, PEER_KEY_DIM // 2)
    half = jnp.einsum('thcd,hcnd->thcn', q, sub_keys).astype(jnp.float32)
    s1, i1 = lax.top_k(half[:, :, 0], PEER_TOPK)
    s2, i2 = lax.top_k(half[:, :, 1], PEER_TOPK)
    cand = (s1[..., :, None] + s2[..., None, :]).reshape(t, PEER_HEADS, PEER_TOPK * PEER_TOPK)
    top_s, top_j = lax.top_k(cand, PEER_TOPK)
    ia = jnp.take_along_axis(i1, top_j // PEER_TOPK, axis=-1)
    ib = jnp.take_along_axis(i2, top_j % PEER_TOPK, axis=-1)
    experts = (ia * N_KEYS + ib).reshape(t, PEER_HEADS * PEER_TOPK)
    gates = jax.nn.softmax(top_s, axis=-1).reshape(t, PEER_HEADS * PEER_TOPK)
    nc = t // PEER_CHUNK

    def chunk_fn(args):
        xc, ec, gc = args
        a = jnp.einsum('cd,ckd->ck', xc, expert_u[ec]).astype(jnp.float32)
        hact = (jax.nn.gelu(a) * gc).astype(xc.dtype)
        return jnp.einsum('ck,ckd->cd', hact, expert_v[ec])

    out = lax.map(chunk_fn, (xt.reshape(nc, PEER_CHUNK, d),
                             experts.reshape(nc, PEER_CHUNK, PEER_HEADS * PEER_TOPK),
                             gates.reshape(nc, PEER_CHUNK, PEER_HEADS * PEER_TOPK)))
    return out.reshape(b, s, d).astype(xn.dtype)

def hybrid_block(x, g_mix, w_in, q_gain, k_gain, w_fourier, w_attn, w_out,
                 g_ffn, w_query, sub_keys, expert_u, expert_v):
    b, s, _ = x.shape
    xn = rmsnorm(x, g_mix)
    proj = xn @ w_in
    cuts = [FOURIER_WIDTH, FOURIER_WIDTH + ATTN_WIDTH, FOURIER_WIDTH + 2 * ATTN_WIDTH,
            FOURIER_WIDTH + 3 * ATTN_WIDTH, FOURIER_WIDTH + 3 * ATTN_WIDTH + D_MODEL]
    f, q, k, v, gate_a, gate_b = jnp.split(proj, cuts, axis=-1)
    hshape = (b, s, N_ATTN_GROUPS, HEADS_PER_GROUP, HEAD_DIM)
    q = partial_rope(rmsnorm(q.reshape(hshape), q_gain[:, None, :]))
    k = partial_rope(rmsnorm(k.reshape(hshape), k_gain[:, None, :]))
    v = v.reshape(hshape)
    outs, logdens = [], []
    for gi, (window, dilation) in enumerate(ATTN_GROUPS):
        o, ld = dilated_window_attention(q[:, :, gi], k[:, :, gi], v[:, :, gi], window, dilation)
        outs.append(o)
        logdens.append(ld)
    wgt = jax.nn.softmax(jnp.stack(logdens, axis=0), axis=0)
    attn = jnp.sum(wgt[..., None] * jnp.stack(outs, axis=0), axis=0)
    attn = attn.reshape(b, s, ATTN_OUT_WIDTH).astype(x.dtype) @ w_attn
    four = fourier_mix(f).astype(x.dtype) @ w_fourier
    mix = jax.nn.sigmoid(gate_a) * four + jax.nn.sigmoid(gate_b) * attn
    h = x + mix @ w_out
    return h + peer(rmsnorm(h, g_ffn), w_query, sub_keys, expert_u, expert_v)

def setup_inputs(seed: int = 0) -> dict:
    key = jax.random.key(seed)
    ks = jax.random.split(key, 16)
    f32 = jnp.float32

    def nrm(k, shape, scale):
        return jax.random.normal(k, shape, f32) * scale

    return {
        'x_prompt': nrm(ks[0], (BATCH, SEQ, D_MODEL), 1.0),
        'x_sample': nrm(ks[1], (DEC_BATCH, DEC_SEQ, D_MODEL), 1.0),
        'g_mix': 1.0 + nrm(ks[2], (DEPTH, D_MODEL), 0.02),
        'w_in': nrm(ks[3], (DEPTH, D_MODEL, IN_WIDTH), D_MODEL ** -0.5),
        'q_gain': 1.0 + nrm(ks[4], (DEPTH, N_ATTN_GROUPS, HEAD_DIM), 0.02),
        'k_gain': 1.0 + nrm(ks[5], (DEPTH, N_ATTN_GROUPS, HEAD_DIM), 0.02),
        'w_fourier': nrm(ks[6], (DEPTH, FOURIER_WIDTH, D_MODEL), FOURIER_WIDTH ** -0.5),
        'w_attn': nrm(ks[7], (DEPTH, ATTN_OUT_WIDTH, D_MODEL), ATTN_OUT_WIDTH ** -0.5),
        'w_out': nrm(ks[8], (DEPTH, D_MODEL, D_MODEL), D_MODEL ** -0.5),
        'g_ffn': 1.0 + nrm(ks[9], (DEPTH, D_MODEL), 0.02),
        'w_query': nrm(ks[10], (DEPTH, D_MODEL, PEER_HEADS * PEER_KEY_DIM), D_MODEL ** -0.5),
        'sub_keys': nrm(ks[11], (DEPTH, PEER_HEADS, 2, N_KEYS, PEER_KEY_DIM // 2), (PEER_KEY_DIM // 2) ** -0.5),
        'expert_u': nrm(ks[12], (DEPTH, N_EXPERTS, D_MODEL), D_MODEL ** -0.5),
        'expert_v': nrm(ks[13], (DEPTH, N_EXPERTS, D_MODEL), 0.25),
    }

def reference(x_prompt, x_sample, g_mix, w_in, q_gain, k_gain, w_fourier, w_attn, w_out,
              g_ffn, w_query, sub_keys, expert_u, expert_v):
    y_prompt = x_prompt
    y_sample = x_sample
    for layer in range(DEPTH):
        y_prompt = hybrid_block(y_prompt, g_mix[layer], w_in[layer], q_gain[layer], k_gain[layer],
                                w_fourier[layer], w_attn[layer], w_out[layer], g_ffn[layer],
                                w_query[layer], sub_keys[layer], expert_u[layer], expert_v[layer])
        y_sample = hybrid_block(y_sample, g_mix[layer], w_in[layer], q_gain[layer], k_gain[layer],
                                w_fourier[layer], w_attn[layer], w_out[layer], g_ffn[layer],
                                w_query[layer], sub_keys[layer], expert_u[layer], expert_v[layer])
    return (y_prompt, y_sample)


_drawn_inputs = setup_inputs


def setup_inputs(seed=0):
    import zlib

    import numpy as np

    out = dict(_drawn_inputs(seed))
    spreads = {}
    factors = {'g_mix': 3.972, 'q_gain': 8.0, 'k_gain': 8.0, 'g_ffn': 12.779}
    for name, (base, spread) in spreads.items():
        noise = np.random.default_rng([zlib.crc32(name.encode()), seed]).standard_normal(out[name].shape)
        drawn = base * np.exp(spread * noise) if base else spread * noise
        out[name] = __import__('jax').numpy.asarray(drawn.astype(out[name].dtype))
    for name, factor in factors.items():
        out[name] = (out[name] * factor).astype(out[name].dtype)
    return out
```

```python
from contextlib import ExitStack

import concourse.bass as bass
import numpy as np
from concourse import mybir

F32 = mybir.dt.float32
BF16 = mybir.dt.bfloat16
U32 = mybir.dt.uint32
ALU = mybir.AluOpType
ACT = mybir.ActivationFunctionType
AX = mybir.AxisListType.X

P = 128
D = 1024
DC = D // P
SEQ = 256
DEC_SEQ = 1024
T = SEQ + DEC_SEQ
TILES = T // P
PHASE = 4
RUN = 64
CHUNKS = ((0, SEQ), (SEQ, 512), (SEQ + 512, 512))
FG = 4
AG = 3
HEADS = 4
ATTN_WIDTH = AG * HEADS * P
SPAN = 64
DILATIONS = (1, 4, 16)
ROPE = 32
ROPE_THETA = 500000.0
SCALE = float(P) ** -0.5
EPS = 1e-6
MASKED = -1e30
LOWEST = -3.0e38
Q_COL = FG * P
K_COL = Q_COL + ATTN_WIDTH
V_COL = K_COL + ATTN_WIDTH
GA_COL = V_COL + ATTN_WIDTH
GB_COL = GA_COL + D
PH = 8
TOPK = 16
SLOTS = PH * TOPK
N_KEYS = 128
GROUP = 16
OCTET = 8
SEG_GROUPS = RUN // GROUP
SEG_OCTETS = RUN // OCTET
SEGS = T // RUN
PROMPT_SEGS = SEQ // RUN


def positions(batch):
    if batch == "prompt":
        return np.array([r + 4 * m for r in range(4) for m in range(64)])
    return np.array([r + 4 * k + 16 * i for r in range(4) for k in range(4) for i in range(64)])


def key_runs(tile):
    if tile < 2:
        return (0, SEQ), (tile * P, P), (tile * P, P)
    return (SEQ, DEC_SEQ), (SEQ + (tile - 2) // 2 * 256, 256), (tile * P, P)


def constants():
    bf16 = np.dtype("bfloat16")
    pp, ps = positions("prompt"), positions("sample")
    pos = np.concatenate([pp, ps])
    half = ROPE // 2
    inv = (np.float32(ROPE_THETA) ** (-np.arange(half, dtype=np.float32) * np.float32(2.0) / np.float32(ROPE)))
    ang = (pos.astype(np.float32)[None, :] * inv.astype(np.float32)[:, None]).astype(np.float64)
    cos, sin = np.cos(ang), np.sin(ang)
    rope_c = np.concatenate([cos, cos]).astype(np.float32)
    rope_s = np.concatenate([-sin, sin]).astype(np.float32)
    swap = np.zeros((ROPE, 2 * ROPE), np.float32)
    for i in range(ROPE):
        swap[(i + half) % ROPE, i] = 1.0

    def dft(p, n):
        a = 2 * np.pi * (np.outer(p, p) % n) / n
        return np.cos(a) / np.sqrt(n), -np.sin(a) / np.sqrt(n)

    c, s = dft(np.arange(P), P)
    chan = np.concatenate([c, -s], axis=1).astype(np.float32)
    dft_s = np.stack(dft(ps, DEC_SEQ)).astype(np.float32)
    dft_p = np.stack(dft(pp, SEQ)).astype(np.float32)
    masks = np.full((TILES, P, DEC_SEQ + 256 + P), MASKED, np.float32)
    for t in range(TILES):
        at = 0
        same = np.zeros(T, bool)
        same[:SEQ] = t < 2
        same[SEQ:] = t >= 2
        q = pos[t * P:(t + 1) * P]
        for (k0, n), dil in zip(key_runs(t), DILATIONS):
            dist = np.abs(q[:, None] - pos[None, k0:k0 + n])
            ok = (dist % dil == 0) & (dist <= SPAN * dil)
            masks[t, :, at:at + n] = np.where(ok, 0.0, MASKED)
            at += n
    ident = np.eye(P, dtype=np.float32)
    select = np.zeros((96, GROUP * P), np.float32)
    for i in range(GROUP):
        for part in range(3):
            select[32 * part + i, i * P:(i + 1) * P] = 1.0
    return {
        "c_ident": ident,
        "c_identb": ident.astype(bf16),
        "c_ropec": rope_c,
        "c_ropes": rope_s,
        "c_swap": swap,
        "c_chan": chan,
        "c_dfts": dft_s,
        "c_dftp": dft_p,
        "c_mask": masks.astype(bf16),
        "c_select": select.astype(bf16),
        "c_iota": np.broadcast_to(np.arange(TOPK, dtype=np.float32), (P, TOPK)).copy(),
    }


def wait_apart(eng, sem, value, noted):
    eng.wait_ge(sem, value)
    eng.sem_inc(noted, 1)


def link(eng, sem, n, per, noted):
    done = [0]

    def step(ins):
        done[0] += 1
        ins.then_inc(sem, 1)
        wait_apart(eng, sem, n * per + done[0], noted)

    def ended():
        assert done[0] == per, (done[0], per)

    step.ended = ended
    return step


class Program:

    def __init__(self, nc, a, ctx):
        self.nc, self.a, self.ctx = nc, a, ctx
        self.stage, self.prefix = ctx, ""
        self.xp = a["x_prompt"][0].rearrange("(m r) d -> r m d", r=4)
        self.xs = a["x_sample"][0].rearrange("(i k r) d -> r k i d", k=4, r=4)
        self.yp = a["y_prompt"][0].rearrange("(m r) d -> r m d", r=4)
        self.ys = a["y_sample"][0].rearrange("(i k r) d -> r k i d", k=4, r=4)
        self.w_in = a["w_in"][0].rearrange("(c p) n -> p c n", p=P)
        self.psum = ctx.enter_context(nc.psum_tensor("psum", [P, 8, 512], F32))
        self.ident = self.sb("ident", [P, P], F32)
        self.xnT = self.sb("xnT", [P, DC, T], F32)
        self.branchT = self.sb("branchT", [P, FG + HEADS, T], F32)

    def sb(self, name, shape, dt):
        return self.stage.enter_context(self.nc.sbuf_tensor(self.prefix + name, shape, dt))

    def sem(self, name):
        return self.stage.enter_context(self.nc.semaphore(self.prefix + name))

    def banks(self, first, n=1):
        return self.psum[:, first:first + n, :].rearrange("p b n -> p (b n)")


def rows_of(pr, view_p, view_s, n, r, b):
    if r is None:
        return [view_p[2 * b + c] for c in range(2)]
    return [view_s[bass.ds(r, 1), 2 * b + c, :, :].rearrange("o i d -> (o i) d") for c in range(2)]


def tile_pairs(eng, body):
    body(0, None)
    with eng.Fori(0, PHASE) as r:
        body(r + 1, r)


def stage_norm(pr):
    nc, a = pr.nc, pr.a
    x = pr.sb("x", [P, 2, D], F32)
    xn = pr.sb("xn", [P, 2, D], F32)
    junk = pr.sb("junk", [P, 2, D], F32)
    g = pr.sb("g", [P, DC], F32)
    stat = pr.sb("stat", [P, 2, 4], F32)
    x_in = [pr.sem(f"x_in{b}") for b in range(2)]
    const_in = pr.sem("const_in")
    squares = pr.sem("squares")
    means = pr.sem("means")
    roots = pr.sem("roots")
    inverse = pr.sem("inverse")
    normed = pr.sem("normed")
    turned = pr.sem("turned")
    stored = pr.sem("stored")

    with nc.Block() as block:
        @block.sync
        def _(sp):
            sp.dma_start(pr.ident[:, :], a["c_ident"]).then_inc(const_in, 16)
            sp.dma_start(g[:, :], a["g_mix"][0].rearrange("(c p) -> p c", p=P),
                         allow_slow_non_contiguous=True).then_inc(const_in, 16)

            def pair(n, r):
                for b in range(2):
                    if r is not None:
                        sp.wait_ge(normed, 2 * n - 1 + b)
                    for c, rows in enumerate(rows_of(pr, pr.xp, pr.xs, n, r, b)):
                        sp.dma_start(x[RUN * c:RUN * (c + 1), b, :], rows).then_inc(x_in[b], 16)

            tile_pairs(sp, pair)

        @block.scalar
        def _(act):
            def pair(n, r):
                for b in range(2):
                    act.wait_ge(x_in[b], 32 * n + 32)
                    nc.scalar.activation(junk[:, b, :], x[:, b, :], ACT.Square,
                                         accum_out=stat[:, b, 0:1]).then_inc(squares, 1)
                    act.wait_ge(means, 2 * n + b + 1)
                    nc.scalar.activation(stat[:, b, 2:3], stat[:, b, 1:2], ACT.Sqrt).then_inc(roots, 1)

            tile_pairs(act, pair)

        @block.vector
        def _(dve):
            dve.wait_ge(const_in, 32)

            def pair(n, r):
                for b in range(2):
                    dve.wait_ge(squares, 2 * n + b + 1)
                    nc.vector.tensor_scalar(stat[:, b, 1:2], stat[:, b, 0:1], 1.0 / D, EPS,
                                            ALU.mult, ALU.add).then_inc(means, 1)
                    dve.wait_ge(roots, 2 * n + b + 1)
                    nc.vector.reciprocal(stat[:, b, 3:4], stat[:, b, 2:3]).then_inc(inverse, 1)
                    dve.wait_ge(inverse, 2 * n + b + 1)
                    nc.vector.tensor_scalar(xn[:, b, :], x[:, b, :], stat[:, b, 3:4], None,
                                            ALU.mult).then_inc(normed, 1)
                    dve.wait_ge(turned, 2 * n + b + 1)
                    col = (2 * n + b) * P
                    nc.vector.tensor_tensor(
                        pr.xnT[:, :, bass.ds(col, P)], pr.psum[:, 2 * b:2 * b + 2, :].rearrange(
                            "p b (c n) -> p (b c) n", n=P),
                        g[:, :].unsqueeze(2).to_broadcast([P, DC, P]), ALU.mult).then_inc(stored, 1)

            tile_pairs(dve, pair)

        @block.tensor
        def _(pe):
            pe.wait_ge(const_in, 32)

            def pair(n, r):
                for b in range(2):
                    pe.wait_ge(normed, 2 * n + b + 1)
                    if r is not None:
                        pe.wait_ge(stored, 2 * n - 1 + b)
                    for c in range(DC):
                        last = nc.tensor.transpose(pr.psum[:, 2 * b + c // 4, c % 4 * P:c % 4 * P + P],
                                                   xn[:, b, c * P:(c + 1) * P], pr.ident[:, :])
                    last.then_inc(turned, 1)

            tile_pairs(pe, pair)


def stage_fourier(pr):
    nc, a = pr.nc, pr.a
    w = pr.sb("w", [P, 2, DC, P], F32)
    fT = pr.branchT[:, FG:2 * FG, :]
    chan = pr.sb("chan", [P, 2 * P], F32)
    spec = pr.sb("spec", [P, TILES, FG * 2 * P], F32)
    table_s = pr.sb("table_s", [P, 2, DEC_SEQ // P, 2, 512], F32)
    table_p = pr.sb("table_p", [P, SEQ // P, 2, SEQ], F32)
    w_loaded = [pr.sem(f"w_loaded{b}") for b in range(2)]
    chan_in = pr.sem("chan_in")
    tp_in = pr.sem("tp_in")
    ts_in = [pr.sem(f"ts_in{b}") for b in range(2)]
    projected = pr.sem("projected")
    f_ready = pr.sem("f_ready")
    chan_done = pr.sem("chan_done")
    spec_ready = pr.sem("spec_ready")
    mixed = pr.sem("mixed")
    four_ready = pr.sem("four_ready")
    units = [(g, c0, n) for c0, n in CHUNKS for g in range(FG)]

    with nc.Block() as block:
        @block.sync
        def _(sp):
            for g in range(FG):
                if g >= 2:
                    sp.wait_ge(projected, 3 * (g - 1))
                sp.dma_start(w[:, g % 2, :, :], pr.w_in[:, :, g * P:(g + 1) * P]).then_inc(w_loaded[g % 2], 16)
                if g == 1:
                    sp.dma_start(chan[:, :], a["c_chan"]).then_inc(chan_in, 16)
            for part in range(2):
                sp.dma_start(table_p[:, :, part, :], a["c_dftp"][part].rearrange(
                    "(t p) k -> p t k", p=P)).then_inc(tp_in, 16)
            for h in range(2):
                for part in range(2):
                    sp.dma_start(table_s[:, h, :, part, :], a["c_dfts"][part][:, h * 512:(h + 1) * 512].rearrange(
                        "(t p) k -> p t k", p=P)).then_inc(ts_in[h], 16)

        @block.tensor
        def _(pe):
            for g in range(FG):
                pe.wait_ge(w_loaded[g % 2], 16 * (g // 2 + 1))
                for c, (c0, n) in enumerate(CHUNKS):
                    if g >= 2:
                        pe.wait_ge(f_ready, 3 * (g - 2) + c + 1)
                    for k in range(DC):
                        last = nc.tensor.matmul(pr.psum[:, g % 2 * 3 + c, 0:n], w[:, g % 2, k, :],
                                                pr.xnT[:, k, c0:c0 + n], start=k == 0, stop=k == DC - 1)
                    last.then_inc(projected, 1)
            pe.wait_ge(f_ready, 3 * FG)
            pe.wait_ge(chan_in, 16)
            for t in range(TILES):
                if t >= 4:
                    pe.wait_ge(spec_ready, t - 3)
                for g in range(FG):
                    last = nc.tensor.matmul(pr.psum[:, 2 * (t % 4) + g // 2, g % 2 * 256:g % 2 * 256 + 256],
                                            fT[:, g, t * P:(t + 1) * P], chan[:, :], start=True, stop=True)
                last.then_inc(chan_done, 1)
            pe.wait_ge(spec_ready, TILES)
            pe.wait_ge(tp_in, 32)
            for u, (g, c0, n) in enumerate(units):
                if u == FG:
                    pe.wait_ge(ts_in[0], 32)
                if u == 2 * FG:
                    pe.wait_ge(ts_in[1], 32)
                if u >= 8:
                    pe.wait_ge(four_ready, u - 7)
                tiles = range(2) if c0 == 0 else range(2, TILES)
                for t in tiles:
                    for part in range(2):
                        table = (table_p[:, t, part, :] if c0 == 0 else
                                 table_s[:, (c0 - SEQ) // 512, t - 2, part, :])
                        last = nc.tensor.matmul(pr.psum[:, u % 8, 0:n],
                                                spec[:, t, (2 * g + part) * P:(2 * g + part + 1) * P],
                                                table, start=t == tiles[0] and part == 0,
                                                stop=t == tiles[-1] and part == 1)
                last.then_inc(mixed, 1)

        @block.scalar
        def _(act):
            for g in range(FG):
                for c, (c0, n) in enumerate(CHUNKS):
                    act.wait_ge(projected, 3 * g + c + 1)
                    nc.scalar.copy(fT[:, g, c0:c0 + n], pr.psum[:, g % 2 * 3 + c, 0:n]).then_inc(f_ready, 1)
            for u, (g, c0, n) in enumerate(units):
                act.wait_ge(mixed, u + 1)
                nc.scalar.copy(pr.branchT[:, g, c0:c0 + n], pr.psum[:, u % 8, 0:n]).then_inc(four_ready, 1)

        @block.vector
        def _(dve):
            for t in range(TILES):
                dve.wait_ge(chan_done, t + 1)
                nc.vector.tensor_copy(spec[:, t, :], pr.banks(2 * (t % 4), 2)).then_inc(spec_ready, 1)


def stage_attention(pr):
    nc, a = pr.nc, pr.a
    w = pr.sb("w", [P, 2, DC, P], F32)
    wv = pr.sb("wv", [P, DC, AG, P], F32)
    qk = pr.sb("qk", [P, 2 * AG, T], F32)
    v = pr.sb("v", [P, TILES, AG, P], F32)
    mask = pr.sb("mask", [P, 2, 1408], BF16)
    identb = pr.sb("identb", [P, P], BF16)
    mean = pr.sb("mean", [P, P], F32)
    swap = pr.sb("swap", [ROPE, 2 * ROPE], F32)
    ropec = pr.sb("ropec", [ROPE, T], F32)
    ropes = pr.sb("ropes", [ROPE, T], F32)
    gain = pr.sb("gain", [P, 2 * AG], F32)
    eps = pr.sb("eps", [P, 1], F32)
    sq = pr.sb("sq", [P, 2, 512], F32)
    root = pr.sb("root", [P, 2, 512], F32)
    rot = pr.sb("rot", [ROPE, 2, 512], F32)
    prob = pr.sb("prob", [P, 2, 1408], F32)
    probT = pr.sb("probT", [P, 1408], F32)
    stat = pr.sb("stat", [P, 2, 4], F32)
    out = pr.sb("out", [P, 2, P], F32)

    const_in = pr.sem("const_in")
    w_loaded = [pr.sem(f"w_loaded{b}") for b in range(2)]
    wv_loaded = pr.sem("wv_loaded")
    mask_in = [pr.sem(f"mask_in{b}") for b in range(2)]
    set_up = pr.sem("set_up")
    raw = pr.sem("raw")
    squared = pr.sem("squared")
    averaged = pr.sem("averaged")
    rooted = pr.sem("rooted")
    inverted = pr.sem("inverted")
    normed = pr.sem("normed")
    swapped = pr.sem("swapped")
    roped = pr.sem("roped")
    v_ready = pr.sem("v_ready")
    scored = pr.sem("scored")
    maxed = pr.sem("maxed")
    shifted = pr.sem("shifted")
    expd = pr.sem("expd")
    turned = pr.sem("turned")
    kept_a = pr.sem("kept_a")
    kept_v = pr.sem("kept_v")
    weighed = pr.sem("weighed")
    summed = pr.sem("summed")
    out_ready = pr.sem("out_ready")
    out_turned = pr.sem("out_turned")
    out_kept = pr.sem("out_kept")

    NB = 2 * AG
    NU = 3 * NB
    NR = NU + TILES
    UNITS = [(j, c0, n) for j in range(NB) for c0, n in CHUNKS]

    def blocks(t):
        return [(g, (k0 // P) + i) for g, (k0, n) in enumerate(key_runs(t)) for i in range(n // P)]

    QUAD = 4
    quads = [(t, i) for t in range(TILES) for i in range(-(-len(blocks(t)) // QUAD))]
    first_quad = [quads.index((t, 0)) for t in range(TILES)] + [len(quads)]
    NQ = len(quads)
    even = [(i + 1) // 2 for i in range(NQ + 1)]

    def quad_bank(q):
        return pr.banks(3 + q % 3)

    def score_banks(t):
        return pr.banks(0, 3)[:, 0:P * len(blocks(t))]

    w_col = [(Q_COL, K_COL)[j % 2] + j // 2 * HEADS * P for j in range(NB)]

    with nc.Block() as block:
        @block.sync
        def _(sp):
            for dst, src in ((identb[:, :], a["c_identb"]), (swap[:, :], a["c_swap"]),
                             (ropec[:, :], a["c_ropec"]), (ropes[:, :], a["c_ropes"])):
                sp.dma_start(dst, src).then_inc(const_in, 16)
            for i, name in enumerate(("q_gain", "k_gain")):
                sp.dma_start(gain[:, :].rearrange("p (g i) -> p i g", i=2)[:, i, :],
                             a[name][0].rearrange("g p -> p g"), allow_slow_non_contiguous=True
                             ).then_inc(const_in, 16)

            def load_w(at, j):
                sp.dma_start(w[:, j % 2, :, :], pr.w_in[:, :, bass.ds(at + w_col[j], P)]
                             ).then_inc(w_loaded[j % 2], 16)

            def load_wv(at):
                for g in range(AG):
                    sp.dma_start(wv[:, :, g, :], pr.w_in[:, :, bass.ds(at + (V_COL + g * HEADS * P), P)]
                                 ).then_inc(wv_loaded, 16)

            load_w(0, 0)
            load_w(0, 1)
            load_wv(0)

            def head(h, ahead):
                at = h * P if not ahead else sp.snap(h * P)
                for j in range(2, NB):
                    sp.wait_ge(raw, NR * h + 3 * (j - 1))
                    load_w(at, j)
                if ahead:
                    for j in range(2):
                        sp.wait_ge(raw, NR * h + 3 * (NB - 1 + j))
                        load_w(at + P, j)
                for t in range(TILES):
                    if t == 0:
                        sp.wait_ge(raw, NR * h + NR)
                    if t >= 2:
                        sp.wait_ge(scored, TILES * h + t - 1)
                    sp.dma_start(mask[:, t % 2, 0:P * len(blocks(t))], a["c_mask"][t][:, 0:P * len(blocks(t))]
                                 ).then_inc(mask_in[t % 2], 16)
                    if t == 0 and ahead:
                        load_wv(at + P)

            with sp.Fori(0, HEADS - 1) as h:
                head(h, True)
            head(HEADS - 1, False)

        @block.tensor
        def _(pe):
            pe.wait_ge(const_in, 96)
            pe.wait_ge(set_up, 2)

            def raw_unit(h, u):
                j, c0, n = UNITS[u]
                if u % 3 == 0:
                    pe.wait_ge(w_loaded[j % 2], 16 * (NB // 2 * h + j // 2 + 1))
                if u >= 3:
                    pe.wait_ge(normed, NU * h + u - 2)
                for k in range(DC):
                    last = nc.tensor.matmul(pr.psum[:, u % 3, 0:n], w[:, j % 2, k, :],
                                            pr.xnT[:, k, c0:c0 + n], start=k == 0, stop=k == DC - 1)
                last.then_inc(raw, 1)

            def mean_unit(h, u):
                n = UNITS[u][2]
                pe.wait_ge(squared, NU * h + u + 1)
                if u >= 2:
                    pe.wait_ge(rooted, NU * h + u - 1)
                nc.tensor.matmul(pr.psum[:, 3 + u % 2, 0:n], mean[:, :], sq[:, u % 2, 0:n],
                                 start=True, stop=True).then_inc(averaged, 1)

            def swap_unit(h, u):
                j, c0, n = UNITS[u]
                pe.wait_ge(normed, NU * h + u + 1)
                if u >= 2:
                    pe.wait_ge(roped, 3 * (NU * h + u - 1))
                nc.tensor.matmul(pr.psum[0:2 * ROPE, 5 + u % 2, 0:n], swap[:, :], qk[0:ROPE, j, c0:c0 + n],
                                 start=True, stop=True).then_inc(swapped, 1)

            def v_tile(h, t):
                u = NU + t
                if t == 0:
                    pe.wait_ge(wv_loaded, 48 * h + 48)
                if t < 3:
                    pe.wait_ge(normed, NU * h + u - 2)
                else:
                    pe.wait_ge(v_ready, TILES * h + t - 2)
                for k in range(DC):
                    last = nc.tensor.matmul(pr.psum[:, u % 3, 0:AG * P], pr.xnT[:, k, t * P:(t + 1) * P],
                                            wv[:, k, :, :], start=k == 0, stop=k == DC - 1)
                last.then_inc(raw, 1)

            def scores(h, t):
                at = 0
                pe.wait_ge(mask_in[t % 2], 16 * (TILES // 2 * h + t // 2 + 1))
                if t >= 1:
                    pe.wait_ge(expd, TILES * h + t)
                for g, (k0, n) in enumerate(key_runs(t)):
                    for c in range(0, n, 512):
                        m = min(512, n - c)
                        s = pr.banks(0, 3)[:, at:at + m]
                        nc.tensor.matmul(s, identb[:, :], mask[:, t % 2, at:at + m], start=True, stop=False)
                        last = nc.tensor.matmul(s, qk[:, 2 * g, t * P:(t + 1) * P],
                                                qk[:, 2 * g + 1, k0 + c:k0 + c + m], start=False, stop=True)
                        at += m
                last.then_inc(scored, 1)

            def turn(h, t):
                n = len(blocks(t))
                pe.wait_ge(expd, TILES * h + t + 1)
                for q in range(first_quad[t], first_quad[t + 1]):
                    if q >= 3:
                        if (q - 3) % 2 == 0:
                            pe.wait_ge(kept_a, even[NQ] * h + even[q - 2])
                        else:
                            pe.wait_ge(kept_v, (NQ - even[NQ]) * h + q - 2 - even[q - 2])
                    x0 = QUAD * (q - first_quad[t])
                    for x in range(x0, min(x0 + QUAD, n)):
                        last = nc.tensor.transpose(quad_bank(q)[:, (x - x0) * P:(x - x0 + 1) * P],
                                                   prob[:, t % 2, x * P:(x + 1) * P], pr.ident[:, :])
                    last.then_inc(turned, 1)

            def weigh(h, t):
                end = first_quad[t + 1]
                pe.wait_ge(kept_a, even[NQ] * h + even[end])
                pe.wait_ge(kept_v, (NQ - even[NQ]) * h + end - even[end])
                bl = blocks(t)
                for x, (g, kt) in enumerate(bl):
                    last = nc.tensor.matmul(pr.psum[:, 6, 0:P], probT[:, x * P:(x + 1) * P], v[:, kt, g, :],
                                            start=x == 0, stop=x == len(bl) - 1)
                last.then_inc(weighed, 1)

            def turn_out(h, t):
                pe.wait_ge(out_ready, TILES * h + t + 1)
                if t >= 1:
                    pe.wait_ge(out_kept, TILES * h + t)
                nc.tensor.transpose(pr.psum[:, 7, 0:P], out[:, t % 2, :], pr.ident[:, :]
                                    ).then_inc(out_turned, 1)

            with pe.Fori(0, HEADS) as h:
                for u in range(NU + 2):
                    if u < NU:
                        raw_unit(h, u)
                    if 1 <= u <= NU:
                        mean_unit(h, u - 1)
                    if u == NU:
                        v_tile(h, 0)
                    if u == NU + 1:
                        v_tile(h, 1)
                        v_tile(h, 2)
                    if u >= 2:
                        swap_unit(h, u - 2)
                for t in range(3, TILES):
                    v_tile(h, t)
                pe.wait_ge(roped, 3 * NU * h + 3 * NU)
                pe.wait_ge(v_ready, TILES * h + TILES)
                scores(h, 0)
                for t in range(TILES):
                    if t + 1 < TILES:
                        scores(h, t + 1)
                    turn(h, t)
                    if t >= 1:
                        turn_out(h, t - 1)
                    weigh(h, t)
                turn_out(h, TILES - 1)
                pe.wait_ge(out_kept, TILES * h + TILES)

        @block.scalar
        def _(act):
            act.wait_ge(set_up, 2)

            def square(h, u):
                n = UNITS[u][2]
                act.wait_ge(raw, NR * h + u + 1)
                if u >= 2:
                    act.wait_ge(averaged, NU * h + u - 1)
                nc.scalar.activation(sq[:, u % 2, 0:n], pr.psum[:, u % 3, 0:n], ACT.Square
                                     ).then_inc(squared, 1)

            def root_of(h, u):
                n = UNITS[u][2]
                act.wait_ge(averaged, NU * h + u + 1)
                if u >= 2:
                    act.wait_ge(normed, NU * h + u - 1)
                nc.scalar.activation(root[:, u % 2, 0:n], pr.psum[:, 3 + u % 2, 0:n], ACT.Sqrt,
                                     bias=eps[:, 0:1]).then_inc(rooted, 1)

            def keep_quads(h, t):
                for q in range(first_quad[t], first_quad[t + 1]):
                    if q % 2 == 0:
                        x = QUAD * (q - first_quad[t])
                        m = P * min(QUAD, len(blocks(t)) - x)
                        act.wait_ge(turned, NQ * h + q + 1)
                        if t >= 1 and q < first_quad[t] + 2:
                            act.wait_ge(weighed, TILES * h + t)
                        nc.scalar.copy(probT[:, x * P:x * P + m], quad_bank(q)[:, 0:m]).then_inc(kept_a, 1)

            with act.Fori(0, HEADS) as h:
                for u in range(NU + 1):
                    if u < NU:
                        square(h, u)
                    if u >= 1:
                        root_of(h, u - 1)
                for t in range(TILES):
                    act.wait_ge(raw, NR * h + NU + t + 1)
                    nc.scalar.copy(v[:, t, :, :].rearrange("p g e -> p (g e)"),
                                   pr.psum[:, (NU + t) % 3, 0:AG * P]).then_inc(v_ready, 1)
                for t in range(TILES + 1):
                    if t < TILES:
                        act.wait_ge(shifted, TILES * h + t + 1)
                        if t >= 2:
                            act.wait_ge(turned, NQ * h + first_quad[t - 1])
                        nc.scalar.activation(prob[:, t % 2, 0:P * len(blocks(t))], score_banks(t), ACT.Exp,
                                             bias=stat[:, t % 2, 1:2], scale=SCALE,
                                             accum_out=stat[:, t % 2, 2:3]).then_inc(expd, 1)
                    if t >= 1:
                        keep_quads(h, t - 1)
                    if t >= 2:
                        act.wait_ge(out_turned, TILES * h + t - 1)
                        nc.scalar.copy(pr.branchT[:, bass.ds(h + FG, 1), (t - 2) * P:(t - 1) * P].rearrange(
                            "p o n -> p (o n)"), pr.psum[:, 7, 0:P]).then_inc(out_kept, 1)
                act.wait_ge(out_turned, TILES * h + TILES)
                nc.scalar.copy(pr.branchT[:, bass.ds(h + FG, 1), (TILES - 1) * P:T].rearrange(
                    "p o n -> p (o n)"), pr.psum[:, 7, 0:P]).then_inc(out_kept, 1)

        @block.vector
        def _(dve):
            nc.vector.memset(mean[:, :], 1.0 / P).then_inc(set_up, 1)
            nc.vector.memset(eps[:, :], EPS).then_inc(set_up, 1)
            dve.wait_ge(const_in, 96)

            def norm_unit(h, u):
                j, c0, n = UNITS[u]
                dve.wait_ge(rooted, NU * h + u + 1)
                nc.vector.reciprocal(root[:, u % 2, 0:n], root[:, u % 2, 0:n]).then_inc(inverted, 1)
                dve.wait_ge(inverted, NU * h + u + 1)
                nc.vector.scalar_tensor_tensor(qk[:, j, c0:c0 + n], pr.psum[:, u % 3, 0:n], gain[:, j:j + 1],
                                               root[:, u % 2, 0:n], ALU.mult, ALU.mult).then_inc(normed, 1)

            def rope_unit(h, u):
                j, c0, n = UNITS[u]
                at = 3 * (NU * h + u)
                dve.wait_ge(swapped, NU * h + u + 1)
                nc.vector.tensor_tensor(rot[:, u % 2, 0:n], pr.psum[0:ROPE, 5 + u % 2, 0:n],
                                        ropes[:, c0:c0 + n], ALU.mult).then_inc(roped, 1)
                nc.vector.tensor_tensor(qk[0:ROPE, j, c0:c0 + n], qk[0:ROPE, j, c0:c0 + n],
                                        ropec[:, c0:c0 + n], ALU.mult).then_inc(roped, 1)
                dve.wait_ge(roped, at + 2)
                nc.vector.tensor_tensor(qk[0:ROPE, j, c0:c0 + n], qk[0:ROPE, j, c0:c0 + n],
                                        rot[:, u % 2, 0:n], ALU.add).then_inc(roped, 1)

            with dve.Fori(0, HEADS) as h:
                for u in range(NU + 1):
                    if u < NU:
                        norm_unit(h, u)
                    if u >= 1:
                        rope_unit(h, u - 1)
                for t in range(TILES + 1):
                    if t < TILES:
                        dve.wait_ge(scored, TILES * h + t + 1)
                        nc.vector.reduce_max(stat[:, t % 2, 0:1], score_banks(t), AX).then_inc(maxed, 1)
                        dve.wait_ge(maxed, TILES * h + t + 1)
                        nc.vector.tensor_scalar(stat[:, t % 2, 1:2], stat[:, t % 2, 0:1], -SCALE, None,
                                                ALU.mult).then_inc(shifted, 1)
                    if t >= 1:
                        s = t - 1
                        for q in range(first_quad[s], first_quad[s + 1]):
                            if q % 2 == 1:
                                x = QUAD * (q - first_quad[s])
                                m = P * min(QUAD, len(blocks(s)) - x)
                                dve.wait_ge(turned, NQ * h + q + 1)
                                if s >= 1 and q < first_quad[s] + 2:
                                    dve.wait_ge(weighed, TILES * h + s)
                                nc.vector.tensor_copy(probT[:, x * P:x * P + m], quad_bank(q)[:, 0:m]
                                                      ).then_inc(kept_v, 1)
                        dve.wait_ge(expd, TILES * h + s + 1)
                        nc.vector.reciprocal(stat[:, s % 2, 3:4], stat[:, s % 2, 2:3]).then_inc(summed, 1)
                        dve.wait_ge(summed, TILES * h + s + 1)
                        dve.wait_ge(weighed, TILES * h + s + 1)
                        if s >= 2:
                            dve.wait_ge(out_turned, TILES * h + s - 1)
                        nc.vector.tensor_scalar(out[:, s % 2, :], pr.psum[:, 6, 0:P], stat[:, s % 2, 3:4],
                                                None, ALU.mult).then_inc(out_ready, 1)


def first_then_loop(eng, count, body):
    body(0, True)
    with eng.Fori(1, count) as i:
        body(i, False)


def stage_mix(pr):
    nc, a = pr.nc, pr.a
    WC = 2 * DC + FG + HEADS
    w = pr.sb("w", [P, 2, WC, P], F32)
    sig = pr.sb("sig", [P, 2, 2, 512], F32)
    part = pr.sb("part", [P, 2, 2, 512], F32)
    w_loaded = [pr.sem(f"w_loaded{b}") for b in range(2)]
    produced = pr.sem("produced")
    gated = pr.sem("gated")
    steps = pr.sem("steps")
    NC = len(CHUNKS)
    w_f = a["w_fourier"][0].rearrange("(c p) n -> p c n", p=P)
    w_a = a["w_attn"][0].rearrange("(c p) n -> p c n", p=P)

    with nc.Block() as block:
        @block.sync
        def _(sp):
            def pair(i, first):
                for b in range(2):
                    if not first:
                        sp.wait_ge(produced, NC * (2 * i + b - 1))
                    at = 0
                    for view, col in ((pr.w_in, GA_COL), (pr.w_in, GB_COL), (w_f, 0), (w_a, 0)):
                        n = view.shape[1]
                        sp.dma_start(w[:, b, at:at + n, :], view[:, :, bass.ds(2 * P * i + (b * P + col), P)]
                                     ).then_inc(w_loaded[b], 16)
                        at += n

            first_then_loop(sp, DC // 2, pair)

        @block.tensor
        def _(pe):
            def pair(i, first):
                for v in range(2 * NC):
                    b, (c0, n) = v // NC, CHUNKS[v % NC]
                    if v % NC == 0:
                        pe.wait_ge(w_loaded[b], 64 * i + 64)
                    if not first or v >= 2:
                        pe.wait_ge(steps, 6 * NC * i + 3 * (v - 1))
                    at = 0
                    for s, (rhs, kc) in enumerate(((pr.xnT, DC), (pr.xnT, DC), (pr.branchT[:, 0:FG, :], FG),
                                                   (pr.branchT[:, FG:FG + HEADS, :], HEADS))):
                        for k in range(kc):
                            last = nc.tensor.matmul(pr.psum[:, 4 * (v % 2) + s, 0:n], w[:, b, at + k, :],
                                                    rhs[:, k, c0:c0 + n], start=k == 0, stop=k == kc - 1)
                        at += kc
                    last.then_inc(produced, 1)

            first_then_loop(pe, DC // 2, pair)

        @block.scalar
        def _(act):
            def pair(i, first):
                for v in range(2 * NC):
                    n = CHUNKS[v % NC][1]
                    act.wait_ge(produced, 2 * NC * i + v + 1)
                    for s in range(2):
                        nc.scalar.activation(sig[:, v % 2, s, 0:n], pr.psum[:, 4 * (v % 2) + s, 0:n],
                                             ACT.Sigmoid).then_inc(gated, 1)

            first_then_loop(act, DC // 2, pair)

        @block.vector
        def _(dve):
            def pair(i, first):
                for v in range(2 * NC):
                    b, (c0, n) = v // NC, CHUNKS[v % NC]
                    at = 6 * NC * i + 3 * v
                    dve.wait_ge(gated, 4 * NC * i + 2 * v + 2)
                    for s in range(2):
                        nc.vector.tensor_tensor(part[:, v % 2, s, 0:n], pr.psum[:, 4 * (v % 2) + 2 + s, 0:n],
                                                sig[:, v % 2, s, 0:n], ALU.mult).then_inc(steps, 1)
                    dve.wait_ge(steps, at + 2)
                    nc.vector.tensor_tensor(
                        pr.mixT[:, bass.ds(2 * i + b, 1), c0:c0 + n].rearrange("p o n -> p (o n)"),
                        part[:, v % 2, 0, 0:n], part[:, v % 2, 1, 0:n], ALU.add).then_inc(steps, 1)

            first_then_loop(dve, DC // 2, pair)


def stage_out(pr):
    nc, a = pr.nc, pr.a
    w = pr.branchT[:, :, :].rearrange("p c n -> p (c n)")[:, 0:DC * D].rearrange("p (c n) -> p c n", c=DC)
    mixb = pr.sb("mixb", [P, 2, DC, P], F32)
    x = pr.sb("x2", [P, 2, D], F32)
    h = pr.sb("h", [P, 2, D], F32)
    xn = pr.sb("xn2", [P, 2, D], F32)
    rest = pr.sb("rest", [P, 2, D], F32)
    parts = pr.sb("parts", [P, 3, D], BF16)
    g = pr.sb("g2", [P, D], F32)
    stat = pr.sb("stat2", [P, 2, 4], F32)
    x_in = [pr.sem(f"x_in{b}") for b in range(2)]
    const_in = pr.sem("const_in")
    picked = pr.sem("picked")
    product = pr.sem("product")
    h_ready = pr.sem("h_ready")
    squares = pr.sem("squares")
    means = pr.sem("means")
    roots = pr.sem("roots")
    inverse = pr.sem("inverse")
    normed = pr.sem("normed")
    split = pr.sem("split")
    first_parts = pr.sem("first_parts")
    turned = pr.sem("turned")
    kept = pr.sem("kept")
    h_out = [pr.sem(f"h_out{b}") for b in range(2)]
    parts_out = pr.sem("parts_out")
    noted = pr.sem("noted")

    with nc.Block() as block:
        @block.sync
        def _(sp):
            sp.dma_start(w, a["w_out"][0].rearrange("(c p) n -> p c n", p=P)).then_inc(const_in, 16)
            sp.dma_start(g[:, :], a["g_ffn"].to_broadcast([P, D])).then_inc(const_in, 16)

            def pair(n, r):
                for b in range(2):
                    k = 2 * n + b
                    if r is not None:
                        sp.wait_ge(h_ready, k - 1)
                    for c, rows in enumerate(rows_of(pr, pr.xp, pr.xs, n, r, b)):
                        sp.dma_start(x[RUN * c:RUN * (c + 1), b, :], rows).then_inc(x_in[b], 16)
                for b in range(2):
                    k = 2 * n + b
                    sp.wait_ge(h_ready, k + 1)
                    sp.dma_start(a["s_h"][bass.ds(k * P, P), :], h[:, b, :]).then_inc(h_out[b], 16)
                    wait_apart(sp, split, 2 * k + 2, noted)
                    for i in range(3):
                        sp.dma_start(a["s_xn"][i][bass.ds(k * P, P), :], parts[:, i, :]).then_inc(parts_out, 16)

            tile_pairs(sp, pair)
            sp.wait_ge(parts_out, 48 * TILES)
            for b in range(2):
                sp.wait_ge(h_out[b], 16 * TILES // 2)

        @block.scalar
        def _(act):
            def pair(n, r):
                for b in range(2):
                    k = 2 * n + b
                    if r is not None:
                        act.wait_ge(product, k - 1)
                    nc.scalar.copy(mixb[:, b, :, :], pr.mixT[:, :, bass.ds(k * P, P)]).then_inc(picked, 1)
                    act.wait_ge(h_ready, k + 1)
                    nc.scalar.activation(rest[:, b, :], h[:, b, :], ACT.Square,
                                         accum_out=stat[:, b, 0:1]).then_inc(squares, 1)
                    act.wait_ge(means, k + 1)
                    nc.scalar.activation(stat[:, b, 2:3], stat[:, b, 1:2], ACT.Sqrt).then_inc(roots, 1)
                    act.wait_ge(normed, k + 1)
                    if b == 1 or r is not None:
                        act.wait_ge(parts_out, 48 * k)
                    nc.scalar.copy(parts[:, 0, :], xn[:, b, :]).then_inc(first_parts, 1)
                    act.wait_ge(split, 2 * k + 1)
                    nc.scalar.copy(parts[:, 1, :], rest[:, b, :]).then_inc(first_parts, 1)
                    act.wait_ge(turned, k + 1)
                    nc.scalar.copy(pr.xnT[:, :, bass.ds(k * P, P)], pr.psum[:, 4 + 2 * b:6 + 2 * b, :].rearrange(
                        "p b (c n) -> p (b c) n", n=P)).then_inc(kept, 1)

            tile_pairs(act, pair)

        @block.vector
        def _(dve):
            dve.wait_ge(const_in, 32)

            def pair(n, r):
                for b in range(2):
                    k = 2 * n + b
                    dve.wait_ge(product, k + 1)
                    dve.wait_ge(x_in[b], 32 * n + 32)
                    if r is not None:
                        dve.wait_ge(h_out[b], 16 * n)
                    nc.vector.tensor_tensor(h[:, b, :], pr.banks(2 * b, 2), x[:, b, :], ALU.add
                                            ).then_inc(h_ready, 1)
                    dve.wait_ge(squares, k + 1)
                    nc.vector.tensor_scalar(stat[:, b, 1:2], stat[:, b, 0:1], 1.0 / D, EPS,
                                            ALU.mult, ALU.add).then_inc(means, 1)
                    dve.wait_ge(roots, k + 1)
                    nc.vector.reciprocal(stat[:, b, 3:4], stat[:, b, 2:3]).then_inc(inverse, 1)
                    dve.wait_ge(inverse, k + 1)
                    if r is not None:
                        dve.wait_ge(turned, k - 1)
                    nc.vector.scalar_tensor_tensor(xn[:, b, :], h[:, b, :], stat[:, b, 3:4], g[:, :],
                                                   ALU.mult, ALU.mult).then_inc(normed, 1)
                    dve.wait_ge(first_parts, 2 * k + 1)
                    nc.vector.tensor_tensor(rest[:, b, :], xn[:, b, :], parts[:, 0, :], ALU.subtract
                                            ).then_inc(split, 1)
                    dve.wait_ge(first_parts, 2 * k + 2)
                    nc.vector.tensor_tensor(parts[:, 2, :], rest[:, b, :], parts[:, 1, :], ALU.subtract
                                            ).then_inc(split, 1)

            tile_pairs(dve, pair)

        @block.tensor
        def _(pe):
            pe.wait_ge(const_in, 32)

            def pair(n, r):
                for b in range(2):
                    k = 2 * n + b
                    pe.wait_ge(picked, k + 1)
                    if r is not None:
                        pe.wait_ge(h_ready, k - 1)
                    for half in range(2):
                        for c in range(DC):
                            last = nc.tensor.matmul(pr.psum[:, 2 * b + half, :], mixb[:, b, c, :],
                                                    w[:, c, half * 512:half * 512 + 512],
                                                    start=c == 0, stop=c == DC - 1)
                    last.then_inc(product, 1)
                    pe.wait_ge(normed, k + 1)
                    if r is not None:
                        pe.wait_ge(kept, k - 1)
                    for c in range(DC):
                        last = nc.tensor.transpose(pr.psum[:, 4 + 2 * b + c // 4, c % 4 * P:c % 4 * P + P],
                                                   xn[:, b, c * P:(c + 1) * P], pr.ident[:, :])
                    last.then_inc(turned, 1)

            tile_pairs(pe, pair)


def stage_keys(pr):
    nc, a = pr.nc, pr.a
    scores = pr.scores
    w = pr.sb("w3", [P, 2, DC, P], F32)
    sk = pr.sb("sk", [P, 2, P], F32)
    skT = pr.sb("skT", [P, 2, P], F32)
    qT = pr.sb("qT", [P, 2, T], F32)
    w_loaded = [pr.sem(f"w_loaded{b}") for b in range(2)]
    turned = pr.sem("turned")
    keys_kept = pr.sem("keys_kept")
    projected = pr.sem("projected")
    q_kept = pr.sem("q_kept")
    scored = pr.sem("scored")
    kept = pr.sem("kept")
    wq = a["w_query"][0].rearrange("(c p) n -> p c n", p=P)
    RUNS = ((0, 4), (4, 4), (8, 2))

    with nc.Block() as block:
        @block.sync
        def _(sp):
            def head(i, first):
                for b in range(2):
                    if not first:
                        sp.wait_ge(projected, 3 * (2 * i + b - 1))
                    sp.dma_start(w[:, b, :, :], wq[:, :, bass.ds(2 * P * i + b * P, P)]).then_inc(w_loaded[b], 16)
                    sp.dma_start(sk[:, b, :], a["sub_keys"][0][bass.ds(i, 1), b, :, :].rearrange(
                        "o n d -> (o n) d")).then_inc(w_loaded[b], 16)

            first_then_loop(sp, PH, head)

        @block.tensor
        def _(pe):
            def head(i, first):
                for b in range(2):
                    m = 2 * i + b
                    pe.wait_ge(w_loaded[b], 32 * i + 32)
                    if not first or b:
                        pe.wait_ge(kept, 3 * m - 1)
                    nc.tensor.transpose(pr.psum[:, 7, 0:P], sk[:, b, :], pr.ident[:, :]).then_inc(turned, 1)
                    for c, (c0, n) in enumerate(CHUNKS):
                        if not first:
                            pe.wait_ge(q_kept, 3 * (m - 2) + c + 1)
                        for k in range(DC):
                            last = nc.tensor.matmul(pr.psum[:, 3 * b + c, 0:n], w[:, b, k, :],
                                                    pr.xnT[:, k, c0:c0 + n], start=k == 0, stop=k == DC - 1)
                        last.then_inc(projected, 1)
                    pe.wait_ge(keys_kept, m + 1)
                    pe.wait_ge(q_kept, 3 * m + 3)
                    for s, (t0, n) in enumerate(RUNS):
                        if not first or b or s == 2:
                            pe.wait_ge(kept, 3 * m + (0, 0, 1)[s] if s != 1 else 3 * m - 1)
                        for t in range(n):
                            last = nc.tensor.matmul(pr.psum[:, 6 + s % 2, t * P:(t + 1) * P],
                                                    qT[:, b, (t0 + t) * P:(t0 + t + 1) * P], skT[:, b, :],
                                                    start=True, stop=True)
                        last.then_inc(scored, 1)

            first_then_loop(pe, PH, head)

        @block.scalar
        def _(act):
            def head(i, first):
                for b in range(2):
                    m = 2 * i + b
                    for c, (c0, n) in enumerate(CHUNKS):
                        act.wait_ge(projected, 3 * m + c + 1)
                        if not first:
                            act.wait_ge(scored, 3 * m - 3)
                        nc.scalar.copy(qT[:, b, c0:c0 + n], pr.psum[:, 3 * b + c, 0:n]).then_inc(q_kept, 1)

            first_then_loop(act, PH, head)

        @block.vector
        def _(dve):
            def head(i, first):
                for b in range(2):
                    m = 2 * i + b
                    dve.wait_ge(turned, m + 1)
                    nc.vector.tensor_copy(skT[:, b, :], pr.psum[:, 7, 0:P]).then_inc(keys_kept, 1)
                    for s, (t0, n) in enumerate(RUNS):
                        dve.wait_ge(scored, 3 * m + s + 1)
                        nc.vector.tensor_copy(
                            scores[:, t0:t0 + n, bass.ds(m, 1), :].rearrange("p t o k -> p t (o k)"),
                            pr.psum[:, 6 + s % 2, 0:n * P].rearrange("p (t k) -> p t k", k=P)).then_inc(kept, 1)

            first_then_loop(dve, PH, head)


def stage_route(pr):
    nc, a = pr.nc, pr.a
    HH = 2 * PH
    sc = pr.sb("sc", [P, HH, N_KEYS], F32)
    free = pr.branchT[:, :, :].rearrange("p c n -> p (c n)")
    NCAND = PH * TOPK * TOPK
    left = free[:, 0:HH * N_KEYS]
    best = pr.sb("best", [P, HH, TOPK], F32)
    besti = pr.sb("besti", [P, HH, TOPK], U32)
    bestf = pr.sb("bestf", [P, HH, TOPK], F32)
    cand = free[:, NCAND:2 * NCAND].rearrange("p (h a b) -> p h a b", h=PH, a=TOPK)
    pick = free[:, 2 * NCAND:4 * NCAND].rearrange("p (c h a b) -> p c h a b", c=2, h=PH, a=TOPK)
    top = pr.sb("top", [P, PH, TOPK], F32)
    topi = pr.sb("topi", [P, PH, TOPK], U32)
    part = pr.sb("part4", [P, 2, PH, TOPK], U32)
    partf = pr.sb("partf", [P, 2, PH, TOPK], F32)
    key = pr.sb("key", [P, 2, PH, TOPK], F32)
    expert = pr.sb("expert", [P, PH, TOPK], F32)
    gate = pr.sb("gate", [P, PH, TOPK], F32)
    total = pr.sb("total", [P, 2, PH], F32)
    iota = pr.sb("iota", [P, TOPK], F32)
    idxT = pr.sb("idxT", [P, P], U32)
    gateT = pr.sb("gateT", [P, P], F32)
    const_in = pr.sem("const_in")
    picked = pr.sem("picked")
    chain = pr.sem("chain")
    shifted = pr.sem("shifted")
    expd = pr.sem("expd")
    noted = pr.sem("noted")
    tail = pr.sem("tail")
    routed = pr.sem("routed")
    turned = pr.sem("turned")
    kept = pr.sem("kept")
    stored = pr.sem("stored")
    CHAIN = 13

    with nc.Block() as block:
        @block.sync
        def _(sp):
            sp.dma_start(iota[:, :], a["c_iota"]).then_inc(const_in, 16)
            with sp.Fori(0, TILES) as t:
                sp.wait_ge(kept, 2 * t + 2)
                for name, src in (("s_idx", idxT), ("s_gate", gateT)):
                    sp.dma_start(a[name][bass.ds(2 * t, 2)].rearrange("c p n -> p c n"),
                                 src[:, :].rearrange("p (c n) -> p c n", c=2)).then_inc(stored, 16)
            sp.wait_ge(stored, 32 * TILES)

        @block.scalar
        def _(act):
            def tile(t, first):
                if not first:
                    act.wait_ge(routed, 2 * t)
                nc.scalar.copy(sc[:, :, :], pr.scores[:, bass.ds(t, 1), :, :].rearrange(
                    "p o h k -> p (o h) k")).then_inc(picked, 1)
                act.wait_ge(shifted, t + 1)
                nc.scalar.activation(gate[:, :, :], gate[:, :, :], ACT.Exp).then_inc(expd, 1)
                act.wait_ge(turned, t + 1)
                if not first:
                    act.wait_ge(stored, 32 * t)
                nc.scalar.copy(idxT[:, :], pr.psum[:, 0, 0:P]).then_inc(kept, 1)
                nc.scalar.copy(gateT[:, :], pr.psum[:, 0, P:2 * P]).then_inc(kept, 1)

            first_then_loop(act, TILES, tile)

        @block.tensor
        def _(pe):
            def tile(t, first):
                pe.wait_ge(routed, 2 * t + 2)
                if not first:
                    pe.wait_ge(kept, 2 * t)
                nc.tensor.transpose(pr.psum[:, 0, 0:P], expert[:, :, :].rearrange("p h k -> p (h k)"),
                                    pr.ident[:, :])
                nc.tensor.transpose(pr.psum[:, 0, P:2 * P], gate[:, :, :].rearrange("p h k -> p (h k)"),
                                    pr.ident[:, :]).then_inc(turned, 1)

            first_then_loop(pe, TILES, tile)

        @block.vector
        def _(dve):
            dve.wait_ge(const_in, 16)

            def top16(step, n, val, idx, src, rest):
                for i in range(n):
                    last = nc.vector.max(val[:, i, 0:8], src[:, i, :])
                step(last)
                for i in range(n):
                    nc.vector.max_index(idx[:, i, 0:8], val[:, i, 0:8], src[:, i, :])
                    last = nc.vector.match_replace(rest[:, i, :], val[:, i, 0:8], src[:, i, :], LOWEST)
                step(last)
                for i in range(n):
                    last = nc.vector.max(val[:, i, 8:16], rest[:, i, :])
                step(last)
                for i in range(n):
                    last = nc.vector.max_index(idx[:, i, 8:16], val[:, i, 8:16], rest[:, i, :])
                step(last)

            def tile(t, first):
                step = link(dve, chain, t, CHAIN, noted)
                wait_apart(dve, picked, t + 1, noted)
                top16(step, HH, best, besti, sc, left.rearrange("p (h k) -> p h k", k=N_KEYS))
                nc.vector.tensor_copy(bestf[:, :, :], besti[:, :, :])
                half = best[:, :, :].rearrange("p (h c) k -> p h c k", c=2)
                full = [P, PH, TOPK, TOPK]
                step(nc.vector.tensor_tensor(cand[:, :, :, :], half[:, :, 0, :].unsqueeze(3).to_broadcast(full),
                                             half[:, :, 1, :].unsqueeze(2).to_broadcast(full), ALU.add))
                flat = cand[:, :, :, :].rearrange("p h a b -> p h (a b)")
                top16(step, PH, top, topi, flat, left.rearrange("p (h k) -> p h k", k=TOPK * TOPK))
                if not first:
                    dve.wait_ge(turned, t)
                nc.vector.tensor_tensor(gate[:, :, :], top[:, :, :],
                                        top[:, :, 0:1].to_broadcast([P, PH, TOPK]), ALU.subtract
                                        ).then_inc(shifted, 1)
                nc.vector.tensor_scalar(part[:, 0, :, :], topi[:, :, :], 4, None, ALU.logical_shift_right)
                step(nc.vector.tensor_scalar(part[:, 1, :, :], topi[:, :, :], TOPK - 1, None, ALU.bitwise_and))
                step(nc.vector.tensor_copy(partf[:, :, :, :], part[:, :, :, :]))
                keys = bestf[:, :, :].rearrange("p (h c) k -> p h c k", c=2)
                for c in range(2):
                    last = nc.vector.tensor_tensor(
                        pick[:, c, :, :, :], partf[:, c, :, :].unsqueeze(3).to_broadcast(full),
                        iota[:, :].unsqueeze(1).unsqueeze(1).to_broadcast(full), ALU.is_equal)
                step(last)
                for c in range(2):
                    last = nc.vector.tensor_tensor(pick[:, c, :, :, :], pick[:, c, :, :, :],
                                                   keys[:, :, c, :].unsqueeze(2).to_broadcast(full), ALU.mult)
                step(last)
                nc.vector.tensor_reduce(key[:, :, :, :].rearrange("p c h k -> p (c h k)"),
                                        pick[:, :, :, :, :].rearrange("p c h k j -> p (c h k) j"), AX, ALU.add)
                dve.wait_ge(expd, t + 1)
                last = nc.vector.tensor_reduce(total[:, 0, :], gate[:, :, :], AX, ALU.add)
                last.then_inc(tail, 1)
                dve.wait_ge(tail, 2 * t + 1)
                nc.vector.scalar_tensor_tensor(expert[:, :, :].rearrange("p h k -> p (h k)"),
                                               key[:, 0, :, :].rearrange("p h k -> p (h k)"), float(N_KEYS),
                                               key[:, 1, :, :].rearrange("p h k -> p (h k)"),
                                               ALU.mult, ALU.add).then_inc(routed, 1)
                nc.vector.reciprocal(total[:, 1, :], total[:, 0, :]).then_inc(tail, 1)
                dve.wait_ge(tail, 2 * t + 2)
                nc.vector.tensor_tensor(gate[:, :, :], gate[:, :, :],
                                        total[:, 1, :].unsqueeze(2).to_broadcast([P, PH, TOPK]), ALU.mult
                                        ).then_inc(routed, 1)
                step.ended()

            first_then_loop(dve, TILES, tile)


def stage_experts(pr):
    nc, a = pr.nc, pr.a
    U_SLOTS, V_SLOTS = OCTET, 2 * OCTET
    u = pr.sb("u", [P, U_SLOTS, D], F32)
    v = pr.sb("v5", [P, V_SLOTS, D], F32)
    idx = pr.sb("idx", [P, 2, GROUP], U32)
    gate = pr.sb("gate5", [P, 2, GROUP], F32)
    xrow = pr.sb("xrow", [96, 2, D], BF16)
    select = pr.sb("select", [96, GROUP, P], BF16)
    hrow = pr.sb("hrow", [GROUP, 2, D], F32)
    y = pr.sb("y", [GROUP, 2, D], F32)
    dot = pr.sb("dot", [P, 2, OCTET], F32)
    act_u = pr.sb("act_u", [P, 2, OCTET], F32)
    weight = pr.sb("weight", [P, 2, GROUP, GROUP], F32)
    u_in = [pr.sem(f"u_in{i}") for i in range(U_SLOTS)]
    v_in = [pr.sem(f"v_in{i}") for i in range(V_SLOTS)]
    const_in = pr.sem("const_in")
    zeroed = pr.sem("zeroed")
    group_in = [pr.sem(f"group_in{b}") for b in range(2)]
    spread = pr.sem("spread")
    dotted = pr.sem("dotted")
    gelued = pr.sem("gelued")
    weighted = pr.sem("weighted")
    noted = pr.sem("noted")
    v_used = pr.sem("v_used")
    y_ready = pr.sem("y_ready")
    y_out = [pr.sem(f"y_out{b}") for b in range(2)]
    LOADS = 6 * 16

    def segments(eng, body):
        body(0, pr.yp[0], True)
        with eng.Fori(1, PROMPT_SEGS) as r:
            body(r, pr.yp[bass.ds(r, 1), :, :].rearrange("o i d -> (o i) d"), False)
        with eng.Fori(0, 4) as r:
            with eng.Fori(0, 4) as k:
                body(PROMPT_SEGS + 4 * r + k, pr.ys[bass.ds(r, 1), bass.ds(k, 1), :, :].rearrange(
                    "o q i d -> (o q i) d"), False)

    with nc.Block() as block:
        @block.sync
        def _(sp):
            sp.dma_start(select[:, :, :].rearrange("p g n -> p (g n)"), a["c_select"]).then_inc(const_in, 16)
            sp.wait_ge(zeroed, 3)

            def segment(n, rows, first):
                for g in range(SEG_GROUPS):
                    b = g % 2
                    if not first or g >= 2:
                        sp.wait_ge(y_ready, SEG_GROUPS * n + g - 1)
                    col = RUN * n + GROUP * g
                    for dst, name in ((idx, "s_idx"), (gate, "s_gate")):
                        sp.dma_start(dst[:, b, :], a[name][bass.ds(n, 1), :, g * GROUP:(g + 1) * GROUP].rearrange(
                            "o p n -> (o p) n")).then_inc(group_in[b], 16)
                    for i in range(3):
                        sp.dma_start(xrow[32 * i:32 * i + GROUP, b, :], a["s_xn"][i][bass.ds(col, GROUP), :]
                                     ).then_inc(group_in[b], 16)
                    sp.dma_start(hrow[:, b, :], a["s_h"][bass.ds(col, GROUP), :]).then_inc(group_in[b], 16)

            segments(sp, segment)

        @block.gpsimd
        def _(pool):
            def segment(n, rows, first):
                for s in range(RUN):
                    g, i = s // GROUP, s % GROUP
                    if i == 0:
                        pool.wait_ge(group_in[g % 2], LOADS * (SEG_GROUPS // 2 * n + g // 2 + 1))
                    if not first or s >= U_SLOTS:
                        wait_apart(pool, dotted, RUN * n + s - U_SLOTS + 1, noted)
                    at = bass.IndirectOffsetOnAxis(ap=idx[:, g % 2, i:i + 1], axis=0)
                    pool.indirect_dma_start(u[:, s % U_SLOTS, :], None, a["expert_u"][0], at
                                            ).then_inc(u_in[s % U_SLOTS], 16)
                    if not first or s >= V_SLOTS:
                        wait_apart(pool, v_used, RUN * n + s - V_SLOTS + 1, noted)
                    pool.indirect_dma_start(v[:, s % V_SLOTS, :], None, a["expert_v"][0], at
                                            ).then_inc(v_in[s % V_SLOTS], 16)

            segments(pool, segment)

        @block.tensor
        def _(pe):
            pe.wait_ge(const_in, 16)
            pe.wait_ge(zeroed, 3)

            def spread_x(n, s, first):
                g, i = s // GROUP, s % GROUP
                if i == 0:
                    pe.wait_ge(group_in[g % 2], LOADS * (SEG_GROUPS // 2 * n + g // 2 + 1))
                if not first or s >= 2:
                    pe.wait_ge(dotted, RUN * n + s - 1)
                for half in range(2):
                    last = nc.tensor.matmul(pr.psum[:, 2 * (s % 2) + half, :], select[:, i, :],
                                            xrow[:, g % 2, half * 512:half * 512 + 512], start=True, stop=True)
                last.then_inc(spread, 1)

            def sum_v(n, s):
                q = s % RUN
                g, i = q // GROUP, q % GROUP
                if i % OCTET == 0:
                    pe.wait_ge(weighted, SEG_OCTETS * n + s // OCTET + 1)
                pe.wait_ge(v_in[q % V_SLOTS], 16 * (RUN // V_SLOTS * n + s // V_SLOTS + 1))
                for half in range(2):
                    last = nc.tensor.matmul(pr.psum[0:GROUP, 4 + 2 * (g % 2) + half, :], weight[:, g % 2, i, :],
                                            v[:, q % V_SLOTS, half * 512:half * 512 + 512],
                                            start=i == 0, stop=i == GROUP - 1)
                last.then_inc(v_used, 1)

            def segment(n, rows, first):
                for s in range(RUN):
                    spread_x(n, s, first)
                    if not first or s >= OCTET:
                        sum_v(n, s - OCTET)

            segments(pe, segment)
            for s in range(RUN - OCTET, RUN):
                sum_v(SEGS - 1, s)

        @block.vector
        def _(dve):
            nc.vector.memset(weight[:, :, :, :], 0.0).then_inc(zeroed, 1)
            nc.vector.memset(xrow[:, 0, :], 0.0).then_inc(zeroed, 1)
            nc.vector.memset(xrow[:, 1, :], 0.0).then_inc(zeroed, 1)
            dve.wait_ge(zeroed, 3)

            def weights(n, o):
                q = o % SEG_OCTETS
                g, c = q // 2, q % 2
                flat = weight[:, g % 2, :, :].rearrange("p i j -> p (i j)")
                at = OCTET * c * (GROUP + 1)
                dve.wait_ge(gelued, SEG_OCTETS * n + o + 1)
                nc.vector.tensor_tensor(flat[:, at:at + (OCTET - 1) * (GROUP + 1) + 1:GROUP + 1],
                                        act_u[:, c, :], gate[:, g % 2, c * OCTET:(c + 1) * OCTET],
                                        ALU.mult).then_inc(weighted, 1)

            def add_h(n, g, first):
                b = g % 2
                dve.wait_ge(v_used, RUN * n + GROUP * (g + 1))
                if not first:
                    dve.wait_ge(y_out[b], 16 * (SEG_GROUPS // 2 * n + g // 2))
                nc.vector.tensor_tensor(y[:, b, :], pr.psum[0:GROUP, 4 + 2 * b:6 + 2 * b, :].rearrange(
                    "p b n -> p (b n)"), hrow[:, b, :], ALU.add).then_inc(y_ready, 1)

            def segment(n, rows, first):
                for s in range(RUN):
                    o = s // OCTET
                    dve.wait_ge(u_in[s % U_SLOTS], 16 * (SEG_OCTETS * n + o + 1))
                    dve.wait_ge(spread, RUN * n + s + 1)
                    nc.vector.tensor_tensor_reduce(u[:, s % U_SLOTS, :], u[:, s % U_SLOTS, :],
                                                   pr.banks(2 * (s % 2), 2), 1.0, 0.0, ALU.mult, ALU.add,
                                                   dot[:, o % 2, s % OCTET:s % OCTET + 1]).then_inc(dotted, 1)
                    if s % OCTET == 0 and (not first or o):
                        weights(n, o - 1)
                    if s % GROUP == OCTET - 1 and (not first or s >= GROUP):
                        add_h(n, s // GROUP - 1, first and s < 3 * GROUP)

            segments(dve, segment)
            weights(SEGS - 1, SEG_OCTETS - 1)
            add_h(SEGS - 1, SEG_GROUPS - 1, False)

        @block.scalar
        def _(act):
            def segment(n, rows, first):
                for o in range(SEG_OCTETS):
                    act.wait_ge(dotted, RUN * n + OCTET * (o + 1))
                    if not first or o >= 2:
                        act.wait_ge(weighted, SEG_OCTETS * n + o - 1)
                    nc.scalar.activation(act_u[:, o % 2, :], dot[:, o % 2, :], ACT.Gelu_apprx_tanh
                                         ).then_inc(gelued, 1)
                    if o % 2 == 1:
                        g = o // 2
                        act.wait_ge(y_ready, SEG_GROUPS * n + g + 1)
                        act.dma_start(rows[g * GROUP:(g + 1) * GROUP, :], y[:, g % 2, :]).then_inc(y_out[g % 2], 16)

            segments(act, segment)
            for b in range(2):
                act.wait_ge(y_out[b], 16 * SEGS * SEG_GROUPS // 2)


def build(nc, a, stop=99):
    with ExitStack() as ctx:
        pr = Program(nc, a, ctx)

        def run(stage):
            with ExitStack() as own:
                pr.stage, pr.prefix = own, stage.__name__.removeprefix("stage_") + "_"
                stage(pr)
            pr.prefix = ""

        run(stage_norm)
        if stop > 1:
            run(stage_fourier)
        if stop > 2:
            run(stage_attention)
        if stop > 3:
            with ExitStack() as mix_ctx:
                pr.stage = mix_ctx
                pr.mixT = pr.sb("mixT", [P, DC, T], F32)
                run(stage_mix)
                if stop > 4:
                    run(stage_out)
        if stop > 5:
            with ExitStack() as score_ctx:
                pr.stage = score_ctx
                pr.scores = pr.sb("scores", [P, TILES, 2 * PH, N_KEYS], F32)
                run(stage_keys)
                if stop > 6:
                    run(stage_route)
        if stop > 7:
            run(stage_experts)
    return pr


_INS = ["x_prompt", "x_sample", "g_mix", "w_in", "q_gain", "k_gain", "w_fourier", "w_attn", "w_out",
        "g_ffn", "w_query", "sub_keys", "expert_u", "expert_v"]
_OUTS = {"y_prompt": (1, SEQ, D), "y_sample": (1, DEC_SEQ, D)}


def kernel(**inputs):
    import concourse.bacc as bacc
    from concourse.bass_utils import run_bass_kernel_spmd

    nc = bacc.Bacc("TRN2", target_bir_lowering=False, num_devices=1)
    arrays, a = {}, {}
    for name, value in [(n, inputs[n]) for n in _INS] + list(constants().items()):
        value = np.ascontiguousarray(value)
        arrays[f"in_{name}"] = value
        a[name] = nc.dram_tensor(f"in_{name}", value.shape, mybir.dt.from_np(value.dtype),
                                 kind="ExternalInput").ap()
    for name, shape in _OUTS.items():
        a[name] = nc.dram_tensor(name, shape, F32, kind="ExternalOutput").ap()
    a["s_h"] = nc.dram_tensor("s_h", (T, D), F32, kind="Internal").ap()
    a["s_xn"] = nc.dram_tensor("s_xn", (3, T, D), BF16, kind="Internal").ap()
    for name, dt in (("s_idx", U32), ("s_gate", F32)):
        a[name] = nc.dram_tensor(name, (SEGS, P, RUN), dt, kind="Internal").ap()
    build(nc, a)
    r = run_bass_kernel_spmd(nc, [arrays], core_ids=[0])
    return tuple(r.results[0][name] for name in _OUTS)
```

```python
from contextlib import ExitStack

import concourse.bass as bass
import numpy as np
from concourse import mybir

F32 = mybir.dt.float32
BF16 = mybir.dt.bfloat16
U32 = mybir.dt.uint32
ALU = mybir.AluOpType
ACT = mybir.ActivationFunctionType
AX = mybir.AxisListType.X

P = 128
D = 1024
DC = D // P
SEQ = 256
DEC_SEQ = 1024
T = SEQ + DEC_SEQ
TILES = T // P
PHASE = 4
RUN = 64
CHUNKS = ((0, SEQ), (SEQ, 512), (SEQ + 512, 512))
FG = 4
AG = 3
HEADS = 4
ATTN_WIDTH = AG * HEADS * P
SPAN = 64
DILATIONS = (1, 4, 16)
ROPE = 32
ROPE_THETA = 500000.0
SCALE = float(P) ** -0.5
EPS = 1e-6
MASKED = -1e30
LOWEST = -3.0e38
Q_COL = FG * P
K_COL = Q_COL + ATTN_WIDTH
V_COL = K_COL + ATTN_WIDTH
GA_COL = V_COL + ATTN_WIDTH
GB_COL = GA_COL + D
PH = 8
TOPK = 16
SLOTS = PH * TOPK
N_KEYS = 128
GROUP = 16
OCTET = 8


def positions(batch):
    if batch == "prompt":
        return np.array([r + 4 * m for r in range(4) for m in range(64)])
    return np.array([r + 4 * k + 16 * i for r in range(4) for k in range(4) for i in range(64)])


def key_runs(tile):
    if tile < 2:
        return (0, SEQ), (tile * P, P), (tile * P, P)
    return (SEQ, DEC_SEQ), (SEQ + (tile - 2) // 2 * 256, 256), (tile * P, P)


def constants():
    bf16 = np.dtype("bfloat16")
    pp, ps = positions("prompt"), positions("sample")
    pos = np.concatenate([pp, ps])
    half = ROPE // 2
    inv = (np.float32(ROPE_THETA) ** (-np.arange(half, dtype=np.float32) * np.float32(2.0) / np.float32(ROPE)))
    ang = (pos.astype(np.float32)[None, :] * inv.astype(np.float32)[:, None]).astype(np.float64)
    cos, sin = np.cos(ang), np.sin(ang)
    rope_c = np.concatenate([cos, cos]).astype(np.float32)
    rope_s = np.concatenate([-sin, sin]).astype(np.float32)
    swap = np.zeros((ROPE, 2 * ROPE), np.float32)
    for i in range(ROPE):
        swap[(i + half) % ROPE, i] = 1.0

    def dft(p, n):
        a = 2 * np.pi * (np.outer(p, p) % n) / n
        return np.cos(a) / np.sqrt(n), -np.sin(a) / np.sqrt(n)

    c, s = dft(np.arange(P), P)
    chan = np.concatenate([c, -s], axis=1).astype(np.float32)
    dft_s = np.stack(dft(ps, DEC_SEQ)).astype(np.float32)
    dft_p = np.stack(dft(pp, SEQ)).astype(np.float32)
    masks = np.full((TILES, P, DEC_SEQ + 256 + P), MASKED, np.float32)
    for t in range(TILES):
        at = 0
        same = np.zeros(T, bool)
        same[:SEQ] = t < 2
        same[SEQ:] = t >= 2
        q = pos[t * P:(t + 1) * P]
        for (k0, n), dil in zip(key_runs(t), DILATIONS):
            dist = np.abs(q[:, None] - pos[None, k0:k0 + n])
            ok = (dist % dil == 0) & (dist <= SPAN * dil)
            masks[t, :, at:at + n] = np.where(ok, 0.0, MASKED)
            at += n
    ident = np.eye(P, dtype=np.float32)
    select = np.zeros((96, GROUP * P), np.float32)
    for i in range(GROUP):
        for part in range(3):
            select[32 * part + i, i * P:(i + 1) * P] = 1.0
    return {
        "c_ident": ident,
        "c_identb": ident.astype(bf16),
        "c_ropec": rope_c,
        "c_ropes": rope_s,
        "c_swap": swap,
        "c_chan": chan,
        "c_dfts": dft_s,
        "c_dftp": dft_p,
        "c_mask": masks.astype(bf16),
        "c_select": select.astype(bf16),
        "c_iota": np.broadcast_to(np.arange(TOPK, dtype=np.float32), (P, TOPK)).copy(),
    }


def wait_apart(eng, sem, value, noted):
    eng.wait_ge(sem, value)
    eng.sem_inc(noted, 1)


class Program:

    def __init__(self, nc, a, ctx):
        self.nc, self.a, self.ctx = nc, a, ctx
        self.stage, self.prefix = ctx, ""
        self.xp = a["x_prompt"][0].rearrange("(m r) d -> r m d", r=4)
        self.xs = a["x_sample"][0].rearrange("(i k r) d -> r k i d", k=4, r=4)
        self.yp = a["y_prompt"][0].rearrange("(m r) d -> r m d", r=4)
        self.ys = a["y_sample"][0].rearrange("(i k r) d -> r k i d", k=4, r=4)
        self.w_in = a["w_in"][0].rearrange("(c p) n -> p c n", p=P)
        self.psum = ctx.enter_context(nc.psum_tensor("psum", [P, 8, 512], F32))
        self.ident = self.sb("ident", [P, P], F32)

    def sb(self, name, shape, dt):
        return self.stage.enter_context(self.nc.sbuf_tensor(self.prefix + name, shape, dt))

    def sem(self, name):
        return self.stage.enter_context(self.nc.semaphore(self.prefix + name))

    def banks(self, first, n=1):
        return self.psum[:, first:first + n, :].rearrange("p b n -> p (b n)")


def rows_of(pr, view_p, view_s, n, r, b):
    if r is None:
        return [view_p[2 * b + c] for c in range(2)]
    return [view_s[bass.ds(r, 1), 2 * b + c, :, :].rearrange("o i d -> (o i) d") for c in range(2)]


def tile_pairs(eng, body):
    body(0, None)
    with eng.Fori(0, PHASE) as r:
        body(r + 1, r)


def stage_norm(pr):
    nc, a = pr.nc, pr.a
    x = pr.sb("x", [P, 2, D], F32)
    xn = pr.sb("xn", [P, 2, D], F32)
    junk = pr.sb("junk", [P, 2, D], F32)
    g = pr.sb("g", [P, DC], F32)
    stat = pr.sb("stat", [P, 2, 4], F32)
    x_in = [pr.sem(f"x_in{b}") for b in range(2)]
    const_in = pr.sem("const_in")
    squares = pr.sem("squares")
    means = pr.sem("means")
    roots = pr.sem("roots")
    inverse = pr.sem("inverse")
    normed = pr.sem("normed")
    turned = pr.sem("turned")
    stored = pr.sem("stored")

    with nc.Block() as block:
        @block.sync
        def _(sp):
            sp.dma_start(pr.ident[:, :], a["c_ident"]).then_inc(const_in, 16)
            sp.dma_start(g[:, :], a["g_mix"][0].rearrange("(c p) -> p c", p=P),
                         allow_slow_non_contiguous=True).then_inc(const_in, 16)

            def pair(n, r):
                for b in range(2):
                    if r is not None:
                        sp.wait_ge(normed, 2 * n - 1 + b)
                    for c, rows in enumerate(rows_of(pr, pr.xp, pr.xs, n, r, b)):
                        sp.dma_start(x[RUN * c:RUN * (c + 1), b, :], rows).then_inc(x_in[b], 16)

            tile_pairs(sp, pair)

        @block.scalar
        def _(act):
            def pair(n, r):
                for b in range(2):
                    act.wait_ge(x_in[b], 32 * n + 32)
                    nc.scalar.activation(junk[:, b, :], x[:, b, :], ACT.Square,
                                         accum_out=stat[:, b, 0:1]).then_inc(squares, 1)
                    act.wait_ge(means, 2 * n + b + 1)
                    nc.scalar.activation(stat[:, b, 2:3], stat[:, b, 1:2], ACT.Sqrt).then_inc(roots, 1)

            tile_pairs(act, pair)

        @block.vector
        def _(dve):
            dve.wait_ge(const_in, 32)

            def pair(n, r):
                for b in range(2):
                    dve.wait_ge(squares, 2 * n + b + 1)
                    nc.vector.tensor_scalar(stat[:, b, 1:2], stat[:, b, 0:1], 1.0 / D, EPS,
                                            ALU.mult, ALU.add).then_inc(means, 1)
                    dve.wait_ge(roots, 2 * n + b + 1)
                    nc.vector.reciprocal(stat[:, b, 3:4], stat[:, b, 2:3]).then_inc(inverse, 1)
                    dve.wait_ge(inverse, 2 * n + b + 1)
                    nc.vector.tensor_scalar(xn[:, b, :], x[:, b, :], stat[:, b, 3:4], None,
                                            ALU.mult).then_inc(normed, 1)
                    dve.wait_ge(turned, 2 * n + b + 1)
                    col = (2 * n + b) * P
                    nc.vector.tensor_tensor(
                        pr.xnT[:, :, bass.ds(col, P)], pr.psum[:, 2 * b:2 * b + 2, :].rearrange(
                            "p b (c n) -> p (b c) n", n=P),
                        g[:, :].unsqueeze(2).to_broadcast([P, DC, P]), ALU.mult).then_inc(stored, 1)

            tile_pairs(dve, pair)

        @block.tensor
        def _(pe):
            pe.wait_ge(const_in, 32)

            def pair(n, r):
                for b in range(2):
                    pe.wait_ge(normed, 2 * n + b + 1)
                    if r is not None:
                        pe.wait_ge(stored, 2 * n - 1 + b)
                    for c in range(DC):
                        last = nc.tensor.transpose(pr.psum[:, 2 * b + c // 4, c % 4 * P:c % 4 * P + P],
                                                   xn[:, b, c * P:(c + 1) * P], pr.ident[:, :])
                    last.then_inc(turned, 1)

            tile_pairs(pe, pair)


def stage_fourier(pr):
    nc, a = pr.nc, pr.a
    w = pr.sb("w", [P, 2, DC, P], F32)
    fT = pr.branchT[:, FG:2 * FG, :]
    chan = pr.sb("chan", [P, 2 * P], F32)
    spec = pr.sb("spec", [P, TILES, FG * 2 * P], F32)
    table_s = pr.sb("table_s", [P, 2, DEC_SEQ // P, 2, 512], F32)
    table_p = pr.sb("table_p", [P, SEQ // P, 2, SEQ], F32)
    w_loaded = [pr.sem(f"w_loaded{b}") for b in range(2)]
    chan_in = pr.sem("chan_in")
    tp_in = pr.sem("tp_in")
    ts_in = [pr.sem(f"ts_in{b}") for b in range(2)]
    projected = pr.sem("projected")
    f_ready = pr.sem("f_ready")
    chan_done = pr.sem("chan_done")
    spec_ready = pr.sem("spec_ready")
    mixed = pr.sem("mixed")
    four_ready = pr.sem("four_ready")
    units = [(g, c0, n) for c0, n in CHUNKS for g in range(FG)]

    with nc.Block() as block:
        @block.sync
        def _(sp):
            for g in range(FG):
                if g >= 2:
                    sp.wait_ge(projected, 3 * (g - 1))
                sp.dma_start(w[:, g % 2, :, :], pr.w_in[:, :, g * P:(g + 1) * P]).then_inc(w_loaded[g % 2], 16)
                if g == 1:
                    sp.dma_start(chan[:, :], a["c_chan"]).then_inc(chan_in, 16)
            for part in range(2):
                sp.dma_start(table_p[:, :, part, :], a["c_dftp"][part].rearrange(
                    "(t p) k -> p t k", p=P)).then_inc(tp_in, 16)
            for h in range(2):
                for part in range(2):
                    sp.dma_start(table_s[:, h, :, part, :], a["c_dfts"][part][:, h * 512:(h + 1) * 512].rearrange(
                        "(t p) k -> p t k", p=P)).then_inc(ts_in[h], 16)

        @block.tensor
        def _(pe):
            for g in range(FG):
                pe.wait_ge(w_loaded[g % 2], 16 * (g // 2 + 1))
                for c, (c0, n) in enumerate(CHUNKS):
                    if g >= 2:
                        pe.wait_ge(f_ready, 3 * (g - 2) + c + 1)
                    for k in range(DC):
                        last = nc.tensor.matmul(pr.psum[:, g % 2 * 3 + c, 0:n], w[:, g % 2, k, :],
                                                pr.xnT[:, k, c0:c0 + n], start=k == 0, stop=k == DC - 1)
                    last.then_inc(projected, 1)
            pe.wait_ge(f_ready, 3 * FG)
            pe.wait_ge(chan_in, 16)
            for t in range(TILES):
                if t >= 4:
                    pe.wait_ge(spec_ready, t - 3)
                for g in range(FG):
                    last = nc.tensor.matmul(pr.psum[:, 2 * (t % 4) + g // 2, g % 2 * 256:g % 2 * 256 + 256],
                                            fT[:, g, t * P:(t + 1) * P], chan[:, :], start=True, stop=True)
                last.then_inc(chan_done, 1)
            pe.wait_ge(spec_ready, TILES)
            pe.wait_ge(tp_in, 32)
            for u, (g, c0, n) in enumerate(units):
                if u == FG:
                    pe.wait_ge(ts_in[0], 32)
                if u == 2 * FG:
                    pe.wait_ge(ts_in[1], 32)
                if u >= 8:
                    pe.wait_ge(four_ready, u - 7)
                tiles = range(2) if c0 == 0 else range(2, TILES)
                for t in tiles:
                    for part in range(2):
                        table = (table_p[:, t, part, :] if c0 == 0 else
                                 table_s[:, (c0 - SEQ) // 512, t - 2, part, :])
                        last = nc.tensor.matmul(pr.psum[:, u % 8, 0:n],
                                                spec[:, t, (2 * g + part) * P:(2 * g + part + 1) * P],
                                                table, start=t == tiles[0] and part == 0,
                                                stop=t == tiles[-1] and part == 1)
                last.then_inc(mixed, 1)

        @block.scalar
        def _(act):
            for g in range(FG):
                for c, (c0, n) in enumerate(CHUNKS):
                    act.wait_ge(projected, 3 * g + c + 1)
                    nc.scalar.copy(fT[:, g, c0:c0 + n], pr.psum[:, g % 2 * 3 + c, 0:n]).then_inc(f_ready, 1)
            for u, (g, c0, n) in enumerate(units):
                act.wait_ge(mixed, u + 1)
                nc.scalar.copy(pr.branchT[:, g, c0:c0 + n], pr.psum[:, u % 8, 0:n]).then_inc(four_ready, 1)

        @block.vector
        def _(dve):
            for t in range(TILES):
                dve.wait_ge(chan_done, t + 1)
                nc.vector.tensor_copy(spec[:, t, :], pr.banks(2 * (t % 4), 2)).then_inc(spec_ready, 1)


def stage_attention(pr):
    nc, a = pr.nc, pr.a
    w = pr.sb("w", [P, 2, DC, P], F32)
    wv = pr.sb("wv", [P, DC, AG, P], F32)
    qk = pr.sb("qk", [P, 2 * AG, T], F32)
    v = pr.sb("v", [P, TILES, AG, P], F32)
    mask = pr.sb("mask", [P, 2, 1408], BF16)
    identb = pr.sb("identb", [P, P], BF16)
    mean = pr.sb("mean", [P, P], F32)
    swap = pr.sb("swap", [ROPE, 2 * ROPE], F32)
    ropec = pr.sb("ropec", [ROPE, T], F32)
    ropes = pr.sb("ropes", [ROPE, T], F32)
    gain = pr.sb("gain", [P, 2 * AG], F32)
    eps = pr.sb("eps", [P, 1], F32)
    sq = pr.sb("sq", [P, 2, 512], F32)
    root = pr.sb("root", [P, 2, 512], F32)
    rot = pr.sb("rot", [ROPE, 2, 512], F32)
    prob = pr.sb("prob", [P, 2, 1408], F32)
    probT = pr.sb("probT", [P, 1408], F32)
    stat = pr.sb("stat", [P, 2, 4], F32)
    out = pr.sb("out", [P, 2, P], F32)

    const_in = pr.sem("const_in")
    w_loaded = [pr.sem(f"w_loaded{b}") for b in range(2)]
    wv_loaded = pr.sem("wv_loaded")
    mask_in = [pr.sem(f"mask_in{b}") for b in range(2)]
    set_up = pr.sem("set_up")
    raw = pr.sem("raw")
    squared = pr.sem("squared")
    averaged = pr.sem("averaged")
    rooted = pr.sem("rooted")
    inverted = pr.sem("inverted")
    normed = pr.sem("normed")
    swapped = pr.sem("swapped")
    roped = pr.sem("roped")
    v_ready = pr.sem("v_ready")
    scored = pr.sem("scored")
    maxed = pr.sem("maxed")
    shifted = pr.sem("shifted")
    expd = pr.sem("expd")
    turned = pr.sem("turned")
    kept_a = pr.sem("kept_a")
    kept_v = pr.sem("kept_v")
    weighed = pr.sem("weighed")
    summed = pr.sem("summed")
    out_ready = pr.sem("out_ready")
    out_turned = pr.sem("out_turned")
    out_kept = pr.sem("out_kept")

    NB = 2 * AG
    NU = 3 * NB
    NR = NU + TILES
    UNITS = [(j, c0, n) for j in range(NB) for c0, n in CHUNKS]

    def blocks(t):
        return [(g, (k0 // P) + i) for g, (k0, n) in enumerate(key_runs(t)) for i in range(n // P)]

    QUAD = 4
    quads = [(t, i) for t in range(TILES) for i in range(-(-len(blocks(t)) // QUAD))]
    first_quad = [quads.index((t, 0)) for t in range(TILES)] + [len(quads)]
    NQ = len(quads)
    even = [(i + 1) // 2 for i in range(NQ + 1)]

    def quad_bank(q):
        return pr.banks(3 + q % 3)

    def score_banks(t):
        return pr.banks(0, 3)[:, 0:P * len(blocks(t))]

    w_col = [(Q_COL, K_COL)[j % 2] + j // 2 * HEADS * P for j in range(NB)]

    with nc.Block() as block:
        @block.sync
        def _(sp):
            for dst, src in ((identb[:, :], a["c_identb"]), (swap[:, :], a["c_swap"]),
                             (ropec[:, :], a["c_ropec"]), (ropes[:, :], a["c_ropes"])):
                sp.dma_start(dst, src).then_inc(const_in, 16)
            for i, name in enumerate(("q_gain", "k_gain")):
                sp.dma_start(gain[:, :].rearrange("p (g i) -> p i g", i=2)[:, i, :],
                             a[name][0].rearrange("g p -> p g"), allow_slow_non_contiguous=True
                             ).then_inc(const_in, 16)

            def load_w(at, j):
                sp.dma_start(w[:, j % 2, :, :], pr.w_in[:, :, bass.ds(at + w_col[j], P)]
                             ).then_inc(w_loaded[j % 2], 16)

            def load_wv(at):
                for g in range(AG):
                    sp.dma_start(wv[:, :, g, :], pr.w_in[:, :, bass.ds(at + (V_COL + g * HEADS * P), P)]
                                 ).then_inc(wv_loaded, 16)

            load_w(0, 0)
            load_w(0, 1)
            load_wv(0)

            def head(h, ahead):
                at = h * P if not ahead else sp.snap(h * P)
                for j in range(2, NB):
                    sp.wait_ge(raw, NR * h + 3 * (j - 1))
                    load_w(at, j)
                if ahead:
                    for j in range(2):
                        sp.wait_ge(raw, NR * h + 3 * (NB - 1 + j))
                        load_w(at + P, j)
                for t in range(TILES):
                    if t == 0:
                        sp.wait_ge(raw, NR * h + NR)
                    if t >= 2:
                        sp.wait_ge(scored, TILES * h + t - 1)
                    sp.dma_start(mask[:, t % 2, 0:P * len(blocks(t))], a["c_mask"][t][:, 0:P * len(blocks(t))]
                                 ).then_inc(mask_in[t % 2], 16)
                    if t == 0 and ahead:
                        load_wv(at + P)

            with sp.Fori(0, HEADS - 1) as h:
                head(h, True)
            head(HEADS - 1, False)

        @block.tensor
        def _(pe):
            pe.wait_ge(const_in, 96)
            pe.wait_ge(set_up, 2)

            def raw_unit(h, u):
                j, c0, n = UNITS[u]
                if u % 3 == 0:
                    pe.wait_ge(w_loaded[j % 2], 16 * (NB // 2 * h + j // 2 + 1))
                if u >= 3:
                    pe.wait_ge(normed, NU * h + u - 2)
                for k in range(DC):
                    last = nc.tensor.matmul(pr.psum[:, u % 3, 0:n], w[:, j % 2, k, :],
                                            pr.xnT[:, k, c0:c0 + n], start=k == 0, stop=k == DC - 1)
                last.then_inc(raw, 1)

            def mean_unit(h, u):
                n = UNITS[u][2]
                pe.wait_ge(squared, NU * h + u + 1)
                if u >= 2:
                    pe.wait_ge(rooted, NU * h + u - 1)
                nc.tensor.matmul(pr.psum[:, 3 + u % 2, 0:n], mean[:, :], sq[:, u % 2, 0:n],
                                 start=True, stop=True).then_inc(averaged, 1)

            def swap_unit(h, u):
                j, c0, n = UNITS[u]
                pe.wait_ge(normed, NU * h + u + 1)
                if u >= 2:
                    pe.wait_ge(roped, 3 * (NU * h + u - 1))
                nc.tensor.matmul(pr.psum[0:2 * ROPE, 5 + u % 2, 0:n], swap[:, :], qk[0:ROPE, j, c0:c0 + n],
                                 start=True, stop=True).then_inc(swapped, 1)

            def v_tile(h, t):
                u = NU + t
                if t == 0:
                    pe.wait_ge(wv_loaded, 48 * h + 48)
                if t < 3:
                    pe.wait_ge(normed, NU * h + u - 2)
                else:
                    pe.wait_ge(v_ready, TILES * h + t - 2)
                for k in range(DC):
                    last = nc.tensor.matmul(pr.psum[:, u % 3, 0:AG * P], pr.xnT[:, k, t * P:(t + 1) * P],
                                            wv[:, k, :, :], start=k == 0, stop=k == DC - 1)
                last.then_inc(raw, 1)

            def scores(h, t):
                at = 0
                pe.wait_ge(mask_in[t % 2], 16 * (TILES // 2 * h + t // 2 + 1))
                if t >= 1:
                    pe.wait_ge(expd, TILES * h + t)
                for g, (k0, n) in enumerate(key_runs(t)):
                    for c in range(0, n, 512):
                        m = min(512, n - c)
                        s = pr.banks(0, 3)[:, at:at + m]
                        nc.tensor.matmul(s, identb[:, :], mask[:, t % 2, at:at + m], start=True, stop=False)
                        last = nc.tensor.matmul(s, qk[:, 2 * g, t * P:(t + 1) * P],
                                                qk[:, 2 * g + 1, k0 + c:k0 + c + m], start=False, stop=True)
                        at += m
                last.then_inc(scored, 1)

            def turn(h, t):
                n = len(blocks(t))
                pe.wait_ge(expd, TILES * h + t + 1)
                for q in range(first_quad[t], first_quad[t + 1]):
                    if q >= 3:
                        if (q - 3) % 2 == 0:
                            pe.wait_ge(kept_a, even[NQ] * h + even[q - 2])
                        else:
                            pe.wait_ge(kept_v, (NQ - even[NQ]) * h + q - 2 - even[q - 2])
                    x0 = QUAD * (q - first_quad[t])
                    for x in range(x0, min(x0 + QUAD, n)):
                        last = nc.tensor.transpose(quad_bank(q)[:, (x - x0) * P:(x - x0 + 1) * P],
                                                   prob[:, t % 2, x * P:(x + 1) * P], pr.ident[:, :])
                    last.then_inc(turned, 1)

            def weigh(h, t):
                end = first_quad[t + 1]
                pe.wait_ge(kept_a, even[NQ] * h + even[end])
                pe.wait_ge(kept_v, (NQ - even[NQ]) * h + end - even[end])
                bl = blocks(t)
                for x, (g, kt) in enumerate(bl):
                    last = nc.tensor.matmul(pr.psum[:, 6, 0:P], probT[:, x * P:(x + 1) * P], v[:, kt, g, :],
                                            start=x == 0, stop=x == len(bl) - 1)
                last.then_inc(weighed, 1)

            def turn_out(h, t):
                pe.wait_ge(out_ready, TILES * h + t + 1)
                if t >= 1:
                    pe.wait_ge(out_kept, TILES * h + t)
                nc.tensor.transpose(pr.psum[:, 7, 0:P], out[:, t % 2, :], pr.ident[:, :]
                                    ).then_inc(out_turned, 1)

            with pe.Fori(0, HEADS) as h:
                for u in range(NU + 2):
                    if u < NU:
                        raw_unit(h, u)
                    if 1 <= u <= NU:
                        mean_unit(h, u - 1)
                    if u == NU:
                        v_tile(h, 0)
                    if u == NU + 1:
                        v_tile(h, 1)
                        v_tile(h, 2)
                    if u >= 2:
                        swap_unit(h, u - 2)
                for t in range(3, TILES):
                    v_tile(h, t)
                pe.wait_ge(roped, 3 * NU * h + 3 * NU)
                pe.wait_ge(v_ready, TILES * h + TILES)
                scores(h, 0)
                for t in range(TILES):
                    if t + 1 < TILES:
                        scores(h, t + 1)
                    turn(h, t)
                    if t >= 1:
                        turn_out(h, t - 1)
                    weigh(h, t)
                turn_out(h, TILES - 1)
                pe.wait_ge(out_kept, TILES * h + TILES)

        @block.scalar
        def _(act):
            act.wait_ge(set_up, 2)

            def square(h, u):
                n = UNITS[u][2]
                act.wait_ge(raw, NR * h + u + 1)
                if u >= 2:
                    act.wait_ge(averaged, NU * h + u - 1)
                nc.scalar.activation(sq[:, u % 2, 0:n], pr.psum[:, u % 3, 0:n], ACT.Square
                                     ).then_inc(squared, 1)

            def root_of(h, u):
                n = UNITS[u][2]
                act.wait_ge(averaged, NU * h + u + 1)
                if u >= 2:
                    act.wait_ge(normed, NU * h + u - 1)
                nc.scalar.activation(root[:, u % 2, 0:n], pr.psum[:, 3 + u % 2, 0:n], ACT.Sqrt,
                                     bias=eps[:, 0:1]).then_inc(rooted, 1)

            def keep_quads(h, t):
                for q in range(first_quad[t], first_quad[t + 1]):
                    if q % 2 == 0:
                        x = QUAD * (q - first_quad[t])
                        m = P * min(QUAD, len(blocks(t)) - x)
                        act.wait_ge(turned, NQ * h + q + 1)
                        if t >= 1 and q < first_quad[t] + 2:
                            act.wait_ge(weighed, TILES * h + t)
                        nc.scalar.copy(probT[:, x * P:x * P + m], quad_bank(q)[:, 0:m]).then_inc(kept_a, 1)

            with act.Fori(0, HEADS) as h:
                for u in range(NU + 1):
                    if u < NU:
                        square(h, u)
                    if u >= 1:
                        root_of(h, u - 1)
                for t in range(TILES):
                    act.wait_ge(raw, NR * h + NU + t + 1)
                    nc.scalar.copy(v[:, t, :, :].rearrange("p g e -> p (g e)"),
                                   pr.psum[:, (NU + t) % 3, 0:AG * P]).then_inc(v_ready, 1)
                for t in range(TILES + 1):
                    if t < TILES:
                        act.wait_ge(shifted, TILES * h + t + 1)
                        if t >= 2:
                            act.wait_ge(turned, NQ * h + first_quad[t - 1])
                        nc.scalar.activation(prob[:, t % 2, 0:P * len(blocks(t))], score_banks(t), ACT.Exp,
                                             bias=stat[:, t % 2, 1:2], scale=SCALE,
                                             accum_out=stat[:, t % 2, 2:3]).then_inc(expd, 1)
                    if t >= 1:
                        keep_quads(h, t - 1)
                    if t >= 2:
                        act.wait_ge(out_turned, TILES * h + t - 1)
                        nc.scalar.copy(pr.branchT[:, bass.ds(h + FG, 1), (t - 2) * P:(t - 1) * P].rearrange(
                            "p o n -> p (o n)"), pr.psum[:, 7, 0:P]).then_inc(out_kept, 1)
                act.wait_ge(out_turned, TILES * h + TILES)
                nc.scalar.copy(pr.branchT[:, bass.ds(h + FG, 1), (TILES - 1) * P:T].rearrange(
                    "p o n -> p (o n)"), pr.psum[:, 7, 0:P]).then_inc(out_kept, 1)

        @block.vector
        def _(dve):
            nc.vector.memset(mean[:, :], 1.0 / P).then_inc(set_up, 1)
            nc.vector.memset(eps[:, :], EPS).then_inc(set_up, 1)
            dve.wait_ge(const_in, 96)

            def norm_unit(h, u):
                j, c0, n = UNITS[u]
                dve.wait_ge(rooted, NU * h + u + 1)
                nc.vector.reciprocal(root[:, u % 2, 0:n], root[:, u % 2, 0:n]).then_inc(inverted, 1)
                dve.wait_ge(inverted, NU * h + u + 1)
                nc.vector.scalar_tensor_tensor(qk[:, j, c0:c0 + n], pr.psum[:, u % 3, 0:n], gain[:, j:j + 1],
                                               root[:, u % 2, 0:n], ALU.mult, ALU.mult).then_inc(normed, 1)

            def rope_unit(h, u):
                j, c0, n = UNITS[u]
                at = 3 * (NU * h + u)
                dve.wait_ge(swapped, NU * h + u + 1)
                nc.vector.tensor_tensor(rot[:, u % 2, 0:n], pr.psum[0:ROPE, 5 + u % 2, 0:n],
                                        ropes[:, c0:c0 + n], ALU.mult).then_inc(roped, 1)
                nc.vector.tensor_tensor(qk[0:ROPE, j, c0:c0 + n], qk[0:ROPE, j, c0:c0 + n],
                                        ropec[:, c0:c0 + n], ALU.mult).then_inc(roped, 1)
                dve.wait_ge(roped, at + 2)
                nc.vector.tensor_tensor(qk[0:ROPE, j, c0:c0 + n], qk[0:ROPE, j, c0:c0 + n],
                                        rot[:, u % 2, 0:n], ALU.add).then_inc(roped, 1)

            with dve.Fori(0, HEADS) as h:
                for u in range(NU + 1):
                    if u < NU:
                        norm_unit(h, u)
                    if u >= 1:
                        rope_unit(h, u - 1)
                for t in range(TILES + 1):
                    if t < TILES:
                        dve.wait_ge(scored, TILES * h + t + 1)
                        nc.vector.reduce_max(stat[:, t % 2, 0:1], score_banks(t), AX).then_inc(maxed, 1)
                        dve.wait_ge(maxed, TILES * h + t + 1)
                        nc.vector.tensor_scalar(stat[:, t % 2, 1:2], stat[:, t % 2, 0:1], -SCALE, None,
                                                ALU.mult).then_inc(shifted, 1)
                    if t >= 1:
                        s = t - 1
                        for q in range(first_quad[s], first_quad[s + 1]):
                            if q % 2 == 1:
                                x = QUAD * (q - first_quad[s])
                                m = P * min(QUAD, len(blocks(s)) - x)
                                dve.wait_ge(turned, NQ * h + q + 1)
                                if s >= 1 and q < first_quad[s] + 2:
                                    dve.wait_ge(weighed, TILES * h + s)
                                nc.vector.tensor_copy(probT[:, x * P:x * P + m], quad_bank(q)[:, 0:m]
                                                      ).then_inc(kept_v, 1)
                        dve.wait_ge(expd, TILES * h + s + 1)
                        nc.vector.reciprocal(stat[:, s % 2, 3:4], stat[:, s % 2, 2:3]).then_inc(summed, 1)
                        dve.wait_ge(summed, TILES * h + s + 1)
                        dve.wait_ge(weighed, TILES * h + s + 1)
                        if s >= 2:
                            dve.wait_ge(out_turned, TILES * h + s - 1)
                        nc.vector.tensor_scalar(out[:, s % 2, :], pr.psum[:, 6, 0:P], stat[:, s % 2, 3:4],
                                                None, ALU.mult).then_inc(out_ready, 1)


def first_then_loop(eng, count, body):
    body(0, True)
    with eng.Fori(1, count) as i:
        body(i, False)


def stage_mix(pr):
    nc, a = pr.nc, pr.a
    WC = 2 * DC + FG + HEADS
    w = pr.sb("w", [P, 2, WC, P], F32)
    sig = pr.sb("sig", [P, 2, 2, 512], F32)
    part = pr.sb("part", [P, 2, 2, 512], F32)
    w_loaded = [pr.sem(f"w_loaded{b}") for b in range(2)]
    produced = pr.sem("produced")
    gated = pr.sem("gated")
    steps = pr.sem("steps")
    NC = len(CHUNKS)
    w_f = a["w_fourier"][0].rearrange("(c p) n -> p c n", p=P)
    w_a = a["w_attn"][0].rearrange("(c p) n -> p c n", p=P)

    with nc.Block() as block:
        @block.sync
        def _(sp):
            def pair(i, first):
                for b in range(2):
                    if not first:
                        sp.wait_ge(produced, NC * (2 * i + b - 1))
                    at = 0
                    for view, col in ((pr.w_in, GA_COL), (pr.w_in, GB_COL), (w_f, 0), (w_a, 0)):
                        n = view.shape[1]
                        sp.dma_start(w[:, b, at:at + n, :], view[:, :, bass.ds(2 * P * i + (b * P + col), P)]
                                     ).then_inc(w_loaded[b], 16)
                        at += n

            first_then_loop(sp, DC // 2, pair)

        @block.tensor
        def _(pe):
            def pair(i, first):
                for v in range(2 * NC):
                    b, (c0, n) = v // NC, CHUNKS[v % NC]
                    if v % NC == 0:
                        pe.wait_ge(w_loaded[b], 64 * i + 64)
                    if not first or v >= 2:
                        pe.wait_ge(steps, 6 * NC * i + 3 * (v - 1))
                    at = 0
                    for s, (rhs, kc) in enumerate(((pr.xnT, DC), (pr.xnT, DC), (pr.branchT[:, 0:FG, :], FG),
                                                   (pr.branchT[:, FG:FG + HEADS, :], HEADS))):
                        for k in range(kc):
                            last = nc.tensor.matmul(pr.psum[:, 4 * (v % 2) + s, 0:n], w[:, b, at + k, :],
                                                    rhs[:, k, c0:c0 + n], start=k == 0, stop=k == kc - 1)
                        at += kc
                    last.then_inc(produced, 1)

            first_then_loop(pe, DC // 2, pair)

        @block.scalar
        def _(act):
            def pair(i, first):
                for v in range(2 * NC):
                    n = CHUNKS[v % NC][1]
                    act.wait_ge(produced, 2 * NC * i + v + 1)
                    for s in range(2):
                        nc.scalar.activation(sig[:, v % 2, s, 0:n], pr.psum[:, 4 * (v % 2) + s, 0:n],
                                             ACT.Sigmoid).then_inc(gated, 1)

            first_then_loop(act, DC // 2, pair)

        @block.vector
        def _(dve):
            def pair(i, first):
                for v in range(2 * NC):
                    b, (c0, n) = v // NC, CHUNKS[v % NC]
                    at = 6 * NC * i + 3 * v
                    dve.wait_ge(gated, 4 * NC * i + 2 * v + 2)
                    for s in range(2):
                        nc.vector.tensor_tensor(part[:, v % 2, s, 0:n], pr.psum[:, 4 * (v % 2) + 2 + s, 0:n],
                                                sig[:, v % 2, s, 0:n], ALU.mult).then_inc(steps, 1)
                    dve.wait_ge(steps, at + 2)
                    nc.vector.tensor_tensor(
                        pr.mixT[:, bass.ds(2 * i + b, 1), c0:c0 + n].rearrange("p o n -> p (o n)"),
                        part[:, v % 2, 0, 0:n], part[:, v % 2, 1, 0:n], ALU.add).then_inc(steps, 1)

            first_then_loop(dve, DC // 2, pair)


def stage_out(pr):
    nc, a = pr.nc, pr.a
    w = pr.branchT[:, :, :].rearrange("p c n -> p (c n)")[:, 0:DC * D].rearrange("p (c n) -> p c n", c=DC)
    mixb = pr.sb("mixb", [P, 2, DC, P], F32)
    x = pr.sb("x2", [P, 2, D], F32)
    h = pr.sb("h", [P, 2, D], F32)
    xn = pr.sb("xn2", [P, 2, D], F32)
    rest = pr.sb("rest", [P, 2, D], F32)
    parts = pr.sb("parts", [P, 3, D], BF16)
    g = pr.sb("g2", [P, D], F32)
    stat = pr.sb("stat2", [P, 2, 4], F32)
    x_in = [pr.sem(f"x_in{b}") for b in range(2)]
    const_in = pr.sem("const_in")
    picked = pr.sem("picked")
    product = pr.sem("product")
    h_ready = pr.sem("h_ready")
    squares = pr.sem("squares")
    means = pr.sem("means")
    roots = pr.sem("roots")
    inverse = pr.sem("inverse")
    normed = pr.sem("normed")
    split = pr.sem("split")
    first_parts = pr.sem("first_parts")
    turned = pr.sem("turned")
    kept = pr.sem("kept")
    h_out = [pr.sem(f"h_out{b}") for b in range(2)]
    parts_out = pr.sem("parts_out")
    noted = pr.sem("noted")

    with nc.Block() as block:
        @block.sync
        def _(sp):
            sp.dma_start(w, a["w_out"][0].rearrange("(c p) n -> p c n", p=P)).then_inc(const_in, 16)
            sp.dma_start(g[:, :], a["g_ffn"].to_broadcast([P, D])).then_inc(const_in, 16)

            def pair(n, r):
                for b in range(2):
                    k = 2 * n + b
                    if r is not None:
                        sp.wait_ge(h_ready, k - 1)
                    for c, rows in enumerate(rows_of(pr, pr.xp, pr.xs, n, r, b)):
                        sp.dma_start(x[RUN * c:RUN * (c + 1), b, :], rows).then_inc(x_in[b], 16)
                for b in range(2):
                    k = 2 * n + b
                    sp.wait_ge(h_ready, k + 1)
                    sp.dma_start(a["s_h"][bass.ds(k * P, P), :], h[:, b, :]).then_inc(h_out[b], 16)
                    wait_apart(sp, split, 2 * k + 2, noted)
                    for i in range(3):
                        sp.dma_start(a["s_xn"][i][bass.ds(k * P, P), :], parts[:, i, :]).then_inc(parts_out, 16)

            tile_pairs(sp, pair)
            sp.wait_ge(parts_out, 48 * TILES)
            for b in range(2):
                sp.wait_ge(h_out[b], 16 * TILES // 2)

        @block.scalar
        def _(act):
            def pair(n, r):
                for b in range(2):
                    k = 2 * n + b
                    if r is not None:
                        act.wait_ge(product, k - 1)
                    nc.scalar.copy(mixb[:, b, :, :], pr.mixT[:, :, bass.ds(k * P, P)]).then_inc(picked, 1)
                    act.wait_ge(h_ready, k + 1)
                    nc.scalar.activation(rest[:, b, :], h[:, b, :], ACT.Square,
                                         accum_out=stat[:, b, 0:1]).then_inc(squares, 1)
                    act.wait_ge(means, k + 1)
                    nc.scalar.activation(stat[:, b, 2:3], stat[:, b, 1:2], ACT.Sqrt).then_inc(roots, 1)
                    act.wait_ge(normed, k + 1)
                    if b == 1 or r is not None:
                        act.wait_ge(parts_out, 48 * k)
                    nc.scalar.copy(parts[:, 0, :], xn[:, b, :]).then_inc(first_parts, 1)
                    act.wait_ge(split, 2 * k + 1)
                    nc.scalar.copy(parts[:, 1, :], rest[:, b, :]).then_inc(first_parts, 1)
                    act.wait_ge(turned, k + 1)
                    nc.scalar.copy(pr.xnT[:, :, bass.ds(k * P, P)], pr.psum[:, 4 + 2 * b:6 + 2 * b, :].rearrange(
                        "p b (c n) -> p (b c) n", n=P)).then_inc(kept, 1)

            tile_pairs(act, pair)

        @block.vector
        def _(dve):
            dve.wait_ge(const_in, 32)

            def pair(n, r):
                for b in range(2):
                    k = 2 * n + b
                    dve.wait_ge(product, k + 1)
                    dve.wait_ge(x_in[b], 32 * n + 32)
                    if r is not None:
                        dve.wait_ge(h_out[b], 16 * n)
                    nc.vector.tensor_tensor(h[:, b, :], pr.banks(2 * b, 2), x[:, b, :], ALU.add
                                            ).then_inc(h_ready, 1)
                    dve.wait_ge(squares, k + 1)
                    nc.vector.tensor_scalar(stat[:, b, 1:2], stat[:, b, 0:1], 1.0 / D, EPS,
                                            ALU.mult, ALU.add).then_inc(means, 1)
                    dve.wait_ge(roots, k + 1)
                    nc.vector.reciprocal(stat[:, b, 3:4], stat[:, b, 2:3]).then_inc(inverse, 1)
                    dve.wait_ge(inverse, k + 1)
                    if r is not None:
                        dve.wait_ge(turned, k - 1)
                    nc.vector.scalar_tensor_tensor(xn[:, b, :], h[:, b, :], stat[:, b, 3:4], g[:, :],
                                                   ALU.mult, ALU.mult).then_inc(normed, 1)
                    dve.wait_ge(first_parts, 2 * k + 1)
                    nc.vector.tensor_tensor(rest[:, b, :], xn[:, b, :], parts[:, 0, :], ALU.subtract
                                            ).then_inc(split, 1)
                    dve.wait_ge(first_parts, 2 * k + 2)
                    nc.vector.tensor_tensor(parts[:, 2, :], rest[:, b, :], parts[:, 1, :], ALU.subtract
                                            ).then_inc(split, 1)

            tile_pairs(dve, pair)

        @block.tensor
        def _(pe):
            pe.wait_ge(const_in, 32)

            def pair(n, r):
                for b in range(2):
                    k = 2 * n + b
                    pe.wait_ge(picked, k + 1)
                    if r is not None:
                        pe.wait_ge(h_ready, k - 1)
                    for half in range(2):
                        for c in range(DC):
                            last = nc.tensor.matmul(pr.psum[:, 2 * b + half, :], mixb[:, b, c, :],
                                                    w[:, c, half * 512:half * 512 + 512],
                                                    start=c == 0, stop=c == DC - 1)
                    last.then_inc(product, 1)
                    pe.wait_ge(normed, k + 1)
                    if r is not None:
                        pe.wait_ge(kept, k - 1)
                    for c in range(DC):
                        last = nc.tensor.transpose(pr.psum[:, 4 + 2 * b + c // 4, c % 4 * P:c % 4 * P + P],
                                                   xn[:, b, c * P:(c + 1) * P], pr.ident[:, :])
                    last.then_inc(turned, 1)

            tile_pairs(pe, pair)


def stage_keys(pr):
    nc, a = pr.nc, pr.a
    run = pr.sb("run", [P, 3, 4, P], F32)
    w = pr.sb("w3", [P, 2, DC, P], F32)
    sk = pr.sb("sk", [P, 2, P], F32)
    skT = pr.sb("skT", [P, 2, P], F32)
    qT = pr.sb("qT", [P, 2, T], F32)
    w_loaded = [pr.sem(f"w_loaded{b}") for b in range(2)]
    turned = pr.sem("turned")
    keys_kept = pr.sem("keys_kept")
    projected = pr.sem("projected")
    q_kept = pr.sem("q_kept")
    scored = pr.sem("scored")
    kept = pr.sem("kept")
    run_out = [pr.sem(f"run_out{s}") for s in range(3)]
    wq = a["w_query"][0].rearrange("(c p) n -> p c n", p=P)
    RUNS = ((0, 4), (4, 4), (8, 2))

    with nc.Block() as block:
        @block.sync
        def _(sp):
            def head(i, first):
                for b in range(2):
                    if not first:
                        sp.wait_ge(projected, 3 * (2 * i + b - 1))
                    sp.dma_start(w[:, b, :, :], wq[:, :, bass.ds(2 * P * i + b * P, P)]).then_inc(w_loaded[b], 16)
                    sp.dma_start(sk[:, b, :], a["sub_keys"][0][bass.ds(i, 1), b, :, :].rearrange(
                        "o n d -> (o n) d")).then_inc(w_loaded[b], 16)

            first_then_loop(sp, PH, head)

        @block.tensor
        def _(pe):
            def head(i, first):
                for b in range(2):
                    m = 2 * i + b
                    pe.wait_ge(w_loaded[b], 32 * i + 32)
                    if not first or b:
                        pe.wait_ge(kept, 3 * m - 1)
                    nc.tensor.transpose(pr.psum[:, 7, 0:P], sk[:, b, :], pr.ident[:, :]).then_inc(turned, 1)
                    for c, (c0, n) in enumerate(CHUNKS):
                        if not first:
                            pe.wait_ge(q_kept, 3 * (m - 2) + c + 1)
                        for k in range(DC):
                            last = nc.tensor.matmul(pr.psum[:, 3 * b + c, 0:n], w[:, b, k, :],
                                                    pr.xnT[:, k, c0:c0 + n], start=k == 0, stop=k == DC - 1)
                        last.then_inc(projected, 1)
                    pe.wait_ge(keys_kept, m + 1)
                    pe.wait_ge(q_kept, 3 * m + 3)
                    for s, (t0, n) in enumerate(RUNS):
                        if not first or b or s == 2:
                            pe.wait_ge(kept, 3 * m + (0, 0, 1)[s] if s != 1 else 3 * m - 1)
                        for t in range(n):
                            last = nc.tensor.matmul(pr.psum[:, 6 + s % 2, t * P:(t + 1) * P],
                                                    qT[:, b, (t0 + t) * P:(t0 + t + 1) * P], skT[:, b, :],
                                                    start=True, stop=True)
                        last.then_inc(scored, 1)

            first_then_loop(pe, PH, head)

        @block.scalar
        def _(act):
            def store_runs(m):
                for s, (t0, n) in enumerate(RUNS):
                    act.wait_ge(kept, 3 * m + s + 1)
                    act.dma_start(a["s_score"][t0:t0 + n, :, bass.ds(m, 1), :].rearrange("t p o k -> p t (o k)"),
                                  run[:, s, 0:n, :]).then_inc(run_out[s], 16)

            def head(i, first):
                for b in range(2):
                    m = 2 * i + b
                    if b or not first:
                        store_runs(m - 1)
                    for c, (c0, n) in enumerate(CHUNKS):
                        act.wait_ge(projected, 3 * m + c + 1)
                        if not first:
                            act.wait_ge(scored, 3 * m - 3)
                        nc.scalar.copy(qT[:, b, c0:c0 + n], pr.psum[:, 3 * b + c, 0:n]).then_inc(q_kept, 1)

            first_then_loop(act, PH, head)
            store_runs(2 * PH - 1)
            for s in range(3):
                act.wait_ge(run_out[s], 16 * 2 * PH)

        @block.vector
        def _(dve):
            def head(i, first):
                for b in range(2):
                    m = 2 * i + b
                    dve.wait_ge(turned, m + 1)
                    nc.vector.tensor_copy(skT[:, b, :], pr.psum[:, 7, 0:P]).then_inc(keys_kept, 1)
                    for s, (t0, n) in enumerate(RUNS):
                        dve.wait_ge(scored, 3 * m + s + 1)
                        if b or not first:
                            dve.wait_ge(run_out[s], 16 * m)
                        nc.vector.tensor_copy(
                            run[:, s, 0:n, :],
                            pr.psum[:, 6 + s % 2, 0:n * P].rearrange("p (t k) -> p t k", k=P)).then_inc(kept, 1)

            first_then_loop(dve, PH, head)


def stage_experts(pr):
    nc, a = pr.nc, pr.a
    HH = 2 * PH
    U_SLOTS, V_SLOTS = OCTET, 2 * OCTET
    GROUPS, OCTETS = P // GROUP, P // OCTET
    u = pr.sb("u", [P, U_SLOTS, D], F32)
    v = pr.sb("v", [P, V_SLOTS, D], F32)
    idx = pr.sb("idx", [P, 2, GROUP], U32)
    gate = pr.sb("gate", [P, 2, GROUP], F32)
    xrow = pr.sb("xrow", [96, 2, D], BF16)
    select = pr.sb("select", [96, GROUP, P], BF16)
    hrow = pr.sb("hrow", [GROUP, 2, D], F32)
    y = pr.sb("y", [GROUP, 2, D], F32)
    dot = pr.sb("dot", [P, 2, OCTET], F32)
    act_u = pr.sb("act_u", [P, 2, OCTET], F32)
    weight = pr.sb("weight", [P, 2, GROUP, GROUP], F32)
    u_in = [pr.sem(f"u_in{i}") for i in range(U_SLOTS)]
    v_in = [pr.sem(f"v_in{i}") for i in range(V_SLOTS)]
    const_in = pr.sem("const_in")
    zeroed = pr.sem("zeroed")
    group_in = [pr.sem(f"group_in{b}") for b in range(2)]
    spread = pr.sem("spread")
    dotted = pr.sem("dotted")
    gelued = pr.sem("gelued")
    weighted = pr.sem("weighted")
    v_used = pr.sem("v_used")
    y_ready = pr.sem("y_ready")
    y_out = [pr.sem(f"y_out{b}") for b in range(2)]
    noted = pr.sem("noted")
    LOADS = 6 * 16

    sc = pr.sb("sc", [P, HH, N_KEYS], F32)
    left = pr.sb("left", [P, HH * N_KEYS], F32)
    best = pr.sb("best", [P, HH, TOPK], F32)
    besti = pr.sb("besti", [P, HH, TOPK], U32)
    bestf = pr.sb("bestf", [P, HH, TOPK], F32)
    cand = pr.sb("cand", [P, PH, TOPK, TOPK], F32)
    pick = pr.sb("pick", [P, 2, PH, TOPK, TOPK], F32)
    top = pr.sb("top", [P, PH, TOPK], F32)
    topi = pr.sb("topi", [P, PH, TOPK], U32)
    part = pr.sb("part", [P, 2, PH, TOPK], U32)
    partf = pr.sb("partf", [P, 2, PH, TOPK], F32)
    key = pr.sb("key", [P, 2, PH, TOPK], F32)
    expert = pr.sb("expert", [P, PH, TOPK], F32)
    share = pr.sb("share", [P, PH, TOPK], F32)
    total = pr.sb("total", [P, 2, PH], F32)
    iota = pr.sb("iota", [P, TOPK], F32)
    idxT = pr.sb("idxT", [P, P], U32)
    gateT = pr.sb("gateT", [P, P], F32)
    sc_in = pr.sem("sc_in")
    phase = pr.sem("phase")
    shifted = pr.sem("shifted")
    expd = pr.sem("expd")
    routed = pr.sem("routed")
    turned = pr.sem("turned")
    kept = pr.sem("kept")
    stored = pr.sem("stored")
    half = best[:, :, :].rearrange("p (h c) k -> p h c k", c=2)
    keys = bestf[:, :, :].rearrange("p (h c) k -> p h c k", c=2)
    full = [P, PH, TOPK, TOPK]
    flat = cand[:, :, :, :].rearrange("p h a b -> p h (a b)")
    left1 = left[:, :].rearrange("p (h k) -> p h k", k=N_KEYS)
    left2 = left[:, :].rearrange("p (h k) -> p h k", k=TOPK * TOPK)
    BEST, BEST_AT, NEXT, NEXT_AT = (HH * i for i in range(4))
    CAND = 4 * HH
    TOP, TOP_AT, TOP_NEXT, TOP_NEXT_AT = (CAND + 1 + PH * i for i in range(4))
    SHIFT = CAND + 1 + 4 * PH
    PARTS, ONE_HOT, VALUES, SUMS, TOTAL, JOIN, SHARES = (SHIFT + x for x in (1, 2, 4, 6, 8, 9, 10))
    STARTS = (BEST, BEST_AT, NEXT, NEXT_AT, CAND, TOP, TOP_AT, TOP_NEXT, TOP_NEXT_AT, SHIFT, PARTS,
              ONE_HOT, VALUES, SUMS, TOTAL, JOIN, SHARES)
    ENDS = tuple(x - 1 for x in STARTS[1:])
    TURN = P - GROUP
    GATES_OCTET, KEPT_OCTET = TOTAL // OCTET - 1, TURN // OCTET - 1

    def tiles(eng, body):
        body(0, True, False)
        with eng.Fori(1, TILES - 1) as n:
            body(n, False, False)
        body(TILES - 1, False, True)

    with nc.Block() as block:
        @block.sync
        def _(sp):
            sp.dma_start(iota[:, :], a["c_iota"]).then_inc(const_in, 16)
            sp.dma_start(select[:, :, :].rearrange("p g n -> p (g n)"), a["c_select"]).then_inc(const_in, 16)

            def load_scores(n):
                sp.dma_start(sc[:, :, :], a["s_score"][bass.ds(n, 1)].rearrange("o p h k -> (o p) h k")
                             ).then_inc(sc_in, 16)

            def store_routes(n):
                wait_apart(sp, kept, 2 * n + 2, noted)
                for name, src in (("s_idx", idxT), ("s_gate", gateT)):
                    sp.dma_start(a[name][bass.ds(n, 1)].rearrange("o p n -> (o p) n"), src[:, :]
                                 ).then_inc(stored, 16)
                wait_apart(sp, stored, 32 * n + 32, noted)

            load_scores(0)
            store_routes(0)
            sp.wait_ge(zeroed, 3)

            def tile(n, first, last):
                if not last:
                    load_scores(n + 1)
                for g in range(GROUPS):
                    b = g % 2
                    if not first or g >= 2:
                        wait_apart(sp, y_ready, GROUPS * n + g - 1, noted)
                    col = P * n + GROUP * g
                    for dst, name in ((idx, "s_idx"), (gate, "s_gate")):
                        sp.dma_start(dst[:, b, :], a[name][bass.ds(n, 1), :, g * GROUP:(g + 1) * GROUP].rearrange(
                            "o p n -> (o p) n")).then_inc(group_in[b], 16)
                    for i in range(3):
                        sp.dma_start(xrow[32 * i:32 * i + GROUP, b, :], a["s_xn"][i][bass.ds(col, GROUP), :]
                                     ).then_inc(group_in[b], 16)
                    sp.dma_start(hrow[:, b, :], a["s_h"][bass.ds(col, GROUP), :]).then_inc(group_in[b], 16)
                if not last:
                    store_routes(n + 1)

            tiles(sp, tile)

        @block.gpsimd
        def _(pool):
            def tile(n, first, last):
                for s in range(P):
                    g, i = s // GROUP, s % GROUP
                    if i == 0:
                        wait_apart(pool, group_in[g % 2], LOADS * (GROUPS // 2 * n + g // 2 + 1), noted)
                    if not first or s >= U_SLOTS:
                        wait_apart(pool, dotted, P * n + s - U_SLOTS + 1, noted)
                    at = bass.IndirectOffsetOnAxis(ap=idx[:, g % 2, i:i + 1], axis=0)
                    pool.indirect_dma_start(u[:, s % U_SLOTS, :], None, a["expert_u"][0], at
                                            ).then_inc(u_in[s % U_SLOTS], 16)
                    if not first or s >= V_SLOTS:
                        wait_apart(pool, v_used, P * n + s - V_SLOTS + 1, noted)
                    pool.indirect_dma_start(v[:, s % V_SLOTS, :], None, a["expert_v"][0], at
                                            ).then_inc(v_in[s % V_SLOTS], 16)

            tiles(pool, tile)

        @block.tensor
        def _(pe):
            def turn_routes(n, bank):
                pe.wait_ge(routed, 2 * n + 2)
                nc.tensor.transpose(pr.psum[:, bank, 0:P], expert[:, :, :].rearrange("p h k -> p (h k)"),
                                    pr.ident[:, :])
                nc.tensor.transpose(pr.psum[:, bank, P:2 * P], share[:, :, :].rearrange("p h k -> p (h k)"),
                                    pr.ident[:, :]).then_inc(turned, 1)

            turn_routes(0, 6)
            pe.wait_ge(kept, 2)
            pe.wait_ge(const_in, 32)
            pe.wait_ge(zeroed, 3)

            def spread_x(n, s, first):
                g, i = s // GROUP, s % GROUP
                if i == 0:
                    pe.wait_ge(group_in[g % 2], LOADS * (GROUPS // 2 * n + g // 2 + 1))
                if not first or s >= 2:
                    pe.wait_ge(dotted, P * n + s - 1)
                for hf in range(2):
                    last = nc.tensor.matmul(pr.psum[:, 2 * (s % 2) + hf, :], select[:, i, :],
                                            xrow[:, g % 2, hf * 512:hf * 512 + 512], start=True, stop=True)
                last.then_inc(spread, 1)

            def sum_v(n, s):
                q = s % P
                g, i = q // GROUP, q % GROUP
                if i % OCTET == 0:
                    pe.wait_ge(weighted, OCTETS * n + s // OCTET + 1)
                pe.wait_ge(v_in[q % V_SLOTS], 16 * (P // V_SLOTS * n + s // V_SLOTS + 1))
                for hf in range(2):
                    last = nc.tensor.matmul(pr.psum[0:GROUP, 4 + 2 * (g % 2) + hf, :], weight[:, g % 2, i, :],
                                            v[:, q % V_SLOTS, hf * 512:hf * 512 + 512],
                                            start=i == 0, stop=i == GROUP - 1)
                last.then_inc(v_used, 1)

            def tile(n, first, last):
                for s in range(P):
                    if s == TURN and not last:
                        pe.wait_ge(y_ready, GROUPS * n + GROUPS - 2)
                        turn_routes(n + 1, 6)
                    if s == TURN + OCTET and not last:
                        pe.wait_ge(kept, 2 * n + 4)
                    spread_x(n, s, first)
                    if not first or s >= OCTET:
                        sum_v(n, s - OCTET)

            tiles(pe, tile)
            for s in range(P - OCTET, P):
                sum_v(TILES - 1, s)

        @block.vector
        def _(dve):
            nc.vector.memset(weight[:, :, :, :], 0.0).then_inc(zeroed, 1)
            nc.vector.memset(xrow[:, 0, :], 0.0).then_inc(zeroed, 1)
            nc.vector.memset(xrow[:, 1, :], 0.0).then_inc(zeroed, 1)
            dve.wait_ge(const_in, 32)

            def route(n, s, fresh):
                if s == BEST:
                    wait_apart(dve, sc_in, 16 * n + 16, noted)
                elif s in STARTS:
                    wait_apart(dve, phase, len(ENDS) * n + STARTS.index(s), noted)
                if s == SHIFT and not fresh:
                    dve.wait_ge(turned, n)
                ins = None
                if BEST <= s < BEST_AT:
                    ins = nc.vector.max(best[:, s, 0:8], sc[:, s, :])
                elif s < NEXT:
                    i = s - BEST_AT
                    nc.vector.max_index(besti[:, i, 0:8], best[:, i, 0:8], sc[:, i, :])
                    ins = nc.vector.match_replace(left1[:, i, :], best[:, i, 0:8], sc[:, i, :], LOWEST)
                elif s < NEXT_AT:
                    i = s - NEXT
                    ins = nc.vector.max(best[:, i, 8:16], left1[:, i, :])
                elif s < CAND:
                    i = s - NEXT_AT
                    ins = nc.vector.max_index(besti[:, i, 8:16], best[:, i, 8:16], left1[:, i, :])
                elif s == CAND:
                    nc.vector.tensor_copy(bestf[:, :, :], besti[:, :, :])
                    ins = nc.vector.tensor_tensor(cand[:, :, :, :], half[:, :, 0, :].unsqueeze(3).to_broadcast(full),
                                                  half[:, :, 1, :].unsqueeze(2).to_broadcast(full), ALU.add)
                elif s < TOP_AT:
                    i = s - TOP
                    ins = nc.vector.max(top[:, i, 0:8], flat[:, i, :])
                elif s < TOP_NEXT:
                    i = s - TOP_AT
                    nc.vector.max_index(topi[:, i, 0:8], top[:, i, 0:8], flat[:, i, :])
                    ins = nc.vector.match_replace(left2[:, i, :], top[:, i, 0:8], flat[:, i, :], LOWEST)
                elif s < TOP_NEXT_AT:
                    i = s - TOP_NEXT
                    ins = nc.vector.max(top[:, i, 8:16], left2[:, i, :])
                elif s < SHIFT:
                    i = s - TOP_NEXT_AT
                    ins = nc.vector.max_index(topi[:, i, 8:16], top[:, i, 8:16], left2[:, i, :])
                elif s == SHIFT:
                    nc.vector.tensor_tensor(share[:, :, :], top[:, :, :], top[:, :, 0:1].to_broadcast(
                        [P, PH, TOPK]), ALU.subtract).then_inc(shifted, 1)
                    nc.vector.tensor_scalar(part[:, 0, :, :], topi[:, :, :], 4, None, ALU.logical_shift_right)
                    ins = nc.vector.tensor_scalar(part[:, 1, :, :], topi[:, :, :], TOPK - 1, None, ALU.bitwise_and)
                elif s == PARTS:
                    ins = nc.vector.tensor_copy(partf[:, :, :, :], part[:, :, :, :])
                elif s < VALUES:
                    c = s - ONE_HOT
                    ins = nc.vector.tensor_tensor(
                        pick[:, c, :, :, :], partf[:, c, :, :].unsqueeze(3).to_broadcast(full),
                        iota[:, :].unsqueeze(1).unsqueeze(1).to_broadcast(full), ALU.is_equal)
                elif s < SUMS:
                    c = s - VALUES
                    ins = nc.vector.tensor_tensor(pick[:, c, :, :, :], pick[:, c, :, :, :],
                                                  keys[:, :, c, :].unsqueeze(2).to_broadcast(full), ALU.mult)
                elif s < TOTAL:
                    c = s - SUMS
                    ins = nc.vector.tensor_reduce(key[:, c, :, :].rearrange("p h k -> p (h k)"),
                                                  pick[:, c, :, :, :].rearrange("p h k j -> p (h k) j"), AX, ALU.add)
                elif s == TOTAL:
                    dve.wait_ge(expd, n + 1)
                    ins = nc.vector.tensor_reduce(total[:, 0, :], share[:, :, :], AX, ALU.add)
                elif s == JOIN:
                    nc.vector.scalar_tensor_tensor(expert[:, :, :].rearrange("p h k -> p (h k)"),
                                                   key[:, 0, :, :].rearrange("p h k -> p (h k)"), float(N_KEYS),
                                                   key[:, 1, :, :].rearrange("p h k -> p (h k)"),
                                                   ALU.mult, ALU.add).then_inc(routed, 1)
                    ins = nc.vector.reciprocal(total[:, 1, :], total[:, 0, :])
                elif s == SHARES:
                    nc.vector.tensor_tensor(share[:, :, :], share[:, :, :],
                                            total[:, 1, :].unsqueeze(2).to_broadcast([P, PH, TOPK]), ALU.mult
                                            ).then_inc(routed, 1)
                if s in ENDS:
                    ins.then_inc(phase, 1)

            def weights(n, o):
                q = o % OCTETS
                g, c = q // 2, q % 2
                diag = weight[:, g % 2, :, :].rearrange("p i j -> p (i j)")
                at = OCTET * c * (GROUP + 1)
                dve.wait_ge(gelued, OCTETS * n + o + 1)
                nc.vector.tensor_tensor(diag[:, at:at + (OCTET - 1) * (GROUP + 1) + 1:GROUP + 1],
                                        act_u[:, c, :], gate[:, g % 2, c * OCTET:(c + 1) * OCTET],
                                        ALU.mult).then_inc(weighted, 1)

            def add_h(n, g, fresh):
                b = g % 2
                dve.wait_ge(v_used, P * n + GROUP * (g + 1))
                if not fresh:
                    dve.wait_ge(y_out[b], 16 * (GROUPS // 2 * n + g // 2))
                nc.vector.tensor_tensor(y[:, b, :], pr.psum[0:GROUP, 4 + 2 * b:6 + 2 * b, :].rearrange(
                    "p b n -> p (b n)"), hrow[:, b, :], ALU.add).then_inc(y_ready, 1)

            def tile(n, first, last):
                for s in range(P):
                    o = s // OCTET
                    dve.wait_ge(u_in[s % U_SLOTS], 16 * (OCTETS * n + o + 1))
                    dve.wait_ge(spread, P * n + s + 1)
                    nc.vector.tensor_tensor_reduce(u[:, s % U_SLOTS, :], u[:, s % U_SLOTS, :],
                                                   pr.banks(2 * (s % 2), 2), 1.0, 0.0, ALU.mult, ALU.add,
                                                   dot[:, o % 2, s % OCTET:s % OCTET + 1]).then_inc(dotted, 1)
                    if s % OCTET == 0 and (not first or o):
                        weights(n, o - 1)
                    if s % GROUP == OCTET - 1 and (not first or s >= GROUP):
                        add_h(n, s // GROUP - 1, first and s < 3 * GROUP)
                    if not last:
                        route(n + 1, s, False)

            for s in range(SHARES + 1):
                route(0, s, True)
            dve.wait_ge(zeroed, 3)
            tiles(dve, tile)
            weights(TILES - 1, OCTETS - 1)
            add_h(TILES - 1, GROUPS - 1, False)

        @block.scalar
        def _(act):
            def gates(n):
                act.wait_ge(shifted, n + 1)
                nc.scalar.activation(share[:, :, :], share[:, :, :], ACT.Exp).then_inc(expd, 1)

            def keep(n, fresh):
                act.wait_ge(turned, n + 1)
                if not fresh:
                    act.wait_ge(stored, 32 * n)
                nc.scalar.copy(idxT[:, :], pr.psum[:, 6, 0:P]).then_inc(kept, 1)
                nc.scalar.copy(gateT[:, :], pr.psum[:, 6, P:2 * P]).then_inc(kept, 1)

            gates(0)
            keep(0, True)

            def tile(n, r, b, first, last):
                for o in range(OCTETS):
                    act.wait_ge(dotted, P * n + OCTET * (o + 1))
                    if o >= 2 or not first:
                        act.wait_ge(weighted, OCTETS * n + o - 1)
                    nc.scalar.activation(act_u[:, o % 2, :], dot[:, o % 2, :], ACT.Gelu_apprx_tanh
                                         ).then_inc(gelued, 1)
                    if o == GATES_OCTET and not last:
                        gates(n + 1)
                    if o == KEPT_OCTET and not last:
                        keep(n + 1, False)
                    if o % 2 == 1:
                        g = o // 2
                        rows = rows_of(pr, pr.yp, pr.ys, n, r, b)[g // (GROUPS // 2)]
                        at = g % (GROUPS // 2) * GROUP
                        act.wait_ge(y_ready, GROUPS * n + g + 1)
                        act.dma_start(rows[at:at + GROUP, :], y[:, g % 2, :]).then_inc(y_out[g % 2], 16)

            for b in range(2):
                tile(b, None, b, b == 0, False)
            with act.Fori(0, PHASE - 1) as r:
                for b in range(2):
                    tile(2 * r + 2 + b, r, b, False, False)
            for b in range(2):
                tile(TILES - 2 + b, PHASE - 1, b, False, b == 1)
            for b in range(2):
                act.wait_ge(y_out[b], 16 * TILES * GROUPS // 2)


def build(nc, a, stop=99):
    with ExitStack() as ctx:
        pr = Program(nc, a, ctx)

        def run(stage):
            with ExitStack() as own:
                pr.stage, pr.prefix = own, stage.__name__.removeprefix("stage_") + "_"
                stage(pr)
            pr.prefix = ""

        with ExitStack() as wide:
            pr.stage = wide
            pr.xnT = pr.sb("xnT", [P, DC, T], F32)
            with ExitStack() as branches:
                pr.stage = branches
                pr.branchT = pr.sb("branchT", [P, FG + HEADS, T], F32)
                run(stage_norm)
                run(stage_fourier)
                run(stage_attention)
                with ExitStack() as mix:
                    pr.stage = mix
                    pr.mixT = pr.sb("mixT", [P, DC, T], F32)
                    run(stage_mix)
                    run(stage_out)
            run(stage_keys)
        run(stage_experts)
    return pr


_INS = ["x_prompt", "x_sample", "g_mix", "w_in", "q_gain", "k_gain", "w_fourier", "w_attn", "w_out",
        "g_ffn", "w_query", "sub_keys", "expert_u", "expert_v"]
_OUTS = {"y_prompt": (1, SEQ, D), "y_sample": (1, DEC_SEQ, D)}


def kernel(**inputs):
    import concourse.bacc as bacc
    from concourse.bass_utils import run_bass_kernel_spmd

    nc = bacc.Bacc("TRN2", target_bir_lowering=False, num_devices=1)
    arrays, a = {}, {}
    for name, value in [(n, inputs[n]) for n in _INS] + list(constants().items()):
        value = np.ascontiguousarray(value)
        arrays[f"in_{name}"] = value
        a[name] = nc.dram_tensor(f"in_{name}", value.shape, mybir.dt.from_np(value.dtype),
                                 kind="ExternalInput").ap()
    for name, shape in _OUTS.items():
        a[name] = nc.dram_tensor(name, shape, F32, kind="ExternalOutput").ap()
    a["s_h"] = nc.dram_tensor("s_h", (T, D), F32, kind="Internal").ap()
    a["s_xn"] = nc.dram_tensor("s_xn", (3, T, D), BF16, kind="Internal").ap()
    for name, dt in (("s_idx", U32), ("s_gate", F32)):
        a[name] = nc.dram_tensor(name, (TILES, P, P), dt, kind="Internal").ap()
    a["s_score"] = nc.dram_tensor("s_score", (TILES, P, 2 * PH, N_KEYS), F32, kind="Internal").ap()
    build(nc, a)
    r = run_bass_kernel_spmd(nc, [arrays], core_ids=[0])
    return tuple(r.results[0][name] for name in _OUTS)
```

```python
from contextlib import ExitStack

import concourse.bass as bass
import numpy as np
from concourse import mybir

F32 = mybir.dt.float32
BF16 = mybir.dt.bfloat16
F32R = mybir.dt.float32r
U32 = mybir.dt.uint32
ALU = mybir.AluOpType
ACT = mybir.ActivationFunctionType
AX = mybir.AxisListType.X

P = 128
D = 1024
DC = D // P
SEQ = 256
DEC_SEQ = 1024
T = SEQ + DEC_SEQ
TILES = T // P
PHASE = 4
RUN = 64
CHUNKS = ((0, SEQ), (SEQ, 512), (SEQ + 512, 512))
FG = 4
AG = 3
HEADS = 4
ATTN_WIDTH = AG * HEADS * P
SPAN = 64
DILATIONS = (1, 4, 16)
ROPE = 32
ROPE_THETA = 500000.0
SCALE = float(P) ** -0.5
EPS = 1e-6
MASKED = -1e30
LOWEST = -3.0e38
Q_COL = FG * P
K_COL = Q_COL + ATTN_WIDTH
V_COL = K_COL + ATTN_WIDTH
GA_COL = V_COL + ATTN_WIDTH
GB_COL = GA_COL + D
PH = 8
TOPK = 16
SLOTS = PH * TOPK
N_KEYS = 128
GROUP = 16
OCTET = 8


def positions(batch):
    if batch == "prompt":
        return np.array([r + 4 * m for r in range(4) for m in range(64)])
    return np.array([r + 4 * k + 16 * i for r in range(4) for k in range(4) for i in range(64)])


def key_runs(tile):
    if tile < 2:
        return (0, SEQ), (tile * P, P), (tile * P, P)
    return (SEQ, DEC_SEQ), (SEQ + (tile - 2) // 2 * 256, 256), (tile * P, P)


def constants():
    bf16 = np.dtype("bfloat16")
    pp, ps = positions("prompt"), positions("sample")
    pos = np.concatenate([pp, ps])
    half = ROPE // 2
    inv = (np.float32(ROPE_THETA) ** (-np.arange(half, dtype=np.float32) * np.float32(2.0) / np.float32(ROPE)))
    ang = (pos.astype(np.float32)[None, :] * inv.astype(np.float32)[:, None]).astype(np.float64)
    cos, sin = np.cos(ang), np.sin(ang)
    rope_c = np.concatenate([cos, cos]).astype(np.float32)
    rope_s = np.concatenate([-sin, sin]).astype(np.float32)

    def dft(p, n):
        a = 2 * np.pi * (np.outer(p, p) % n) / n
        return np.cos(a) / np.sqrt(n), -np.sin(a) / np.sqrt(n)

    c, s = dft(np.arange(P), P)
    chan = np.concatenate([c, -s], axis=1).astype(np.float32)
    dft_s = np.stack(dft(ps, DEC_SEQ)).astype(np.float32)
    dft_p = np.stack(dft(pp, SEQ)).astype(np.float32)
    masks = np.full((TILES, P, DEC_SEQ + 256 + P), MASKED, np.float32)
    for t in range(TILES):
        at = 0
        same = np.zeros(T, bool)
        same[:SEQ] = t < 2
        same[SEQ:] = t >= 2
        q = pos[t * P:(t + 1) * P]
        for (k0, n), dil in zip(key_runs(t), DILATIONS):
            dist = np.abs(q[:, None] - pos[None, k0:k0 + n])
            ok = (dist % dil == 0) & (dist <= SPAN * dil)
            masks[t, :, at:at + n] = np.where(ok, 0.0, MASKED)
            at += n
    ident = np.eye(P, dtype=np.float32)
    select = np.zeros((96, GROUP * P), np.float32)
    for i in range(GROUP):
        for part in range(3):
            select[32 * part + i, i * P:(i + 1) * P] = 1.0
    return {
        "c_ident": ident,
        "c_identb": ident.astype(bf16),
        "c_ropec": rope_c,
        "c_ropes": rope_s,
        "c_chan": chan,
        "c_dfts": dft_s,
        "c_dftp": dft_p,
        "c_mask": masks.astype(bf16),
        "c_select": select.astype(bf16),
        "c_iota": np.broadcast_to(np.arange(TOPK, dtype=np.float32), (P, TOPK)).copy(),
    }


def wait_apart(eng, sem, value, noted):
    eng.wait_ge(sem, value)
    eng.sem_inc(noted, 1)


def high_bits(copy, high, x):
    return copy(high, x)


def parts(high, low, w_high, w_low):
    return (w_high, high), (w_high, low), (w_low, high)


class Program:

    def __init__(self, nc, a, ctx):
        self.nc, self.a, self.ctx = nc, a, ctx
        self.stage, self.prefix = ctx, ""
        self.xp = a["x_prompt"][0].rearrange("(m r) d -> r m d", r=4)
        self.xs = a["x_sample"][0].rearrange("(i k r) d -> r k i d", k=4, r=4)
        self.yp = a["y_prompt"][0].rearrange("(m r) d -> r m d", r=4)
        self.ys = a["y_sample"][0].rearrange("(i k r) d -> r k i d", k=4, r=4)
        self.w_in = a["w_in"][0].rearrange("(c p) n -> p c n", p=P)
        self.psum = ctx.enter_context(nc.psum_tensor("psum", [P, 8, 512], F32))
        self.ident = self.sb("ident", [P, P], F32)
        self.noted = self.sem("noted")
        self.top = self.sb("first_top", [P, PH, TOPK], F32)
        self.key = self.sb("first_key", [P, 2, PH, TOPK], F32)

    def sb(self, name, shape, dt):
        return self.stage.enter_context(self.nc.sbuf_tensor(self.prefix + name, shape, dt))

    def sb_at_one_place(self, *phases):
        tensors = []
        for i, phase in enumerate(phases):
            with ExitStack() as own:
                for name, shape, dt in phase:
                    keep = self.stage if i == len(phases) - 1 else own
                    tensors.append(keep.enter_context(self.nc.sbuf_tensor(self.prefix + name, shape, dt)))
        return tensors

    def sem(self, name):
        return self.stage.enter_context(self.nc.semaphore(self.prefix + name))

    def banks(self, first, n=1):
        return self.psum[:, first:first + n, :].rearrange("p b n -> p (b n)")


def rows_of(pr, view_p, view_s, n, r, b):
    if r is None:
        return [view_p[2 * b + c] for c in range(2)]
    return [view_s[bass.ds(r, 1), 2 * b + c, :, :].rearrange("o i d -> (o i) d") for c in range(2)]


def tile_pairs(eng, body):
    body(0, None)
    with eng.Fori(0, PHASE) as r:
        body(r + 1, r)


def stage_norm(pr):
    nc, a = pr.nc, pr.a
    x = pr.sb("x", [P, 2, D], F32)
    xn = pr.sb("xn", [P, 2, D], F32)
    junk = pr.sb("junk", [P, 2, D], F32)
    whole = pr.sb("whole", [P, 2, DC, P], F32)
    g = pr.sb("g", [P, DC], F32)
    stat = pr.sb("stat", [P, 2, 4], F32)
    x_in = [pr.sem(f"x_in{b}") for b in range(2)]
    const_in = pr.sem("const_in")
    squares = pr.sem("squares")
    means = pr.sem("means")
    roots = pr.sem("roots")
    inverse = pr.sem("inverse")
    normed = pr.sem("normed")
    turned = pr.sem("turned")
    stored = pr.sem("stored")
    high = pr.sem("high")
    low = pr.sem("low")
    noted = pr.noted

    with nc.Block() as block:
        @block.sync
        def _(sp):
            sp.dma_start(pr.ident[:, :], a["c_ident"]).then_inc(const_in, 16)
            sp.dma_start(g[:, :], a["g_mix"][0].rearrange("(c p) -> p c", p=P),
                         allow_slow_non_contiguous=True).then_inc(const_in, 16)

            def pair(n, r):
                for b in range(2):
                    if r is not None:
                        sp.wait_ge(normed, 2 * n - 1 + b)
                    for c, rows in enumerate(rows_of(pr, pr.xp, pr.xs, n, r, b)):
                        sp.dma_start(x[RUN * c:RUN * (c + 1), b, :], rows).then_inc(x_in[b], 16)

            tile_pairs(sp, pair)

        @block.scalar
        def _(act):
            def pair(n, r):
                for b in range(2):
                    act.wait_ge(x_in[b], 32 * n + 32)
                    nc.scalar.activation(junk[:, b, :], x[:, b, :], ACT.Square,
                                         accum_out=stat[:, b, 0:1]).then_inc(squares, 1)
                    act.wait_ge(means, 2 * n + b + 1)
                    nc.scalar.activation(stat[:, b, 2:3], stat[:, b, 1:2], ACT.Sqrt).then_inc(roots, 1)

            tile_pairs(act, pair)

        @block.vector
        def _(dve):
            dve.wait_ge(const_in, 32)

            def store(b, k, first):
                dve.wait_ge(turned, k + 1)
                if not first:
                    dve.wait_ge(low, k)
                nc.vector.tensor_tensor(
                    whole[:, b, :, :], pr.psum[:, 2 * b:2 * b + 2, :].rearrange(
                        "p b (c n) -> p (b c) n", n=P),
                    g[:, :].unsqueeze(2).to_broadcast([P, DC, P]), ALU.mult).then_inc(stored, 1)
                dve.wait_ge(stored, k + 1)
                high_bits(nc.vector.tensor_copy, pr.xhiT[:, :, bass.ds(k * P, P)], whole[:, b, :, :]).then_inc(high, 1)

            def pair(n, r):
                for b in range(2):
                    dve.wait_ge(squares, 2 * n + b + 1)
                    nc.vector.tensor_scalar(stat[:, b, 1:2], stat[:, b, 0:1], 1.0 / D, EPS,
                                            ALU.mult, ALU.add).then_inc(means, 1)
                    dve.wait_ge(roots, 2 * n + b + 1)
                    nc.vector.reciprocal(stat[:, b, 3:4], stat[:, b, 2:3]).then_inc(inverse, 1)
                    dve.wait_ge(inverse, 2 * n + b + 1)
                    nc.vector.tensor_scalar(xn[:, b, :], x[:, b, :], stat[:, b, 3:4], None,
                                            ALU.mult).then_inc(normed, 1)
                    if b == 1:
                        store(0, 2 * n, r is None)
                    elif r is not None:
                        store(1, 2 * n - 1, False)

            tile_pairs(dve, pair)
            store(1, TILES - 1, False)

        @block.gpsimd
        def _(pool):
            pool.sem_inc(low, 1)

            def pair(n, r):
                for b in range(2):
                    k = 2 * n + b
                    wait_apart(pool, high, k + 1, noted)
                    nc.gpsimd.tensor_tensor(pr.xnT[:, :, bass.ds(k * P, P)], whole[:, b, :, :],
                                            pr.xhiT[:, :, bass.ds(k * P, P)], ALU.subtract).then_inc(low, 1)

            tile_pairs(pool, pair)

        @block.tensor
        def _(pe):
            pe.wait_ge(const_in, 32)

            def pair(n, r):
                for b in range(2):
                    pe.wait_ge(normed, 2 * n + b + 1)
                    if r is not None:
                        pe.wait_ge(stored, 2 * n - 1 + b)
                    for c in range(DC):
                        last = nc.tensor.transpose(pr.psum[:, 2 * b + c // 4, c % 4 * P:c % 4 * P + P],
                                                   xn[:, b, c * P:(c + 1) * P], pr.ident[:, :])
                    last.then_inc(turned, 1)

            tile_pairs(pe, pair)


def stage_fourier(pr):
    nc, a = pr.nc, pr.a
    TABLE = [P, DEC_SEQ // P, 2, 512]
    table_1, w, w_hi, w_lo, fT = pr.sb_at_one_place(
        (("table_1", TABLE, F32),),
        (("w", [P, 2, DC, P], F32), ("w_hi", [P, 2, DC, P], F32R), ("w_lo", [P, 2, DC, P], F32R),
         ("fT", [P, FG, T], F32)))
    chan = pr.sb("chan", [P, 2 * P], F32)
    spec = pr.sb("spec", [P, TILES, FG * 2 * P], F32)
    out = pr.sb("out", [P, 2, 512], F32)
    table_s = (pr.sb("table_0", TABLE, F32), table_1)
    table_p = pr.sb("table_p", [P, SEQ // P, 2, SEQ], F32)
    w_loaded = [pr.sem(f"w_loaded{b}") for b in range(2)]
    chan_in = pr.sem("chan_in")
    tp_in = pr.sem("tp_in")
    ts_in = [pr.sem(f"ts_in{b}") for b in range(2)]
    projected = pr.sem("projected")
    f_ready = pr.sem("f_ready")
    chan_done = pr.sem("chan_done")
    spec_ready = pr.sem("spec_ready")
    mixed = pr.sem("mixed")
    four_ready = pr.sem("four_ready")
    four_out = [pr.sem(f"four_out{b}") for b in range(2)]
    high = pr.sem("high")
    halved = pr.sem("halved")
    units = [(g, c0, n) for c0, n in CHUNKS for g in range(FG)]

    with nc.Block() as block:
        @block.sync
        def _(sp):
            for g in range(FG):
                if g >= 2:
                    sp.wait_ge(halved, g - 1)
                sp.dma_start(w[:, g % 2, :, :], pr.w_in[:, :, g * P:(g + 1) * P]).then_inc(w_loaded[g % 2], 16)
                if g == 1:
                    sp.dma_start(chan[:, :], a["c_chan"]).then_inc(chan_in, 16)
            for part in range(2):
                sp.dma_start(table_p[:, :, part, :], a["c_dftp"][part].rearrange(
                    "(t p) k -> p t k", p=P)).then_inc(tp_in, 16)
            for h in range(2):
                if h == 1:
                    sp.wait_ge(chan_done, TILES)
                for part in range(2):
                    sp.dma_start(table_s[h][:, :, part, :], a["c_dfts"][part][:, h * 512:(h + 1) * 512].rearrange(
                        "(t p) k -> p t k", p=P)).then_inc(ts_in[h], 16)

        @block.tensor
        def _(pe):
            for g in range(FG):
                pe.wait_ge(halved, g + 1)
                for c, (c0, n) in enumerate(CHUNKS):
                    if g >= 2:
                        pe.wait_ge(f_ready, 3 * (g - 2) + c + 1)
                    for k in range(DC):
                        for i, (ws, xs) in enumerate(parts(pr.xhiT, pr.xnT, w_hi, w_lo)):
                            last = nc.tensor.matmul(pr.psum[:, g % 2 * 3 + c, 0:n],
                                                    ws[:, g % 2, k, :],
                                                    xs[:, k, c0:c0 + n],
                                                    start=k == 0 and i == 0, stop=k == DC - 1 and i == 2)
                    last.then_inc(projected, 1)
            pe.wait_ge(f_ready, 3 * FG)
            pe.wait_ge(chan_in, 16)
            for t in range(TILES):
                if t >= 4:
                    pe.wait_ge(spec_ready, t - 3)
                for g in range(FG):
                    last = nc.tensor.matmul(pr.psum[:, 2 * (t % 4) + g // 2, g % 2 * 256:g % 2 * 256 + 256],
                                            fT[:, g, t * P:(t + 1) * P], chan[:, :], start=True, stop=True)
                last.then_inc(chan_done, 1)
            pe.wait_ge(spec_ready, TILES)
            pe.wait_ge(tp_in, 32)
            for u, (g, c0, n) in enumerate(units):
                if u == FG:
                    pe.wait_ge(ts_in[0], 32)
                if u == 2 * FG:
                    pe.wait_ge(ts_in[1], 32)
                if u >= 8:
                    pe.wait_ge(four_ready, u - 7)
                tiles = range(2) if c0 == 0 else range(2, TILES)
                for t in tiles:
                    for part in range(2):
                        table = (table_p[:, t, part, :] if c0 == 0 else
                                 table_s[(c0 - SEQ) // 512][:, t - 2, part, :])
                        last = nc.tensor.matmul(pr.psum[:, u % 8, 0:n],
                                                spec[:, t, (2 * g + part) * P:(2 * g + part + 1) * P],
                                                table, start=t == tiles[0] and part == 0,
                                                stop=t == tiles[-1] and part == 1)
                last.then_inc(mixed, 1)

        @block.scalar
        def _(act):
            for g in range(FG):
                for c, (c0, n) in enumerate(CHUNKS):
                    act.wait_ge(projected, 3 * g + c + 1)
                    nc.scalar.copy(fT[:, g, c0:c0 + n], pr.psum[:, g % 2 * 3 + c, 0:n]).then_inc(f_ready, 1)
            for u, (g, c0, n) in enumerate(units):
                act.wait_ge(mixed, u + 1)
                if u >= 2:
                    act.wait_ge(four_out[u % 2], 16 * (u // 2))
                nc.scalar.copy(out[:, u % 2, 0:n], pr.psum[:, u % 8, 0:n]).then_inc(four_ready, 1)
                act.wait_ge(four_ready, u + 1)
                act.dma_start(a["s_branch"][g][:, c0:c0 + n], out[:, u % 2, 0:n]).then_inc(four_out[u % 2], 16)
            for b in range(2):
                act.wait_ge(four_out[b], 16 * len(units) // 2)

        @block.vector
        def _(dve):
            for g in range(FG):
                dve.wait_ge(w_loaded[g % 2], 16 * (g // 2 + 1))
                if g >= 2:
                    dve.wait_ge(projected, 3 * (g - 1))
                high_bits(nc.vector.tensor_copy, w_hi[:, g % 2, :, :], w[:, g % 2, :, :]).then_inc(high, 1)
                dve.wait_ge(high, g + 1)
                nc.vector.tensor_tensor(w_lo[:, g % 2, :, :], w[:, g % 2, :, :], w_hi[:, g % 2, :, :], ALU.subtract
                                        ).then_inc(halved, 1)
            for t in range(TILES):
                dve.wait_ge(chan_done, t + 1)
                nc.vector.tensor_copy(spec[:, t, :], pr.banks(2 * (t % 4), 2)).then_inc(spec_ready, 1)


def stage_attention(pr):
    nc, a = pr.nc, pr.a
    RAW = 3
    KEYS = 1408
    w = pr.sb("w", [P, RAW, DC, P], F32)
    prob, probT, out, headT, w_hi, w_lo, wv_hi, wv_lo = pr.sb_at_one_place(
        (("prob", [P, 2, KEYS], F32), ("probT", [P, 2, KEYS], F32), ("out", [P, 2, P], F32),
         ("headT", [P, T], F32)),
        (("w_hi", [P, 2, DC, P], F32R), ("w_lo", [P, 2, DC, P], F32R),
         ("wv_hi", [P, DC, AG, P], F32R), ("wv_lo", [P, DC, AG, P], F32R)))
    qk = pr.sb("qk", [P, 2 * AG, T], F32)
    v = pr.sb("v", [P, TILES, AG, P], F32)
    mask = pr.sb("mask", [P, 2, 1408], BF16)
    identb = pr.sb("identb", [P, P], BF16)
    mean = pr.sb("mean", [P, P], F32)
    ropec = pr.sb("ropec", [ROPE, T], F32)
    ropes = pr.sb("ropes", [ROPE, T], F32)
    gain = pr.sb("gain", [P, 2 * AG], F32)
    eps = pr.sb("eps", [P, 1], F32)
    sq = pr.sb("sq", [P, 2, 512], F32)
    root = pr.sb("root", [P, 2, 512], F32)
    rot = pr.sb("rot", [ROPE, 2, 512], F32)
    stat = pr.sb("stat", [P, 4, 4], F32)

    const_in = pr.sem("const_in")
    w_loaded = [pr.sem(f"w_loaded{b}") for b in range(RAW)]
    mask_in = [pr.sem(f"mask_in{b}") for b in range(2)]
    set_up = pr.sem("set_up")
    raw = pr.sem("raw")
    squared = pr.sem("squared")
    averaged = pr.sem("averaged")
    rooted = pr.sem("rooted")
    inverted = pr.sem("inverted")
    normed = pr.sem("normed")
    swapped = [pr.sem(f"swapped{b}") for b in range(2)]
    roped = pr.sem("roped")
    v_ready = pr.sem("v_ready")
    scored = pr.sem("scored")
    maxed = pr.sem("maxed")
    shifted = pr.sem("shifted")
    expd = pr.sem("expd")
    turned = pr.sem("turned")
    kept_a = pr.sem("kept_a")
    kept_v = pr.sem("kept_v")
    weighed = pr.sem("weighed")
    summed = pr.sem("summed")
    out_ready = pr.sem("out_ready")
    out_turned = pr.sem("out_turned")
    out_kept = pr.sem("out_kept")
    head_out = pr.sem("head_out")
    high = pr.sem("high")
    halved = pr.sem("halved")

    NB = 2 * AG
    NU = 3 * NB
    NR = NU + TILES
    UNITS = [(j, c0, n) for j in range(NB) for c0, n in CHUNKS]

    def blocks(t):
        return [(g, (k0 // P) + i) for g, (k0, n) in enumerate(key_runs(t)) for i in range(n // P)]

    QUAD = 4
    quads = [(t, i) for t in range(TILES) for i in range(-(-len(blocks(t)) // QUAD))]
    first_quad = [quads.index((t, 0)) for t in range(TILES)] + [len(quads)]
    NQ = len(quads)
    even = [(i + 1) // 2 for i in range(NQ + 1)]

    def quad_bank(q):
        return pr.banks(3 + q % 3)

    def score_banks(t):
        return pr.banks(0, 3)[:, 0:P * len(blocks(t))]

    NW = NB + AG
    ORDER = (0, 1, 2, 6, 3, 7, 4, 8, 5)
    BEFORE = (1, 4, 5, 7, 8, 10, 11, 13)
    w_col = ([(Q_COL, K_COL)[j % 2] + j // 2 * HEADS * P for j in range(NB)]
             + [V_COL + g * HEADS * P for g in range(AG)])

    def weight_parts(i):
        j = ORDER[i]
        if j < NB:
            return w_hi[:, j % 2, :, :], w_lo[:, j % 2, :, :]
        return wv_hi[:, :, j - NB, :], wv_lo[:, :, j - NB, :]

    with nc.Block() as block:
        @block.sync
        def _(sp):
            for dst, src in ((identb[:, :], a["c_identb"]), (ropec[:, :], a["c_ropec"]),
                             (ropes[:, :], a["c_ropes"])):
                sp.dma_start(dst, src).then_inc(const_in, 16)
            for i, name in enumerate(("q_gain", "k_gain")):
                sp.dma_start(gain[:, :].rearrange("p (g i) -> p i g", i=2)[:, i, :],
                             a[name][0].rearrange("g p -> p g"), allow_slow_non_contiguous=True
                             ).then_inc(const_in, 16)

            def load_w(at, i):
                sp.dma_start(w[:, i % RAW, :, :], pr.w_in[:, :, bass.ds(at + w_col[ORDER[i]], P)]
                             ).then_inc(w_loaded[i % RAW], 16)

            for i in range(RAW):
                load_w(0, i)

            def swap_unit(h, u):
                j, c0, n = UNITS[u]
                if u >= 2:
                    wait_apart(sp, roped, 3 * (NU * h + u - 1), pr.noted)
                sp.wait_ge(normed, NU * h + u + 1)
                for to, row in ((0, ROPE // 2), (ROPE // 2, 0)):
                    sp.dma_start(rot[to:to + ROPE // 2, u % 2, 0:n], qk[row:row + ROPE // 2, j, c0:c0 + n]
                                 ).then_inc(swapped[u % 2], 16)

            def head(h, ahead):
                at = h * P if not ahead else sp.snap(h * P)
                def load(i):
                    if i < NW or ahead:
                        sp.wait_ge(halved, NW * h + i - RAW + 1)
                        load_w(at if i < NW else at + P, i % NW)

                load(RAW)
                for u in range(NU):
                    swap_unit(h, u)
                    if u in BEFORE:
                        load(BEFORE.index(u) + 1 + RAW)
                for t in range(TILES):
                    if t == 0:
                        sp.wait_ge(raw, NR * h + NR)
                    if t >= 2:
                        sp.wait_ge(scored, TILES * h + t - 1)
                    sp.dma_start(mask[:, t % 2, 0:P * len(blocks(t))], a["c_mask"][t][:, 0:P * len(blocks(t))]
                                 ).then_inc(mask_in[t % 2], 16)

            with sp.Fori(0, HEADS - 1) as h:
                head(h, True)
            head(HEADS - 1, False)

        @block.tensor
        def _(pe):
            pe.wait_ge(const_in, 80)
            pe.wait_ge(set_up, 2)

            def raw_unit(h, u):
                j, c0, n = UNITS[u]
                if u % 3 == 0:
                    pe.wait_ge(halved, NW * h + ORDER.index(j) + 1)
                if u >= 3:
                    pe.wait_ge(normed, NU * h + u - 2)
                for k in range(DC):
                    for i, (ws, xs) in enumerate(parts(pr.xhiT, pr.xnT, w_hi, w_lo)):
                        last = nc.tensor.matmul(pr.psum[:, u % 3, 0:n], ws[:, j % 2, k, :],
                                                xs[:, k, c0:c0 + n],
                                                start=k == 0 and i == 0, stop=k == DC - 1 and i == 2)
                last.then_inc(raw, 1)

            def mean_unit(h, u):
                n = UNITS[u][2]
                pe.wait_ge(squared, NU * h + u + 1)
                if u >= 2:
                    pe.wait_ge(rooted, NU * h + u - 1)
                nc.tensor.matmul(pr.psum[:, 3 + u % 2, 0:n], mean[:, :], sq[:, u % 2, 0:n],
                                 start=True, stop=True).then_inc(averaged, 1)

            def v_tile(h, t):
                u = NU + t
                if t == 0:
                    pe.wait_ge(halved, NW * (h + 1))
                if t < 3:
                    pe.wait_ge(normed, NU * h + u - 2)
                else:
                    pe.wait_ge(v_ready, TILES * h + t - 2)
                for k in range(DC):
                    for i, (ws, xs) in enumerate(parts(pr.xhiT, pr.xnT, wv_hi, wv_lo)):
                        last = nc.tensor.matmul(pr.psum[:, u % 3, 0:AG * P],
                                                xs[:, k, t * P:(t + 1) * P],
                                                ws[:, k, :, :],
                                                start=k == 0 and i == 0, stop=k == DC - 1 and i == 2)
                last.then_inc(raw, 1)

            def scores(h, t):
                at = 0
                pe.wait_ge(mask_in[t % 2], 16 * (TILES // 2 * h + t // 2 + 1))
                if t >= 1:
                    pe.wait_ge(expd, TILES * h + t)
                for g, (k0, n) in enumerate(key_runs(t)):
                    for c in range(0, n, 512):
                        m = min(512, n - c)
                        s = pr.banks(0, 3)[:, at:at + m]
                        nc.tensor.matmul(s, identb[:, :], mask[:, t % 2, at:at + m], start=True, stop=False)
                        last = nc.tensor.matmul(s, qk[:, 2 * g, t * P:(t + 1) * P],
                                                qk[:, 2 * g + 1, k0 + c:k0 + c + m], start=False, stop=True)
                        at += m
                last.then_inc(scored, 1)

            def turn(h, t):
                n = len(blocks(t))
                pe.wait_ge(expd, TILES * h + t + 1)
                for q in range(first_quad[t], first_quad[t + 1]):
                    if q >= 3:
                        if (q - 3) % 2 == 0:
                            pe.wait_ge(kept_a, even[NQ] * h + even[q - 2])
                        else:
                            pe.wait_ge(kept_v, (NQ - even[NQ]) * h + q - 2 - even[q - 2])
                    x0 = QUAD * (q - first_quad[t])
                    for x in range(x0, min(x0 + QUAD, n)):
                        last = nc.tensor.transpose(quad_bank(q)[:, (x - x0) * P:(x - x0 + 1) * P],
                                                   prob[:, t % 2, x * P:(x + 1) * P], pr.ident[:, :])
                    last.then_inc(turned, 1)

            def weigh(h, t):
                end = first_quad[t + 1]
                pe.wait_ge(kept_a, even[NQ] * h + even[end])
                pe.wait_ge(kept_v, (NQ - even[NQ]) * h + end - even[end])
                bl = blocks(t)
                for x, (g, kt) in enumerate(bl):
                    last = nc.tensor.matmul(pr.psum[:, 6, 0:P], probT[:, t % 2, x * P:(x + 1) * P], v[:, kt, g, :],
                                            start=x == 0, stop=x == len(bl) - 1)
                last.then_inc(weighed, 1)

            def turn_out(h, t):
                pe.wait_ge(out_ready, TILES * h + t + 1)
                if t >= 1:
                    pe.wait_ge(out_kept, TILES * h + t)
                nc.tensor.transpose(pr.psum[:, 7, 0:P], out[:, t % 2, :], pr.ident[:, :]
                                    ).then_inc(out_turned, 1)

            with pe.Fori(0, HEADS) as h:
                for u in range(NU + 2):
                    if u < NU:
                        raw_unit(h, u)
                    if 1 <= u <= NU:
                        mean_unit(h, u - 1)
                    if u == NU:
                        v_tile(h, 0)
                    if u == NU + 1:
                        v_tile(h, 1)
                        v_tile(h, 2)
                for t in range(3, TILES):
                    v_tile(h, t)
                pe.wait_ge(roped, 3 * NU * h + 3 * NU)
                pe.wait_ge(v_ready, TILES * h + TILES)
                scores(h, 0)
                for t in range(TILES):
                    if t + 1 < TILES:
                        scores(h, t + 1)
                    if t >= 2:
                        turn_out(h, t - 2)
                    if t >= 1:
                        weigh(h, t - 1)
                    turn(h, t)
                turn_out(h, TILES - 2)
                weigh(h, TILES - 1)
                turn_out(h, TILES - 1)
                pe.wait_ge(out_kept, TILES * h + TILES)

        @block.scalar
        def _(act):
            act.wait_ge(set_up, 2)

            def split_high(h, i):
                j = ORDER[i]
                act.wait_ge(w_loaded[i % RAW], 16 * (NW // RAW * h + i // RAW + 1))
                if 2 <= j < NB:
                    act.wait_ge(raw, NR * h + 3 * (j - 1))
                high_bits(nc.scalar.copy, weight_parts(i)[0], w[:, i % RAW, :, :]).then_inc(high, 1)

            def square(h, u):
                n = UNITS[u][2]
                act.wait_ge(raw, NR * h + u + 1)
                if u >= 2:
                    act.wait_ge(averaged, NU * h + u - 1)
                nc.scalar.activation(sq[:, u % 2, 0:n], pr.psum[:, u % 3, 0:n], ACT.Square
                                     ).then_inc(squared, 1)

            def root_of(h, u):
                n = UNITS[u][2]
                act.wait_ge(averaged, NU * h + u + 1)
                if u >= 2:
                    act.wait_ge(normed, NU * h + u - 1)
                nc.scalar.activation(root[:, u % 2, 0:n], pr.psum[:, 3 + u % 2, 0:n], ACT.Sqrt,
                                     bias=eps[:, 0:1]).then_inc(rooted, 1)

            def keep_quads(h, t):
                for q in range(first_quad[t], first_quad[t + 1]):
                    if q % 2 == 0:
                        x = QUAD * (q - first_quad[t])
                        m = P * min(QUAD, len(blocks(t)) - x)
                        act.wait_ge(turned, NQ * h + q + 1)
                        if t >= 2 and q < first_quad[t] + 2:
                            act.wait_ge(weighed, TILES * h + t - 1)
                        nc.scalar.copy(probT[:, t % 2, x * P:x * P + m], quad_bank(q)[:, 0:m]).then_inc(kept_a, 1)

            def keep_out(h, t):
                act.wait_ge(out_turned, TILES * h + t + 1)
                nc.scalar.copy(headT[:, t * P:(t + 1) * P], pr.psum[:, 7, 0:P]).then_inc(out_kept, 1)

            with act.Fori(0, HEADS) as h:
                for u in range(NU + 1):
                    if u in BEFORE:
                        split_high(h, BEFORE.index(u) + 1)
                    if u < NU:
                        square(h, u)
                    if u >= 1:
                        root_of(h, u - 1)
                for t in range(TILES):
                    act.wait_ge(raw, NR * h + NU + t + 1)
                    nc.scalar.copy(v[:, t, :, :].rearrange("p g e -> p (g e)"),
                                   pr.psum[:, (NU + t) % 3, 0:AG * P]).then_inc(v_ready, 1)
                for t in range(TILES + 1):
                    if t < TILES:
                        act.wait_ge(shifted, TILES * h + t + 1)
                        if t >= 2:
                            act.wait_ge(turned, NQ * h + first_quad[t - 1])
                        nc.scalar.activation(prob[:, t % 2, 0:P * len(blocks(t))], score_banks(t), ACT.Exp,
                                             bias=stat[:, t % 4, 1:2], scale=SCALE,
                                             accum_out=stat[:, t % 4, 2:3]).then_inc(expd, 1)
                    if t >= 1:
                        keep_quads(h, t - 1)
                    if t >= 2:
                        keep_out(h, t - 2)
                keep_out(h, TILES - 1)
                act.wait_ge(out_kept, TILES * h + TILES)
                act.dma_start(a["s_branch"][bass.ds(h + FG, 1)].rearrange("o p n -> (o p) n"), headT[:, :]
                              ).then_inc(head_out, 16)
                act.wait_ge(head_out, 16 * h + 16)

        @block.vector
        def _(dve):
            nc.vector.memset(mean[:, :], 1.0 / P).then_inc(set_up, 1)
            nc.vector.memset(eps[:, :], EPS).then_inc(set_up, 1)
            dve.wait_ge(const_in, 80)

            def norm_unit(h, u):
                j, c0, n = UNITS[u]
                dve.wait_ge(rooted, NU * h + u + 1)
                nc.vector.reciprocal(root[:, u % 2, 0:n], root[:, u % 2, 0:n]).then_inc(inverted, 1)
                dve.wait_ge(inverted, NU * h + u + 1)
                nc.vector.scalar_tensor_tensor(qk[:, j, c0:c0 + n], pr.psum[:, u % 3, 0:n], gain[:, j:j + 1],
                                               root[:, u % 2, 0:n], ALU.mult, ALU.mult).then_inc(normed, 1)

            def rope_unit(h, u):
                j, c0, n = UNITS[u]
                at = 3 * (NU * h + u)
                dve.wait_ge(swapped[u % 2], 32 * (NU // 2 * h + u // 2 + 1))
                nc.vector.tensor_tensor(rot[:, u % 2, 0:n], rot[:, u % 2, 0:n],
                                        ropes[:, c0:c0 + n], ALU.mult).then_inc(roped, 1)
                nc.vector.tensor_tensor(qk[0:ROPE, j, c0:c0 + n], qk[0:ROPE, j, c0:c0 + n],
                                        ropec[:, c0:c0 + n], ALU.mult).then_inc(roped, 1)
                dve.wait_ge(roped, at + 2)
                nc.vector.tensor_tensor(qk[0:ROPE, j, c0:c0 + n], qk[0:ROPE, j, c0:c0 + n],
                                        rot[:, u % 2, 0:n], ALU.add).then_inc(roped, 1)

            def halve(h, i):
                top, low = weight_parts(i)
                if i == 0:
                    dve.wait_ge(w_loaded[0], 16 * (NW // RAW * h + 1))
                    high_bits(nc.vector.tensor_copy, top, w[:, 0, :, :]).then_inc(high, 1)
                dve.wait_ge(high, NW * h + i + 1)
                nc.vector.tensor_tensor(low, w[:, i % RAW, :, :], top, ALU.subtract).then_inc(halved, 1)

            with dve.Fori(0, HEADS) as h:
                halve(h, 0)
                for u in range(NU + 2):
                    if u in BEFORE:
                        halve(h, BEFORE.index(u) + 1)
                    if u < NU:
                        norm_unit(h, u)
                    if u >= 2:
                        rope_unit(h, u - 2)
                for t in range(TILES + 2):
                    if t < TILES:
                        dve.wait_ge(scored, TILES * h + t + 1)
                        nc.vector.reduce_max(stat[:, t % 4, 0:1], score_banks(t), AX).then_inc(maxed, 1)
                        dve.wait_ge(maxed, TILES * h + t + 1)
                        nc.vector.tensor_scalar(stat[:, t % 4, 1:2], stat[:, t % 4, 0:1], -SCALE, None,
                                                ALU.mult).then_inc(shifted, 1)
                    if 1 <= t <= TILES:
                        s = t - 1
                        dve.wait_ge(expd, TILES * h + s + 1)
                        nc.vector.reciprocal(stat[:, s % 4, 3:4], stat[:, s % 4, 2:3]).then_inc(summed, 1)
                        for q in range(first_quad[s], first_quad[s + 1]):
                            if q % 2 == 1:
                                x = QUAD * (q - first_quad[s])
                                m = P * min(QUAD, len(blocks(s)) - x)
                                dve.wait_ge(turned, NQ * h + q + 1)
                                if s >= 2 and q < first_quad[s] + 2:
                                    dve.wait_ge(weighed, TILES * h + s - 1)
                                nc.vector.tensor_copy(probT[:, s % 2, x * P:x * P + m], quad_bank(q)[:, 0:m]
                                                      ).then_inc(kept_v, 1)
                    if t >= 2:
                        s = t - 2
                        dve.wait_ge(summed, TILES * h + s + 1)
                        dve.wait_ge(weighed, TILES * h + s + 1)
                        if s >= 2:
                            dve.wait_ge(out_turned, TILES * h + s - 1)
                        nc.vector.tensor_scalar(out[:, s % 2, :], pr.psum[:, 6, 0:P], stat[:, s % 4, 3:4],
                                                None, ALU.mult).then_inc(out_ready, 1)


def first_then_loop(eng, count, body):
    body(0, True)
    with eng.Fori(1, count) as i:
        body(i, False)


def stage_mix(pr):
    nc, a = pr.nc, pr.a
    WC = 2 * DC + FG + HEADS
    branchT = pr.sb("branchT", [P, FG + HEADS, T], F32)
    w = pr.sb("w", [P, 2, WC, P], F32)
    w_hi = pr.sb("w_hi", [P, 2 * DC, P], F32R)
    w_lo = pr.sb("w_lo", [P, 2 * DC, P], F32R)
    sig = pr.sb("sig", [P, 2, 512], F32)
    w_loaded = [pr.sem(f"w_loaded{b}") for b in range(2)]
    produced = pr.sem("produced")
    gated = pr.sem("gated")
    steps = pr.sem("steps")
    branch_in = [pr.sem(f"branch_in{c}") for c in range(len(CHUNKS))]
    judged = pr.sem("judged")
    high = pr.sem("high")
    halved = pr.sem("halved")
    NC = len(CHUNKS)
    w_f = a["w_fourier"][0].rearrange("(c p) n -> p c n", p=P)
    w_a = a["w_attn"][0].rearrange("(c p) n -> p c n", p=P)

    with nc.Block() as block:
        @block.sync
        def _(sp):
            def pair(i, first):
                for b in range(2):
                    if not first:
                        sp.wait_ge(produced, NC * (2 * i + b - 1))
                    at = 0
                    for view, col in ((pr.w_in, GA_COL), (pr.w_in, GB_COL), (w_f, 0), (w_a, 0)):
                        n = view.shape[1]
                        sp.dma_start(w[:, b, at:at + n, :], view[:, :, bass.ds(2 * P * i + (b * P + col), P)]
                                     ).then_inc(w_loaded[b], 16)
                        at += n
                    if first and b == 0:
                        for c, (c0, n) in enumerate(CHUNKS):
                            sp.dma_start(branchT[:, :, c0:c0 + n], a["s_branch"][:, :, c0:c0 + n].rearrange(
                                "c p n -> p c n")).then_inc(branch_in[c], 16)

            first_then_loop(sp, DC // 2, pair)

        @block.tensor
        def _(pe):
            def pair(i, first):
                for v in range(2 * NC):
                    b, (c0, n) = v // NC, CHUNKS[v % NC]
                    if not first or v >= 2:
                        pe.wait_ge(steps, 6 * NC * i + 3 * (v - 1))
                    for s in range(2):
                        if v % NC == 0:
                            pe.wait_ge(halved, 4 * i + 2 * b + s + 1)
                        for k in range(DC):
                            for part, (ws, xs) in enumerate(parts(pr.xhiT, pr.xnT, w_hi, w_lo)):
                                last = nc.tensor.matmul(pr.psum[:, 4 * (v % 2) + s, 0:n],
                                                        ws[:, s * DC + k, :], xs[:, k, c0:c0 + n],
                                                        start=k == 0 and part == 0,
                                                        stop=k == DC - 1 and part == 2)
                    if v % NC == NC - 1:
                        last.then_inc(judged, 1)
                    if first and b == 0:
                        pe.wait_ge(branch_in[v % NC], 16)
                    for s, (k0, kc) in enumerate(((0, FG), (FG, HEADS))):
                        for k in range(k0, k0 + kc):
                            last = nc.tensor.matmul(pr.psum[:, 4 * (v % 2) + 2 + s, 0:n], w[:, b, 2 * DC + k, :],
                                                    branchT[:, k, c0:c0 + n], start=k == k0, stop=k == k0 + kc - 1)
                    last.then_inc(produced, 1)

            first_then_loop(pe, DC // 2, pair)

        @block.scalar
        def _(act):
            def pair(i, first):
                for v in range(2 * NC):
                    n = CHUNKS[v % NC][1]
                    act.wait_ge(produced, 2 * NC * i + v + 1)
                    if not first or v:
                        act.wait_ge(steps, 6 * NC * i + 3 * v)
                    for s in range(2):
                        nc.scalar.activation(sig[:, s, 0:n], pr.psum[:, 4 * (v % 2) + s, 0:n],
                                             ACT.Sigmoid).then_inc(gated, 1)

            first_then_loop(act, DC // 2, pair)

        @block.vector
        def _(dve):
            def halve(b, i):
                dve.wait_ge(w_loaded[b], 64 * i + 64)
                for s in range(2):
                    x, top = w[:, b, s * DC:(s + 1) * DC, :], w_hi[:, s * DC:(s + 1) * DC, :]
                    high_bits(nc.vector.tensor_copy, top, x).then_inc(high, 1)
                    dve.wait_ge(high, 4 * i + 2 * b + s + 1)
                    nc.vector.tensor_tensor(w_lo[:, s * DC:(s + 1) * DC, :], x, top, ALU.subtract
                                            ).then_inc(halved, 1)

            def pair(i, last):
                for v in range(2 * NC):
                    b, (c0, n) = v // NC, CHUNKS[v % NC]
                    at = 6 * NC * i + 3 * v
                    if v % NC == NC - 1 and not (last and b):
                        dve.wait_ge(judged, 2 * i + b + 1)
                        halve(1 - b, i + b)
                    dve.wait_ge(gated, 4 * NC * i + 2 * v + 2)
                    for s in range(2):
                        nc.vector.tensor_tensor(sig[:, s, 0:n], pr.psum[:, 4 * (v % 2) + 2 + s, 0:n],
                                                sig[:, s, 0:n], ALU.mult).then_inc(steps, 1)
                    dve.wait_ge(steps, at + 2)
                    nc.vector.tensor_tensor(
                        pr.mixT[:, bass.ds(2 * i + b, 1), c0:c0 + n].rearrange("p o n -> p (o n)"),
                        sig[:, 0, 0:n], sig[:, 1, 0:n], ALU.add).then_inc(steps, 1)

            halve(0, 0)
            with dve.Fori(0, DC // 2 - 1) as i:
                pair(i, False)
            pair(DC // 2 - 1, True)


def stage_out(pr):
    nc, a = pr.nc, pr.a
    w = pr.sb("w4", [P, DC, D], F32)
    mixb = pr.sb("mixb", [P, 2, DC, P], F32)
    x = pr.sb("x2", [P, 2, D], F32)
    h = pr.sb("h", [P, 2, D], F32)
    xn = pr.sb("xn2", [P, 2, D], F32)
    rest = pr.sb("rest", [P, 2, D], F32)
    parts = pr.sb("parts", [P, 3, D], BF16)
    g = pr.sb("g2", [P, D], F32)
    stat = pr.sb("stat2", [P, 2, 4], F32)
    x_in = [pr.sem(f"x_in{b}") for b in range(2)]
    g_in = pr.sem("g_in")
    w_in = [pr.sem(f"w_in{c}") for c in range(DC)]
    picked = pr.sem("picked")
    product = pr.sem("product")
    h_ready = pr.sem("h_ready")
    squares = pr.sem("squares")
    means = pr.sem("means")
    roots = pr.sem("roots")
    inverse = pr.sem("inverse")
    normed = pr.sem("normed")
    split = pr.sem("split")
    first_parts = pr.sem("first_parts")
    turned = pr.sem("turned")
    high = pr.sem("high")
    kept = pr.sem("kept")
    h_out = [pr.sem(f"h_out{b}") for b in range(2)]
    parts_out = pr.sem("parts_out")
    noted = pr.noted

    with nc.Block() as block:
        @block.sync
        def _(sp):
            for c in range(DC):
                sp.dma_start(w[:, c, :], a["w_out"][0][c * P:(c + 1) * P, :]).then_inc(w_in[c], 16)
            sp.dma_start(g[:, :], a["g_ffn"].to_broadcast([P, D])).then_inc(g_in, 16)

            def pair(n, r):
                for b in range(2):
                    k = 2 * n + b
                    if r is not None:
                        sp.wait_ge(h_ready, k - 1)
                    for c, rows in enumerate(rows_of(pr, pr.xp, pr.xs, n, r, b)):
                        sp.dma_start(x[RUN * c:RUN * (c + 1), b, :], rows).then_inc(x_in[b], 16)
                for b in range(2):
                    k = 2 * n + b
                    sp.wait_ge(h_ready, k + 1)
                    sp.dma_start(a["s_h"][bass.ds(k * P, P), :], h[:, b, :]).then_inc(h_out[b], 16)
                    wait_apart(sp, split, 2 * k + 2, noted)
                    for i in range(3):
                        sp.dma_start(a["s_xn"][i][bass.ds(k * P, P), :], parts[:, i, :]).then_inc(parts_out, 16)

            tile_pairs(sp, pair)
            sp.wait_ge(parts_out, 48 * TILES)
            for b in range(2):
                sp.wait_ge(h_out[b], 16 * TILES // 2)

        @block.scalar
        def _(act):
            def pick(b, k):
                nc.scalar.copy(mixb[:, b, :, :], pr.mixT[:, :, bass.ds(k * P, P)]).then_inc(picked, 1)

            def pair(n, r, last):
                for b in range(2):
                    k = 2 * n + b
                    act.wait_ge(h_ready, k + 1)
                    nc.scalar.activation(rest[:, b, :], h[:, b, :], ACT.Square,
                                         accum_out=stat[:, b, 0:1]).then_inc(squares, 1)
                    act.wait_ge(means, k + 1)
                    nc.scalar.activation(stat[:, b, 2:3], stat[:, b, 1:2], ACT.Sqrt).then_inc(roots, 1)
                    if not last:
                        act.wait_ge(product, k + 1)
                        pick(b, k + 2)
                    act.wait_ge(normed, k + 1)
                    if b == 1 or r is not None:
                        act.wait_ge(parts_out, 48 * k)
                    nc.scalar.copy(parts[:, 0, :], xn[:, b, :]).then_inc(first_parts, 1)
                    act.wait_ge(split, 2 * k + 1)
                    nc.scalar.copy(parts[:, 1, :], rest[:, b, :]).then_inc(first_parts, 1)

            for b in range(2):
                pick(b, b)
            pair(0, None, False)
            with act.Fori(0, PHASE - 1) as r:
                pair(r + 1, r, False)
            pair(PHASE, PHASE - 1, True)

        @block.vector
        def _(dve):
            dve.wait_ge(g_in, 16)

            def keep(b, k):
                rows = pr.psum[:, 4 + 2 * b:6 + 2 * b, :].rearrange("p b (c n) -> p (b c) n", n=P)
                top = pr.xhiT[:, :, bass.ds(k * P, P)]
                dve.wait_ge(turned, k + 1)
                high_bits(nc.vector.tensor_copy, top, rows).then_inc(high, 1)
                dve.wait_ge(high, k + 1)
                nc.vector.tensor_tensor(pr.xnT[:, :, bass.ds(k * P, P)], rows, top, ALU.subtract
                                        ).then_inc(kept, 1)

            def pair(n, r):
                for b in range(2):
                    k = 2 * n + b
                    dve.wait_ge(product, k + 1)
                    dve.wait_ge(x_in[b], 32 * n + 32)
                    if r is not None:
                        dve.wait_ge(h_out[b], 16 * n)
                    nc.vector.tensor_tensor(h[:, b, :], pr.banks(2 * b, 2), x[:, b, :], ALU.add
                                            ).then_inc(h_ready, 1)
                    if b == 1:
                        keep(0, k - 1)
                    elif r is not None:
                        keep(1, k - 1)
                    dve.wait_ge(squares, k + 1)
                    nc.vector.tensor_scalar(stat[:, b, 1:2], stat[:, b, 0:1], 1.0 / D, EPS,
                                            ALU.mult, ALU.add).then_inc(means, 1)
                    dve.wait_ge(roots, k + 1)
                    nc.vector.reciprocal(stat[:, b, 3:4], stat[:, b, 2:3]).then_inc(inverse, 1)
                    dve.wait_ge(inverse, k + 1)
                    if r is not None:
                        dve.wait_ge(turned, k - 1)
                    nc.vector.scalar_tensor_tensor(xn[:, b, :], h[:, b, :], stat[:, b, 3:4], g[:, :],
                                                   ALU.mult, ALU.mult).then_inc(normed, 1)
                    dve.wait_ge(first_parts, 2 * k + 1)
                    nc.vector.tensor_tensor(rest[:, b, :], xn[:, b, :], parts[:, 0, :], ALU.subtract
                                            ).then_inc(split, 1)
                    dve.wait_ge(first_parts, 2 * k + 2)
                    nc.vector.tensor_tensor(parts[:, 2, :], rest[:, b, :], parts[:, 1, :], ALU.subtract
                                            ).then_inc(split, 1)

            tile_pairs(dve, pair)
            keep(1, TILES - 1)

        @block.tensor
        def _(pe):
            def turn(b, k, first):
                pe.wait_ge(normed, k + 1)
                if not first:
                    pe.wait_ge(kept, k)
                for c in range(DC):
                    last = nc.tensor.transpose(pr.psum[:, 4 + 2 * b + c // 4, c % 4 * P:c % 4 * P + P],
                                               xn[:, b, c * P:(c + 1) * P], pr.ident[:, :])
                last.then_inc(turned, 1)

            def pair(n, r):
                for b in range(2):
                    k = 2 * n + b
                    pe.wait_ge(picked, k + 1)
                    if r is not None:
                        pe.wait_ge(h_ready, k - 1)
                    for half in range(2):
                        for c in range(DC):
                            if r is None and b == 0 and half == 0:
                                pe.wait_ge(w_in[c], 16)
                            last = nc.tensor.matmul(pr.psum[:, 2 * b + half, :], mixb[:, b, c, :],
                                                    w[:, c, half * 512:half * 512 + 512],
                                                    start=c == 0, stop=c == DC - 1)
                    last.then_inc(product, 1)
                    if b == 1:
                        turn(0, k - 1, r is None)
                    elif r is not None:
                        turn(1, k - 1, False)

            tile_pairs(pe, pair)
            turn(1, TILES - 1, False)


def stage_keys(pr):
    nc, a = pr.nc, pr.a
    run = pr.sb("run", [P, 3, 4, P], F32)
    w = pr.sb("w3", [P, 2, DC, P], F32)
    w_hi = pr.sb("w_hi", [P, 2, DC, P], F32R)
    w_lo = pr.sb("w_lo", [P, 2, DC, P], F32R)
    sk = pr.sb("sk", [P, 2, P], F32)
    skT = pr.sb("skT", [P, 2, P], F32)
    qT = pr.sb("qT", [P, 2, T], F32)
    w_loaded = [pr.sem(f"w_loaded{b}") for b in range(2)]
    high = pr.sem("high")
    halved = pr.sem("halved")
    turned = pr.sem("turned")
    keys_kept = pr.sem("keys_kept")
    projected = pr.sem("projected")
    q_kept = pr.sem("q_kept")
    scored = pr.sem("scored")
    kept = pr.sem("kept")
    run_out = [pr.sem(f"run_out{s}") for s in range(3)]
    wq = a["w_query"][0].rearrange("(c p) n -> p c n", p=P)
    RUNS = ((0, 4), (4, 4), (8, 2))
    LOADED = (48, 32)
    best = pr.sb("best", [P, 2, TOPK], F32)
    besti = pr.sb("besti", [P, 2, TOPK], U32)
    bestf = pr.sb("bestf", [P, 2, TOPK], F32)
    left = pr.sb("left", [P, TOPK * TOPK], F32)
    cand = pr.sb("cand", [P, TOPK, TOPK], F32)
    pick = pr.sb("pick", [P, 2, TOPK, TOPK], F32)
    top = pr.sb("top", [P, TOPK], F32)
    topi = pr.sb("topi", [P, TOPK], U32)
    part = pr.sb("part", [P, 2, TOPK], U32)
    partf = pr.sb("partf", [P, 2, TOPK], F32)
    iota = pr.sb("iota", [P, TOPK], F32)
    found = pr.sem("found")
    noted = pr.noted
    HALF_STEPS, SUM_STEPS = 4, 9
    HEAD_STEPS = 2 * HALF_STEPS + SUM_STEPS

    with nc.Block() as block:
        @block.sync
        def _(sp):
            sp.dma_start(iota[:, :], a["c_iota"]).then_inc(w_loaded[0], 16)

            def head(i, first):
                for b in range(2):
                    if not first:
                        sp.wait_ge(projected, 3 * (2 * i + b - 1))
                    sp.dma_start(w[:, b, :, :], wq[:, :, bass.ds(2 * P * i + b * P, P)]).then_inc(w_loaded[b], 16)
                    sp.dma_start(sk[:, b, :], a["sub_keys"][0][bass.ds(i, 1), b, :, :].rearrange(
                        "o n d -> (o n) d")).then_inc(w_loaded[b], 16)

            first_then_loop(sp, PH, head)

        @block.tensor
        def _(pe):
            def head(i, first):
                for b in range(2):
                    m = 2 * i + b
                    pe.wait_ge(w_loaded[b], 32 * i + LOADED[b])
                    if not first or b:
                        pe.wait_ge(kept, 3 * m - 1)
                    nc.tensor.transpose(pr.psum[:, 7, 0:P], sk[:, b, :], pr.ident[:, :]).then_inc(turned, 1)
                    pe.wait_ge(halved, m + 1)
                    for c, (c0, n) in enumerate(CHUNKS):
                        if not first:
                            pe.wait_ge(q_kept, 3 * (m - 2) + c + 1)
                        for k in range(DC):
                            for s, (ws, xs) in enumerate(parts(pr.xhiT, pr.xnT, w_hi, w_lo)):
                                last = nc.tensor.matmul(pr.psum[:, 3 * b + c, 0:n], ws[:, b, k, :],
                                                        xs[:, k, c0:c0 + n],
                                                        start=k == 0 and s == 0, stop=k == DC - 1 and s == 2)
                        last.then_inc(projected, 1)
                    pe.wait_ge(keys_kept, m + 1)
                    pe.wait_ge(q_kept, 3 * m + 3)
                    for s, (t0, n) in enumerate(RUNS):
                        if not first or b or s == 2:
                            pe.wait_ge(kept, 3 * m + (0, 0, 1)[s] if s != 1 else 3 * m - 1)
                        for t in range(n):
                            last = nc.tensor.matmul(pr.psum[:, 6 + s % 2, t * P:(t + 1) * P],
                                                    qT[:, b, (t0 + t) * P:(t0 + t + 1) * P], skT[:, b, :],
                                                    start=True, stop=True)
                        last.then_inc(scored, 1)

            first_then_loop(pe, PH, head)

        @block.scalar
        def _(act):
            def store_runs(m):
                for s, (t0, n) in enumerate(RUNS):
                    act.wait_ge(kept, 3 * m + s + 1)
                    act.dma_start(a["s_score"][t0:t0 + n, :, bass.ds(m, 1), :].rearrange("t p o k -> p t (o k)"),
                                  run[:, s, 0:n, :]).then_inc(run_out[s], 16)

            def head(i, first):
                for b in range(2):
                    m = 2 * i + b
                    if b or not first:
                        store_runs(m - 1)
                    for c, (c0, n) in enumerate(CHUNKS):
                        act.wait_ge(projected, 3 * m + c + 1)
                        if not first:
                            act.wait_ge(scored, 3 * m - 3)
                        nc.scalar.copy(qT[:, b, c0:c0 + n], pr.psum[:, 3 * b + c, 0:n]).then_inc(q_kept, 1)

            first_then_loop(act, PH, head)
            store_runs(2 * PH - 1)
            for s in range(3):
                act.wait_ge(run_out[s], 16 * 2 * PH)

        @block.vector
        def _(dve):
            def halve(b, i):
                dve.wait_ge(w_loaded[b], 32 * i + LOADED[b])
                high_bits(nc.vector.tensor_copy, w_hi[:, b, :, :], w[:, b, :, :]).then_inc(high, 1)
                dve.wait_ge(high, 2 * i + b + 1)
                nc.vector.tensor_tensor(w_lo[:, b, :, :], w[:, b, :, :], w_hi[:, b, :, :], ALU.subtract
                                        ).then_inc(halved, 1)

            def best_of(values, indices, x, rest, at):
                nc.vector.max(values[:, 0:8], x).then_inc(found, 1)
                wait_apart(dve, found, at + 1, noted)
                nc.vector.max_index(indices[:, 0:8], values[:, 0:8], x)
                nc.vector.match_replace(rest, values[:, 0:8], x, LOWEST).then_inc(found, 1)
                wait_apart(dve, found, at + 2, noted)
                nc.vector.max(values[:, 8:16], rest).then_inc(found, 1)
                wait_apart(dve, found, at + 3, noted)
                nc.vector.max_index(indices[:, 8:16], values[:, 8:16], rest).then_inc(found, 1)

            def best_keys(b, at):
                best_of(best[:, b, :], besti[:, b, :], run[:, 0, 0, :], left[:, 0:N_KEYS], at)
                wait_apart(dve, found, at + HALF_STEPS, noted)

            def best_sums(i, at):
                pairs = [P, TOPK, TOPK]
                nc.vector.tensor_copy(bestf[:, :, :], besti[:, :, :])
                nc.vector.tensor_tensor(cand[:, :, :], best[:, 0, :].unsqueeze(2).to_broadcast(pairs),
                                        best[:, 1, :].unsqueeze(1).to_broadcast(pairs), ALU.add).then_inc(found, 1)
                wait_apart(dve, found, at + 1, noted)
                best_of(top[:, :], topi[:, :], cand[:, :, :].rearrange("p a b -> p (a b)"), left[:, :], at + 1)
                wait_apart(dve, found, at + 5, noted)
                nc.vector.tensor_scalar(part[:, 0, :], topi[:, :], 4, None, ALU.logical_shift_right)
                nc.vector.tensor_scalar(part[:, 1, :], topi[:, :], TOPK - 1, None, ALU.bitwise_and)
                nc.vector.tensor_copy(pr.top[:, bass.ds(i, 1), :], top[:, :].unsqueeze(1)).then_inc(found, 1)
                dve.wait_ge(found, at + 6)
                nc.vector.tensor_copy(partf[:, :, :], part[:, :, :]).then_inc(found, 1)
                dve.wait_ge(found, at + 7)
                for c in range(2):
                    ins = nc.vector.tensor_tensor(pick[:, c, :, :], partf[:, c, :].unsqueeze(2).to_broadcast(pairs),
                                                  iota[:, :].unsqueeze(1).to_broadcast(pairs), ALU.is_equal)
                ins.then_inc(found, 1)
                dve.wait_ge(found, at + 8)
                for c in range(2):
                    ins = nc.vector.tensor_tensor(pick[:, c, :, :], pick[:, c, :, :],
                                                  bestf[:, c, :].unsqueeze(1).to_broadcast(pairs), ALU.mult)
                ins.then_inc(found, 1)
                dve.wait_ge(found, at + 9)
                for c in range(2):
                    nc.vector.tensor_reduce(pr.key[:, c, bass.ds(i, 1), :].rearrange("p o k -> p (o k)"),
                                            pick[:, c, :, :], AX, ALU.add)

            def head(i, first, last):
                for b in range(2):
                    m = 2 * i + b
                    dve.wait_ge(turned, m + 1)
                    nc.vector.tensor_copy(skT[:, b, :], pr.psum[:, 7, 0:P]).then_inc(keys_kept, 1)
                    if not (last and b):
                        halve(1 - b, i + b)
                    for s, (t0, n) in enumerate(RUNS):
                        dve.wait_ge(scored, 3 * m + s + 1)
                        if b or not first:
                            dve.wait_ge(run_out[s], 16 * m)
                        nc.vector.tensor_copy(
                            run[:, s, 0:n, :],
                            pr.psum[:, 6 + s % 2, 0:n * P].rearrange("p (t k) -> p t k", k=P)).then_inc(kept, 1)
                    wait_apart(dve, kept, 3 * m + 1, noted)
                    best_keys(b, HEAD_STEPS * i + HALF_STEPS * b)
                best_sums(i, HEAD_STEPS * i + 2 * HALF_STEPS)

            halve(0, 0)
            head(0, True, False)
            with dve.Fori(1, PH - 1) as i:
                head(i, False, False)
            head(PH - 1, False, True)


def stage_experts(pr):
    nc, a = pr.nc, pr.a
    HH = 2 * PH
    U_SLOTS, V_SLOTS = OCTET, 2 * OCTET
    GROUPS, OCTETS = P // GROUP, P // OCTET
    u = pr.sb("u", [P, U_SLOTS, D], F32)
    v = pr.sb("v", [P, V_SLOTS, D], F32)
    idx = pr.sb("idx", [P, 2, GROUP], U32)
    gate = pr.sb("gate", [P, 2, GROUP], F32)
    xrow = pr.sb("xrow", [96, 2, D], BF16)
    select = pr.sb("select", [96, GROUP, P], BF16)
    hrow = pr.sb("hrow", [GROUP, 2, D], F32)
    y = pr.sb("y", [GROUP, 2, D], F32)
    dot = pr.sb("dot", [P, 2, OCTET], F32)
    act_u = pr.sb("act_u", [P, 2, OCTET], F32)
    weight = pr.sb("weight", [P, 2, GROUP, GROUP], F32)
    u_in = [pr.sem(f"u_in{i}") for i in range(U_SLOTS)]
    v_in = [pr.sem(f"v_in{i}") for i in range(V_SLOTS)]
    const_in = pr.sem("const_in")
    zeroed = pr.sem("zeroed")
    group_in = [pr.sem(f"group_in{b}") for b in range(2)]
    spread = pr.sem("spread")
    dotted = pr.sem("dotted")
    gelued = pr.sem("gelued")
    weighted = pr.sem("weighted")
    v_used = pr.sem("v_used")
    y_ready = pr.sem("y_ready")
    y_out = [pr.sem(f"y_out{b}") for b in range(2)]
    noted = pr.noted
    LOADS = 6 * 16

    sc = pr.sb("sc", [P, HH, N_KEYS], F32)
    left = pr.sb("left", [P, HH * N_KEYS], F32)
    best = pr.sb("best", [P, HH, TOPK], F32)
    besti = pr.sb("besti", [P, HH, TOPK], U32)
    bestf = pr.sb("bestf", [P, HH, TOPK], F32)
    cand = pr.sb("cand", [P, PH, TOPK, TOPK], F32)
    pick = pr.sb("pick", [P, 2, PH, TOPK, TOPK], F32)
    top = pr.sb("top", [P, PH, TOPK], F32)
    topi = pr.sb("topi", [P, PH, TOPK], U32)
    part = pr.sb("part", [P, 2, PH, TOPK], U32)
    partf = pr.sb("partf", [P, 2, PH, TOPK], F32)
    key = pr.sb("key", [P, 2, PH, TOPK], F32)
    expert = pr.sb("expert", [P, PH, TOPK], F32)
    share = pr.sb("share", [P, PH, TOPK], F32)
    total = pr.sb("total", [P, 2, PH], F32)
    iota = pr.sb("iota", [P, TOPK], F32)
    idxT = pr.sb("idxT", [P, P], U32)
    gateT = pr.sb("gateT", [P, P], F32)
    sc_in = pr.sem("sc_in")
    phase = pr.sem("phase")
    shifted = pr.sem("shifted")
    expd = pr.sem("expd")
    routed = pr.sem("routed")
    turned = pr.sem("turned")
    kept = pr.sem("kept")
    stored = pr.sem("stored")
    half = best[:, :, :].rearrange("p (h c) k -> p h c k", c=2)
    keys = bestf[:, :, :].rearrange("p (h c) k -> p h c k", c=2)
    full = [P, PH, TOPK, TOPK]
    flat = cand[:, :, :, :].rearrange("p h a b -> p h (a b)")
    left1 = left[:, :].rearrange("p (h k) -> p h k", k=N_KEYS)
    left2 = left[:, :].rearrange("p (h k) -> p h k", k=TOPK * TOPK)
    BEST, BEST_AT, NEXT, NEXT_AT = (HH * i for i in range(4))
    CAND = 4 * HH
    TOP, TOP_AT, TOP_NEXT, TOP_NEXT_AT = (CAND + 1 + PH * i for i in range(4))
    SHIFT = CAND + 1 + 4 * PH
    PARTS, ONE_HOT, VALUES, SUMS, TOTAL, JOIN, SHARES = (SHIFT + x for x in (1, 2, 4, 6, 8, 9, 10))
    STARTS = (BEST, BEST_AT, NEXT, NEXT_AT, CAND, TOP, TOP_AT, TOP_NEXT, TOP_NEXT_AT, SHIFT, PARTS,
              ONE_HOT, VALUES, SUMS, TOTAL, JOIN, SHARES)
    ENDS = tuple(x - 1 for x in STARTS[1:])
    TURN = P - GROUP
    GATES_OCTET, KEPT_OCTET = TOTAL // OCTET - 1, TURN // OCTET - 1

    def tiles(eng, body):
        body(0, True, False)
        with eng.Fori(1, TILES - 1) as n:
            body(n, False, False)
        body(TILES - 1, False, True)

    with nc.Block() as block:
        @block.sync
        def _(sp):
            sp.dma_start(iota[:, :], a["c_iota"]).then_inc(const_in, 16)
            sp.dma_start(select[:, :, :].rearrange("p g n -> p (g n)"), a["c_select"]).then_inc(const_in, 16)

            def load_scores(n):
                sp.dma_start(sc[:, :, :], a["s_score"][bass.ds(n, 1)].rearrange("o p h k -> (o p) h k")
                             ).then_inc(sc_in, 16)

            def store_routes(n):
                wait_apart(sp, kept, 2 * n + 2, noted)
                for name, src in (("s_idx", idxT), ("s_gate", gateT)):
                    sp.dma_start(a[name][bass.ds(n, 1)].rearrange("o p n -> (o p) n"), src[:, :]
                                 ).then_inc(stored, 16)
                wait_apart(sp, stored, 32 * n + 32, noted)

            store_routes(0)
            sp.wait_ge(zeroed, 3)

            def tile(n, first, last):
                if not last:
                    load_scores(n + 1)
                for g in range(GROUPS):
                    b = g % 2
                    if not first or g >= 2:
                        wait_apart(sp, y_ready, GROUPS * n + g - 1, noted)
                    col = P * n + GROUP * g
                    for dst, name in ((idx, "s_idx"), (gate, "s_gate")):
                        sp.dma_start(dst[:, b, :], a[name][bass.ds(n, 1), :, g * GROUP:(g + 1) * GROUP].rearrange(
                            "o p n -> (o p) n")).then_inc(group_in[b], 16)
                    for i in range(3):
                        sp.dma_start(xrow[32 * i:32 * i + GROUP, b, :], a["s_xn"][i][bass.ds(col, GROUP), :]
                                     ).then_inc(group_in[b], 16)
                    sp.dma_start(hrow[:, b, :], a["s_h"][bass.ds(col, GROUP), :]).then_inc(group_in[b], 16)
                if not last:
                    store_routes(n + 1)

            tiles(sp, tile)

        @block.gpsimd
        def _(pool):
            def tile(n, first, last):
                for s in range(P):
                    g, i = s // GROUP, s % GROUP
                    if i == 0:
                        wait_apart(pool, group_in[g % 2], LOADS * (GROUPS // 2 * n + g // 2 + 1), noted)
                    if not first or s >= U_SLOTS:
                        wait_apart(pool, dotted, P * n + s - U_SLOTS + 1, noted)
                    at = bass.IndirectOffsetOnAxis(ap=idx[:, g % 2, i:i + 1], axis=0)
                    pool.indirect_dma_start(u[:, s % U_SLOTS, :], None, a["expert_u"][0], at
                                            ).then_inc(u_in[s % U_SLOTS], 16)
                    if not first or s >= V_SLOTS:
                        wait_apart(pool, v_used, P * n + s - V_SLOTS + 1, noted)
                    pool.indirect_dma_start(v[:, s % V_SLOTS, :], None, a["expert_v"][0], at
                                            ).then_inc(v_in[s % V_SLOTS], 16)

            tiles(pool, tile)

        @block.tensor
        def _(pe):
            def turn_routes(n, bank):
                pe.wait_ge(routed, 2 * n + 2)
                nc.tensor.transpose(pr.psum[:, bank, 0:P], expert[:, :, :].rearrange("p h k -> p (h k)"),
                                    pr.ident[:, :])
                nc.tensor.transpose(pr.psum[:, bank, P:2 * P], share[:, :, :].rearrange("p h k -> p (h k)"),
                                    pr.ident[:, :]).then_inc(turned, 1)

            turn_routes(0, 6)
            pe.wait_ge(kept, 2)
            pe.wait_ge(const_in, 32)
            pe.wait_ge(zeroed, 3)

            def spread_x(n, s, first):
                g, i = s // GROUP, s % GROUP
                if i == 0:
                    pe.wait_ge(group_in[g % 2], LOADS * (GROUPS // 2 * n + g // 2 + 1))
                if not first or s >= 2:
                    pe.wait_ge(dotted, P * n + s - 1)
                for hf in range(2):
                    last = nc.tensor.matmul(pr.psum[:, 2 * (s % 2) + hf, :], select[:, i, :],
                                            xrow[:, g % 2, hf * 512:hf * 512 + 512], start=True, stop=True)
                last.then_inc(spread, 1)

            def sum_v(n, s):
                q = s % P
                g, i = q // GROUP, q % GROUP
                if i % OCTET == 0:
                    pe.wait_ge(weighted, OCTETS * n + s // OCTET + 1)
                pe.wait_ge(v_in[q % V_SLOTS], 16 * (P // V_SLOTS * n + s // V_SLOTS + 1))
                for hf in range(2):
                    last = nc.tensor.matmul(pr.psum[0:GROUP, 4 + 2 * (g % 2) + hf, :], weight[:, g % 2, i, :],
                                            v[:, q % V_SLOTS, hf * 512:hf * 512 + 512],
                                            start=i == 0, stop=i == GROUP - 1)
                last.then_inc(v_used, 1)

            def tile(n, first, last):
                for s in range(P):
                    if s == TURN and not last:
                        pe.wait_ge(y_ready, GROUPS * n + GROUPS - 2)
                        turn_routes(n + 1, 6)
                    if s == TURN + OCTET and not last:
                        pe.wait_ge(kept, 2 * n + 4)
                    spread_x(n, s, first)
                    if not first or s >= OCTET:
                        sum_v(n, s - OCTET)

            tiles(pe, tile)
            for s in range(P - OCTET, P):
                sum_v(TILES - 1, s)

        @block.vector
        def _(dve):
            nc.vector.memset(weight[:, :, :, :], 0.0).then_inc(zeroed, 1)
            nc.vector.memset(xrow[:, 0, :], 0.0).then_inc(zeroed, 1)
            nc.vector.memset(xrow[:, 1, :], 0.0).then_inc(zeroed, 1)
            dve.wait_ge(const_in, 32)

            def route(n, s):
                if s == BEST:
                    wait_apart(dve, sc_in, 16 * n, noted)
                elif s in STARTS:
                    wait_apart(dve, phase, len(ENDS) * n + STARTS.index(s), noted)
                if s == SHIFT:
                    dve.wait_ge(turned, n)
                ins = None
                if BEST <= s < BEST_AT:
                    ins = nc.vector.max(best[:, s, 0:8], sc[:, s, :])
                elif s < NEXT:
                    i = s - BEST_AT
                    nc.vector.max_index(besti[:, i, 0:8], best[:, i, 0:8], sc[:, i, :])
                    ins = nc.vector.match_replace(left1[:, i, :], best[:, i, 0:8], sc[:, i, :], LOWEST)
                elif s < NEXT_AT:
                    i = s - NEXT
                    ins = nc.vector.max(best[:, i, 8:16], left1[:, i, :])
                elif s < CAND:
                    i = s - NEXT_AT
                    ins = nc.vector.max_index(besti[:, i, 8:16], best[:, i, 8:16], left1[:, i, :])
                elif s == CAND:
                    nc.vector.tensor_copy(bestf[:, :, :], besti[:, :, :])
                    ins = nc.vector.tensor_tensor(cand[:, :, :, :], half[:, :, 0, :].unsqueeze(3).to_broadcast(full),
                                                  half[:, :, 1, :].unsqueeze(2).to_broadcast(full), ALU.add)
                elif s < TOP_AT:
                    i = s - TOP
                    ins = nc.vector.max(top[:, i, 0:8], flat[:, i, :])
                elif s < TOP_NEXT:
                    i = s - TOP_AT
                    nc.vector.max_index(topi[:, i, 0:8], top[:, i, 0:8], flat[:, i, :])
                    ins = nc.vector.match_replace(left2[:, i, :], top[:, i, 0:8], flat[:, i, :], LOWEST)
                elif s < TOP_NEXT_AT:
                    i = s - TOP_NEXT
                    ins = nc.vector.max(top[:, i, 8:16], left2[:, i, :])
                elif s < SHIFT:
                    i = s - TOP_NEXT_AT
                    ins = nc.vector.max_index(topi[:, i, 8:16], top[:, i, 8:16], left2[:, i, :])
                elif s == SHIFT:
                    nc.vector.tensor_tensor(share[:, :, :], top[:, :, :], top[:, :, 0:1].to_broadcast(
                        [P, PH, TOPK]), ALU.subtract).then_inc(shifted, 1)
                    nc.vector.tensor_scalar(part[:, 0, :, :], topi[:, :, :], 4, None, ALU.logical_shift_right)
                    ins = nc.vector.tensor_scalar(part[:, 1, :, :], topi[:, :, :], TOPK - 1, None, ALU.bitwise_and)
                elif s == PARTS:
                    ins = nc.vector.tensor_copy(partf[:, :, :, :], part[:, :, :, :])
                elif s < VALUES:
                    c = s - ONE_HOT
                    ins = nc.vector.tensor_tensor(
                        pick[:, c, :, :, :], partf[:, c, :, :].unsqueeze(3).to_broadcast(full),
                        iota[:, :].unsqueeze(1).unsqueeze(1).to_broadcast(full), ALU.is_equal)
                elif s < SUMS:
                    c = s - VALUES
                    ins = nc.vector.tensor_tensor(pick[:, c, :, :, :], pick[:, c, :, :, :],
                                                  keys[:, :, c, :].unsqueeze(2).to_broadcast(full), ALU.mult)
                elif s < TOTAL:
                    c = s - SUMS
                    ins = nc.vector.tensor_reduce(key[:, c, :, :].rearrange("p h k -> p (h k)"),
                                                  pick[:, c, :, :, :].rearrange("p h k j -> p (h k) j"), AX, ALU.add)
                elif s == TOTAL:
                    dve.wait_ge(expd, n + 1)
                    ins = nc.vector.tensor_reduce(total[:, 0, :], share[:, :, :], AX, ALU.add)
                elif s == JOIN:
                    nc.vector.scalar_tensor_tensor(expert[:, :, :].rearrange("p h k -> p (h k)"),
                                                   key[:, 0, :, :].rearrange("p h k -> p (h k)"), float(N_KEYS),
                                                   key[:, 1, :, :].rearrange("p h k -> p (h k)"),
                                                   ALU.mult, ALU.add).then_inc(routed, 1)
                    ins = nc.vector.reciprocal(total[:, 1, :], total[:, 0, :])
                elif s == SHARES:
                    nc.vector.tensor_tensor(share[:, :, :], share[:, :, :],
                                            total[:, 1, :].unsqueeze(2).to_broadcast([P, PH, TOPK]), ALU.mult
                                            ).then_inc(routed, 1)
                if s in ENDS:
                    ins.then_inc(phase, 1)

            def weights(n, o):
                q = o % OCTETS
                g, c = q // 2, q % 2
                diag = weight[:, g % 2, :, :].rearrange("p i j -> p (i j)")
                at = OCTET * c * (GROUP + 1)
                dve.wait_ge(gelued, OCTETS * n + o + 1)
                nc.vector.tensor_tensor(diag[:, at:at + (OCTET - 1) * (GROUP + 1) + 1:GROUP + 1],
                                        act_u[:, c, :], gate[:, g % 2, c * OCTET:(c + 1) * OCTET],
                                        ALU.mult).then_inc(weighted, 1)

            def add_h(n, g, fresh):
                b = g % 2
                dve.wait_ge(v_used, P * n + GROUP * (g + 1))
                if not fresh:
                    dve.wait_ge(y_out[b], 16 * (GROUPS // 2 * n + g // 2))
                nc.vector.tensor_tensor(y[:, b, :], pr.psum[0:GROUP, 4 + 2 * b:6 + 2 * b, :].rearrange(
                    "p b n -> p (b n)"), hrow[:, b, :], ALU.add).then_inc(y_ready, 1)

            def tile(n, first, last):
                for s in range(P):
                    o = s // OCTET
                    dve.wait_ge(u_in[s % U_SLOTS], 16 * (OCTETS * n + o + 1))
                    dve.wait_ge(spread, P * n + s + 1)
                    nc.vector.tensor_tensor_reduce(u[:, s % U_SLOTS, :], u[:, s % U_SLOTS, :],
                                                   pr.banks(2 * (s % 2), 2), 1.0, 0.0, ALU.mult, ALU.add,
                                                   dot[:, o % 2, s % OCTET:s % OCTET + 1]).then_inc(dotted, 1)
                    if s % OCTET == 0 and (not first or o):
                        weights(n, o - 1)
                    if s % GROUP == OCTET - 1 and (not first or s >= GROUP):
                        add_h(n, s // GROUP - 1, first and s < 3 * GROUP)
                    if not last:
                        route(n + 1, s)

            def route_first():
                nc.vector.tensor_tensor(share[:, :, :], pr.top[:, :, :], pr.top[:, :, 0:1].to_broadcast(
                    [P, PH, TOPK]), ALU.subtract).then_inc(shifted, 1)
                nc.vector.scalar_tensor_tensor(expert[:, :, :].rearrange("p h k -> p (h k)"),
                                               pr.key[:, 0, :, :].rearrange("p h k -> p (h k)"), float(N_KEYS),
                                               pr.key[:, 1, :, :].rearrange("p h k -> p (h k)"),
                                               ALU.mult, ALU.add).then_inc(routed, 1)
                dve.wait_ge(expd, 1)
                nc.vector.tensor_reduce(total[:, 0, :], share[:, :, :], AX, ALU.add).then_inc(phase, 1)
                dve.wait_ge(phase, 1)
                nc.vector.reciprocal(total[:, 1, :], total[:, 0, :]).then_inc(phase, 1)
                dve.wait_ge(phase, 2)
                nc.vector.tensor_tensor(share[:, :, :], share[:, :, :],
                                        total[:, 1, :].unsqueeze(2).to_broadcast([P, PH, TOPK]), ALU.mult
                                        ).then_inc(routed, 1)
                dve.sem_inc(phase, len(ENDS) - 2)

            route_first()
            dve.wait_ge(zeroed, 3)
            tiles(dve, tile)
            weights(TILES - 1, OCTETS - 1)
            add_h(TILES - 1, GROUPS - 1, False)

        @block.scalar
        def _(act):
            def gates(n):
                act.wait_ge(shifted, n + 1)
                nc.scalar.activation(share[:, :, :], share[:, :, :], ACT.Exp).then_inc(expd, 1)

            def keep(n, fresh):
                act.wait_ge(turned, n + 1)
                if not fresh:
                    act.wait_ge(stored, 32 * n)
                nc.scalar.copy(idxT[:, :], pr.psum[:, 6, 0:P]).then_inc(kept, 1)
                nc.scalar.copy(gateT[:, :], pr.psum[:, 6, P:2 * P]).then_inc(kept, 1)

            gates(0)
            keep(0, True)

            def tile(n, r, b, first, last):
                for o in range(OCTETS):
                    act.wait_ge(dotted, P * n + OCTET * (o + 1))
                    if o >= 2 or not first:
                        act.wait_ge(weighted, OCTETS * n + o - 1)
                    nc.scalar.activation(act_u[:, o % 2, :], dot[:, o % 2, :], ACT.Gelu_apprx_tanh
                                         ).then_inc(gelued, 1)
                    if o == GATES_OCTET and not last:
                        gates(n + 1)
                    if o == KEPT_OCTET and not last:
                        keep(n + 1, False)
                    if o % 2 == 1:
                        g = o // 2
                        rows = rows_of(pr, pr.yp, pr.ys, n, r, b)[g // (GROUPS // 2)]
                        at = g % (GROUPS // 2) * GROUP
                        act.wait_ge(y_ready, GROUPS * n + g + 1)
                        act.dma_start(rows[at:at + GROUP, :], y[:, g % 2, :]).then_inc(y_out[g % 2], 16)

            for b in range(2):
                tile(b, None, b, b == 0, False)
            with act.Fori(0, PHASE - 1) as r:
                for b in range(2):
                    tile(2 * r + 2 + b, r, b, False, False)
            for b in range(2):
                tile(TILES - 2 + b, PHASE - 1, b, False, b == 1)
            for b in range(2):
                act.wait_ge(y_out[b], 16 * TILES * GROUPS // 2)


def build(nc, a, stop=99):
    with ExitStack() as ctx:
        pr = Program(nc, a, ctx)

        def run(stage):
            with ExitStack() as own:
                pr.stage, pr.prefix = own, stage.__name__.removeprefix("stage_") + "_"
                stage(pr)
            pr.prefix = ""

        with ExitStack() as wide:
            pr.stage = wide
            pr.xhiT = pr.sb("xhiT", [P, DC, T], F32R)
            pr.xnT = pr.sb("xnT", [P, DC, T], F32R)
            run(stage_norm)
            run(stage_fourier)
            run(stage_attention)
            with ExitStack() as mix:
                pr.stage = mix
                pr.mixT = pr.sb("mixT", [P, DC, T], F32)
                run(stage_mix)
                run(stage_out)
            run(stage_keys)
        run(stage_experts)
    return pr


_INS = ["x_prompt", "x_sample", "g_mix", "w_in", "q_gain", "k_gain", "w_fourier", "w_attn", "w_out",
        "g_ffn", "w_query", "sub_keys", "expert_u", "expert_v"]
_OUTS = {"y_prompt": (1, SEQ, D), "y_sample": (1, DEC_SEQ, D)}


def kernel(**inputs):
    import concourse.bacc as bacc
    from concourse.bass_utils import run_bass_kernel_spmd

    nc = bacc.Bacc("TRN2", target_bir_lowering=False, num_devices=1)
    arrays, a = {}, {}
    for name, value in [(n, inputs[n]) for n in _INS] + list(constants().items()):
        value = np.ascontiguousarray(value)
        arrays[f"in_{name}"] = value
        a[name] = nc.dram_tensor(f"in_{name}", value.shape, mybir.dt.from_np(value.dtype),
                                 kind="ExternalInput").ap()
    for name, shape in _OUTS.items():
        a[name] = nc.dram_tensor(name, shape, F32, kind="ExternalOutput").ap()
    a["s_h"] = nc.dram_tensor("s_h", (T, D), F32, kind="Internal").ap()
    a["s_branch"] = nc.dram_tensor("s_branch", (FG + HEADS, P, T), F32, kind="Internal").ap()
    a["s_xn"] = nc.dram_tensor("s_xn", (3, T, D), BF16, kind="Internal").ap()
    for name, dt in (("s_idx", U32), ("s_gate", F32)):
        a[name] = nc.dram_tensor(name, (TILES, P, P), dt, kind="Internal").ap()
    a["s_score"] = nc.dram_tensor("s_score", (TILES, P, 2 * PH, N_KEYS), F32, kind="Internal").ap()
    build(nc, a)
    r = run_bass_kernel_spmd(nc, [arrays], core_ids=[0])
    return tuple(r.results[0][name] for name in _OUTS)
```
